# Optimizing a Trainium2 kernel written in Bass

```python
import math
import jax
import jax.numpy as jnp
from jax import lax
import numpy as np

D_MODEL = 1024
BATCH = 1
SEQ = 128
DEPTH = 2
DEC_BATCH = 1
DEC_SEQ = 512
PAST_LEN = 128

GRID_W = 64
H_A = 4
DK_A = 128
DV_A = 128
CONV_K = 3
CHUNK = 64
H_B = 4
DQK_B = 64
DV_B = 2 * DQK_B
H_C = 8
NOPE_C = 128
ROPE_C = 64
V_C = 128
Q_LORA = 384
KV_LORA = 256
D_FF = 2816
N_EXPERTS = 8
TOP_K = 2
D_FF_EXPERT = 1408
ROPE_BASE = 10000.0
Q_BLOCK = 128
EPS = 1e-6
EVEN_IN_SIZES = (H_A * DK_A, H_A * DK_A, H_A * DV_A, H_A * DV_A, H_A, H_A, H_A, H_A,
                 H_B * 2 * DQK_B, H_B * 2 * DQK_B, H_B * DV_B)
EVEN_IN = sum(EVEN_IN_SIZES)
ODD_IN = Q_LORA + KV_LORA + ROPE_C

kernel_name = 'hybrid_deltanet_diffattn_mla_dit_step'

f32 = jnp.float32

def rmsnorm(x, w):
    xf = x.astype(f32)
    y = xf * lax.rsqrt(jnp.mean(xf * xf, axis=-1, keepdims=True) + EPS)
    return (y * w.astype(f32)).astype(x.dtype)

def l2norm(x):
    xf = x.astype(f32)
    return xf * lax.rsqrt(jnp.sum(xf * xf, axis=-1, keepdims=True) + EPS)

def modulate(x, w, shift, scale):
    return rmsnorm(x, w) * (1.0 + scale) + shift

def split_cols(x, sizes):
    idx = [int(i) for i in np.cumsum(sizes)[:-1]]
    return jnp.split(x, idx, axis=-1)

def axial_rope_tables(n_tokens, rot_dim):
    n_rows = n_tokens // GRID_W
    rr, cc = jnp.meshgrid(jnp.arange(n_rows), jnp.arange(GRID_W), indexing='ij')
    rows = rr.reshape(-1).astype(f32)
    cols = cc.reshape(-1).astype(f32)
    per_axis = rot_dim // 2
    inv = ROPE_BASE ** (-jnp.arange(0, per_axis, 2, dtype=f32) / per_axis)
    ang_r = rows[:, None] * inv[None, :]
    ang_c = cols[:, None] * inv[None, :]
    ang = jnp.concatenate([ang_r, ang_r, ang_c, ang_c], axis=-1)
    return jnp.cos(ang), jnp.sin(ang)

def apply_rope(x, cos, sin):
    shape = (cos.shape[0],) + (1,) * (x.ndim - 3) + (cos.shape[1],)
    cos, sin = cos.reshape(shape), sin.reshape(shape)
    half = x.shape[-1] // 2
    xf = x.astype(f32)

    def rot_half(u):
        u1, u2 = jnp.split(u, 2, axis=-1)
        return jnp.concatenate([-u2, u1], axis=-1)

    xr = jnp.concatenate([rot_half(xf[..., :half]), rot_half(xf[..., half:])], axis=-1)
    return (xf * cos + xr * sin).astype(x.dtype)

def short_conv(x, w):
    pad = CONV_K // 2
    L = x.shape[1]
    xp = jnp.pad(x, ((0, 0), (pad, CONV_K - 1 - pad), (0, 0)))
    y = xp[:, 0:L] * w[0]
    for j in range(1, CONV_K):
        y = y + xp[:, j:j + L] * w[j]
    return jax.nn.silu(y)

def gated_delta_chunked(q, k, v, g, beta, s0):
    B, H, L, dk = q.shape
    dv = v.shape[-1]
    n = L // CHUNK

    def chunks(t):
        return t.astype(f32).reshape((B, H, n, CHUNK) + t.shape[3:])

    q, k, v, g, beta = chunks(q), chunks(k), chunks(v), chunks(g), chunks(beta)
    g = jnp.cumsum(g, axis=-1)
    incl = jnp.tril(jnp.ones((CHUNK, CHUNK), bool))
    strict = jnp.tril(jnp.ones((CHUNK, CHUNK), bool), -1)
    gdiff = g[..., :, None] - g[..., None, :]
    decay = jnp.where(incl, jnp.exp(jnp.where(incl, gdiff, 0.0)), 0.0)
    kb = k * beta[..., None]
    m = jnp.where(strict, jnp.einsum('bhncd,bhnsd->bhncs', kb, k) * decay, 0.0)
    a = m + jnp.eye(CHUNK, dtype=f32)
    rhs = jnp.concatenate([v * beta[..., None], kb * jnp.exp(g)[..., None]], axis=-1)
    sol = lax.linalg.triangular_solve(a, rhs, left_side=True, lower=True, unit_diagonal=True)
    u, w = sol[..., :dv], sol[..., dv:]
    a_intra = jnp.einsum('bhncd,bhnsd->bhncs', q, k) * decay
    xs = tuple(jnp.moveaxis(t, 2, 0) for t in (q, k, u, w, g, a_intra))

    def step(s, inp):
        q_i, k_i, u_i, w_i, g_i, a_i = inp
        v_new = u_i - jnp.einsum('bhcd,bhde->bhce', w_i, s)
        o = (jnp.einsum('bhcd,bhde->bhce', q_i * jnp.exp(g_i)[..., None], s)
             + jnp.einsum('bhcs,bhse->bhce', a_i, v_new))
        g_last = g_i[..., -1]
        k_dec = k_i * jnp.exp(g_last[..., None] - g_i)[..., None]
        s = s * jnp.exp(g_last)[..., None, None] + jnp.einsum('bhcd,bhce->bhde', k_dec, v_new)
        return s, o

    s_fin, o = lax.scan(step, s0.astype(f32), xs)
    o = jnp.moveaxis(o, 0, 2).reshape(B, H, L, dv)
    return o, s_fin

def bidir_gated_delta(q, k, v, g, beta, s0_f, s0_b):
    o_f, s_f = gated_delta_chunked(q, k, v, g[0], beta[0], s0_f)

    def rev(t):
        return jnp.flip(t, axis=2)

    o_b, s_b = gated_delta_chunked(rev(q), rev(k), rev(v), rev(g[1]), rev(beta[1]), s0_b)
    return o_f + rev(o_b), s_f, s_b

def map_query_blocks(fn, q):
    B, H, L = q.shape[:3]
    nb = L // Q_BLOCK
    qb = jnp.moveaxis(q.reshape((B, H, nb, Q_BLOCK) + q.shape[3:]), 2, 0)
    out = jnp.moveaxis(lax.map(fn, qb), 0, 2)
    return out.reshape(B, H, L, out.shape[-1])

def diff_attend(q, k, v, lam):
    s = jnp.einsum('bhqtd,bhktd->bhtqk', q, k).astype(f32) * (DQK_B ** -0.5)
    p = jax.nn.softmax(s, axis=-1)
    a = p[:, :, 0] - lam * p[:, :, 1]
    return jnp.einsum('bhqk,bhke->bhqe', a, v.astype(f32))

def softmax_attend(q, k, v):
    s = jnp.einsum('bhqd,bhkd->bhqk', q, k).astype(f32) * (q.shape[-1] ** -0.5)
    p = jax.nn.softmax(s, axis=-1)
    return jnp.einsum('bhqk,bhke->bhqe', p, v.astype(f32))

def delta_diff_project(h, w_in, conv_w, a_log, dt_bias, cos, sin):
    B, L, _ = h.shape
    qa, ka, va, z, af, ab, bf, bb, qb, kb, vb = split_cols(h @ w_in, EVEN_IN_SIZES)
    qkv = short_conv(jnp.concatenate([qa, ka, va], axis=-1), conv_w)
    qa, ka, va = split_cols(qkv, (H_A * DK_A, H_A * DK_A, H_A * DV_A))

    def heads(t, d):
        return t.reshape(B, L, -1, d).transpose(0, 2, 1, 3)

    qa = l2norm(heads(qa, DK_A)) * (DK_A ** -0.5)
    ka = l2norm(heads(ka, DK_A))
    va = heads(va, DV_A).astype(f32)
    a = jnp.stack([af, ab]).astype(f32)
    g = -jnp.exp(a_log.astype(f32))[:, None, None, :] * jax.nn.softplus(a + dt_bias.astype(f32)[:, None, None, :])
    beta = jax.nn.sigmoid(jnp.stack([bf, bb]).astype(f32))
    g = g.transpose(0, 1, 3, 2)
    beta = beta.transpose(0, 1, 3, 2)
    z = z.reshape(B, L, H_A, DV_A)
    qb = qb.reshape(B, L, H_B, 2, DQK_B)
    kb = kb.reshape(B, L, H_B, 2, DQK_B)
    if cos is not None:
        qb = apply_rope(qb, cos, sin)
        kb = apply_rope(kb, cos, sin)
    qb = qb.transpose(0, 2, 1, 3, 4)
    kb = kb.transpose(0, 2, 1, 3, 4)
    vb = heads(vb, DV_B)
    return qa, ka, va, g, beta, z, qb, kb, vb

def delta_diff_output(o_a, z, o_b, onorm, subln, lam_init, w_out):
    B, _, L, _ = o_a.shape
    ya = (rmsnorm(o_a.transpose(0, 2, 1, 3), onorm) * jax.nn.silu(z.astype(f32))).reshape(B, L, H_A * DV_A)
    yb = (rmsnorm(o_b, subln) * (1.0 - lam_init)).transpose(0, 2, 1, 3).reshape(B, L, H_B * DV_B)
    y = jnp.concatenate([ya, yb], axis=-1)
    return y.astype(w_out.dtype) @ w_out

def mla_project(h, w_in, q_norm, kv_norm, w_uq, cos, sin):
    B, L, _ = h.shape
    cq, ckv, kr = split_cols(h @ w_in, (Q_LORA, KV_LORA, ROPE_C))
    q = (rmsnorm(cq, q_norm) @ w_uq).reshape(B, L, H_C, NOPE_C + ROPE_C)
    ckv = rmsnorm(ckv, kv_norm)
    if cos is not None:
        q = jnp.concatenate([q[..., :NOPE_C], apply_rope(q[..., NOPE_C:], cos, sin)], axis=-1)
        kr = apply_rope(kr, cos, sin)
    return q.transpose(0, 2, 1, 3), ckv, kr

def mla_keys_values(ckv, kr, w_ukv):
    B, L, _ = ckv.shape
    kv = (ckv @ w_ukv).reshape(B, L, H_C, NOPE_C + V_C)
    k = jnp.concatenate([kv[..., :NOPE_C], jnp.broadcast_to(kr[:, :, None, :], (B, L, H_C, ROPE_C))], axis=-1)
    return k.transpose(0, 2, 1, 3), kv[..., NOPE_C:].transpose(0, 2, 1, 3)

def mla_output(o, w_out):
    B, _, L, _ = o.shape
    return o.transpose(0, 2, 1, 3).reshape(B, L, H_C * V_C).astype(w_out.dtype) @ w_out

def swiglu(h, w_gu, w_down):
    gt, up = jnp.split(h @ w_gu, 2, axis=-1)
    return (jax.nn.silu(gt) * up) @ w_down

def moe_ffn(h, router_w, w_gu, w_down):
    B, L, D = h.shape
    x = h.reshape(B * L, D)
    probs = jax.nn.softmax((x @ router_w).astype(f32), axis=-1)
    top_p, top_i = lax.top_k(probs, TOP_K)
    top_p = top_p / jnp.sum(top_p, axis=-1, keepdims=True)
    gates = jnp.einsum('nk,nke->ne', top_p, jax.nn.one_hot(top_i, N_EXPERTS, dtype=f32))
    y = jnp.zeros((B * L, D), f32)
    for e in range(N_EXPERTS):
        y = y + gates[:, e:e + 1] * swiglu(x, w_gu[e], w_down[e]).astype(f32)
    return y.reshape(B, L, D)

def setup_inputs(seed: int = 0) -> dict:
    key = jax.random.key(seed)
    ks = iter(jax.random.split(key, 40))
    D = D_MODEL
    n_even = (DEPTH + 1) // 2
    n_odd = DEPTH // 2

    def nrm(shape, scale):
        return jax.random.normal(next(ks), shape, jnp.float32) * scale

    def gain(shape):
        return 1.0 + nrm(shape, 0.02)

    w_a_out = H_A * DV_A + H_B * DV_B
    return {
        'x_prompt': nrm((BATCH, SEQ, D), 1.0),
        'x_sample': nrm((DEC_BATCH, DEC_SEQ, D), 1.0),
        'state_delta': nrm((DEC_BATCH, n_even, 2, H_A, DK_A, DV_A), 0.1),
        'cache_diff_k': nrm((DEC_BATCH, n_even, H_B, PAST_LEN, 2 * DQK_B), 1.0),
        'cache_diff_v': nrm((DEC_BATCH, n_even, H_B, PAST_LEN, DV_B), 1.0),
        'cache_mla_ckv': nrm((DEC_BATCH, n_odd, PAST_LEN, KV_LORA), 1.0),
        'cache_mla_krope': nrm((DEC_BATCH, n_odd, PAST_LEN, ROPE_C), 1.0),
        'c': nrm((DEC_BATCH, D), 1.0),
        'c_ctx': nrm((D,), 1.0),
        'mod_w': nrm((DEPTH, D, 6 * D), 0.5 * D ** -0.5),
        'mod_b': nrm((DEPTH, 6 * D), 0.02),
        'norm_mix': gain((DEPTH, D)),
        'norm_ffn': gain((DEPTH, D)),
        'final_norm': gain((D,)),
        'ev_w_in': nrm((n_even, D, EVEN_IN), D ** -0.5),
        'ev_conv_w': nrm((n_even, CONV_K, 2 * H_A * DK_A + H_A * DV_A), CONV_K ** -0.5),
        'ev_a_log': jnp.log(jax.random.uniform(next(ks), (n_even, 2, H_A), jnp.float32, 0.05, 1.0)),
        'ev_dt_bias': nrm((n_even, 2, H_A), 0.1),
        'ev_onorm': gain((n_even, DV_A)),
        'ev_lambda': nrm((n_even, 4, DQK_B), 0.1),
        'ev_subln': gain((n_even, DV_B)),
        'ev_w_out': nrm((n_even, w_a_out, D), w_a_out ** -0.5),
        'ffn_w_gu': nrm((n_even, D, 2 * D_FF), D ** -0.5),
        'ffn_w_down': nrm((n_even, D_FF, D), D_FF ** -0.5),
        'od_w_in': nrm((n_odd, D, ODD_IN), D ** -0.5),
        'od_q_norm': gain((n_odd, Q_LORA)),
        'od_kv_norm': gain((n_odd, KV_LORA)),
        'od_w_uq': nrm((n_odd, Q_LORA, H_C * (NOPE_C + ROPE_C)), Q_LORA ** -0.5),
        'od_w_ukv': nrm((n_odd, KV_LORA, H_C * (NOPE_C + V_C)), KV_LORA ** -0.5),
        'od_w_out': nrm((n_odd, H_C * V_C, D), (H_C * V_C) ** -0.5),
        'moe_router': nrm((n_odd, D, N_EXPERTS), D ** -0.5),
        'moe_w_gu': nrm((n_odd, N_EXPERTS, D, 2 * D_FF_EXPERT), D ** -0.5),
        'moe_w_down': nrm((n_odd, N_EXPERTS, D_FF_EXPERT, D), D_FF_EXPERT ** -0.5),
    }

def reference(x_prompt, x_sample, state_delta, cache_diff_k, cache_diff_v, cache_mla_ckv, cache_mla_krope,
              c, c_ctx, mod_w, mod_b, norm_mix, norm_ffn, final_norm,
              ev_w_in, ev_conv_w, ev_a_log, ev_dt_bias, ev_onorm, ev_lambda, ev_subln, ev_w_out,
              ffn_w_gu, ffn_w_down, od_w_in, od_q_norm, od_kv_norm, od_w_uq, od_w_ukv, od_w_out,
              moe_router, moe_w_gu, moe_w_down):
    bp, lp, _ = x_prompt.shape
    bs, ls, _ = x_sample.shape
    pl = cache_diff_k.shape[3]
    cos_b, sin_b = axial_rope_tables(ls, DQK_B)
    cos_c, sin_c = axial_rope_tables(ls, ROPE_C)
    xp, xs = x_prompt, x_sample
    sd_new, dk_new, dv_new, ckv_new, kr_new = [], [], [], [], []
    for layer in range(DEPTH):
        j = layer // 2
        m_p = jnp.split((jax.nn.silu(c_ctx) @ mod_w[layer] + mod_b[layer])[None, None, :], 6, axis=-1)
        m_s = jnp.split((jax.nn.silu(c) @ mod_w[layer] + mod_b[layer])[:, None, :], 6, axis=-1)
        hp = modulate(xp, norm_mix[layer], m_p[0], m_p[1])
        hs = modulate(xs, norm_mix[layer], m_s[0], m_s[1])
        if layer % 2 == 0:
            lam_init = 0.8 - 0.6 * math.exp(-0.3 * layer)
            lp_ = ev_lambda[j].astype(f32)
            lam = jnp.exp(jnp.sum(lp_[0] * lp_[1])) - jnp.exp(jnp.sum(lp_[2] * lp_[3])) + lam_init
            qa, ka, va, g, beta, z, qb, kb, vb = delta_diff_project(
                hp, ev_w_in[j], ev_conv_w[j], ev_a_log[j], ev_dt_bias[j], None, None)
            s0 = jnp.zeros((bp, H_A, DK_A, DV_A), f32)
            o_a, s_f, s_b = bidir_gated_delta(qa, ka, va, g, beta, s0, s0)
            o_b = map_query_blocks(lambda qq: diff_attend(qq, kb, vb, lam), qb)
            mix_p = delta_diff_output(o_a, z, o_b, ev_onorm[j], ev_subln[j], lam_init, ev_w_out[j])
            sd_new.append(jnp.stack([s_f, s_b], axis=1))
            dk_new.append(kb.reshape(bp, H_B, lp, 2 * DQK_B))
            dv_new.append(vb)
            qa, ka, va, g, beta, z, qb, kb, vb = delta_diff_project(
                hs, ev_w_in[j], ev_conv_w[j], ev_a_log[j], ev_dt_bias[j], cos_b, sin_b)
            o_a, _, _ = bidir_gated_delta(qa, ka, va, g, beta, state_delta[:, j, 0], state_delta[:, j, 1])
            k_all = jnp.concatenate([kb, cache_diff_k[:, j].reshape(bs, H_B, pl, 2, DQK_B)], axis=2)
            v_all = jnp.concatenate([vb, cache_diff_v[:, j]], axis=2)
            o_b = map_query_blocks(lambda qq: diff_attend(qq, k_all, v_all, lam), qb)
            mix_s = delta_diff_output(o_a, z, o_b, ev_onorm[j], ev_subln[j], lam_init, ev_w_out[j])
        else:
            q, ckv, kr = mla_project(hp, od_w_in[j], od_q_norm[j], od_kv_norm[j], od_w_uq[j], None, None)
            k, v = mla_keys_values(ckv, kr, od_w_ukv[j])
            o = map_query_blocks(lambda qq: softmax_attend(qq, k, v), q)
            mix_p = mla_output(o, od_w_out[j])
            ckv_new.append(ckv)
            kr_new.append(kr)
            q, ckv, kr = mla_project(hs, od_w_in[j], od_q_norm[j], od_kv_norm[j], od_w_uq[j], cos_c, sin_c)
            ckv_all = jnp.concatenate([ckv, cache_mla_ckv[:, j]], axis=1)
            kr_all = jnp.concatenate([kr, cache_mla_krope[:, j]], axis=1)
            k_s, v_s = mla_keys_values(ckv_all, kr_all, od_w_ukv[j])
            o = map_query_blocks(lambda qq: softmax_attend(qq, k_s, v_s), q)
            mix_s = mla_output(o, od_w_out[j])
        xp = xp + (m_p[2] * mix_p).astype(xp.dtype)
        xs = xs + (m_s[2] * mix_s).astype(xs.dtype)
        hp = modulate(xp, norm_ffn[layer], m_p[3], m_p[4])
        hs = modulate(xs, norm_ffn[layer], m_s[3], m_s[4])
        if layer % 2 == 0:
            fp = swiglu(hp, ffn_w_gu[j], ffn_w_down[j])
            fs = swiglu(hs, ffn_w_gu[j], ffn_w_down[j])
        else:
            fp = moe_ffn(hp, moe_router[j], moe_w_gu[j], moe_w_down[j])
            fs = moe_ffn(hs, moe_router[j], moe_w_gu[j], moe_w_down[j])
        xp = xp + (m_p[5] * fp).astype(xp.dtype)
        xs = xs + (m_s[5] * fs).astype(xs.dtype)
    y_prompt = rmsnorm(xp, final_norm)
    y_sample = rmsnorm(xs, final_norm)
    return (y_prompt, y_sample, jnp.stack(sd_new, axis=1), jnp.stack(dk_new, axis=1), jnp.stack(dv_new, axis=1),
            jnp.stack(ckv_new, axis=1), jnp.stack(kr_new, axis=1))


_drawn_inputs = setup_inputs


def setup_inputs(seed=0):
    import zlib

    import numpy as np

    out = dict(_drawn_inputs(seed))
    spreads = {}
    factors = {'state_delta': 5.325,
     'cache_mla_ckv': 4.481,
     'cache_mla_krope': 7.53,
     'norm_ffn': 3.698,
     'final_norm': 7.41,
     'ev_dt_bias': 4.488,
     'ev_onorm': 5.167,
     'ev_lambda': 3.712,
     'ev_subln': 8.0,
     'od_q_norm': 7.662,
     'od_kv_norm': 9.437}
    for name, (base, spread) in spreads.items():
        noise = np.random.default_rng([zlib.crc32(name.encode()), seed]).standard_normal(out[name].shape)
        drawn = base * np.exp(spread * noise) if base else spread * noise
        out[name] = jnp.asarray(drawn.astype(out[name].dtype))
    for name, factor in factors.items():
        out[name] = (out[name] * factor).astype(out[name].dtype)
    return out
```

```python
from contextlib import ExitStack

import numpy as np
import concourse.bass as bass
from concourse import mybir

ALU = mybir.AluOpType
ACT = mybir.ActivationFunctionType
AX = mybir.AxisListType
F32 = mybir.dt.float32
U32 = mybir.dt.uint32

P = 128
D = 1024
KD = D // P
SEQ, DEC_SEQ, PAST = 128, 512, 128
T = SEQ + DEC_SEQ
NT = T // P
HT = T // 2
TK = T + PAST
SEGS = ((0, SEQ, 0), (SEQ, T, 1))
H = 4
HC = 8
ROPE = 64
FC = 2816 // P
NE = 8
EC = 1408 // P
WS = 5
WB = 2048
LEVELS = 7
NEG = -30000.0
EPS = 1e-6
LAM_INIT = 0.8 - 0.6
LK = 11

C_ID, C_ONE, C_TRI, C_NEG, C_LVL, C_ROT = 0, 128, 256, 512, 768, 768 + LEVELS * 256
C_IOTA = C_ROT + 128
C_EPS = C_IOTA + 8
C_COLS = C_EPS + 1
S_NORM, S_MODB, S_CONV = 0, 40, 136
S_ONORM, S_SUBLN, S_QN, S_KVN, S_DTB, S_ALOG, S_C = 172, 173, 174, 177, 179, 187, 195
S_COLS = S_C + 16


class Ring:

    def __init__(self, slots):
        self.slots, self.used, self.stages = slots, [0] * slots, {}

    def plan(self, stage, each, turns=1):
        per = [(each - s + self.slots - 1) // self.slots for s in range(self.slots)]
        self.stages[stage] = (list(self.used), per, each, turns)
        self.used = [u + turns * p for u, p in zip(self.used, per)]

    def use(self, stage, j, turn=0):
        before, per, _, _ = self.stages[stage]
        s = j % self.slots
        return s, turn * per[s] + before[s] + j // self.slots


class Steps:

    def __init__(self, eng, sem):
        self.eng, self.sem, self.n, self.off = eng, sem, 0, 0

    def did(self, ins):
        ins.then_inc(self.sem, 1)
        self.n += 1

    def sync(self):
        self.eng.wait_ge(self.sem, self.n + self.off)

    def then(self, ins):
        self.did(ins)
        self.sync()

    def loop(self, turn, each):
        self.start, self.off = self.n, turn * each

    def end(self, each, turns):
        assert self.n - self.start == each, (self.n - self.start, each)
        self.n, self.off = self.start + each * turns, 0


def spread(ap, axis, n):
    v = ap.unsqueeze(axis)
    shape = list(v.shape)
    shape[axis] = n
    return v.broadcast_to(shape)


def attention_items(heads):
    return [(h, t) for h in range(heads) for t in range(NT)]


def attention_plan(heads, streams):
    items = attention_items(heads)
    plan = []
    for i in range(len(items) + 2):
        if i < len(items):
            plan += [("scores", i, s) for s in range(streams)]
        if 1 <= i <= len(items):
            plan.append(("turn", i - 1, 0))
        if i >= 2:
            plan.append(("values", i - 2, 0))
    return plan


def program(nc, I, O):
    with ExitStack() as ctx:
        def sb(name, shape, dt=F32):
            return ctx.enter_context(nc.sbuf_tensor(name, shape, dt))

        def sem(name):
            return ctx.enter_context(nc.semaphore(name))

        wring = sb("wring", [P, WS, WB])
        xT = sb("xT", [P, KD * T])
        hT = sb("hT", [P, KD, T])
        tmp = sb("tmp", [P, KD * T])
        arena = sb("arena", [P, 25600])
        cst = sb("cst", [P, C_COLS])
        cossin = sb("cossin", [P, 2, DEC_SEQ])
        wsm = sb("wsm", [P, S_COLS])
        lam_in = sb("lam_in", [64, 4])
        lam_pr = sb("lam_pr", [64, 2])
        lam_e = sb("lam_e", [P, 2])
        neglam = sb("neglam", [P, 1])
        csilu = sb("csilu", [P, KD * 2])
        modcol = sb("modcol", [P, 12 * 16])
        modA = sb("modA", [P, 4, KD, 2])
        std = sb("std", [P, T])
        gates_sb = sb("gates_sb", [P, 5 * 16])
        dsm = sb("dsm", [P, 7, 2, NT, H])
        att = sb("att", [P, 16])
        osd = sb("osd", [P, NT * H])

        ps = ctx.enter_context(nc.psum_tensor("ps", [P, 4, 1024], F32))

        def pair(slot, n=HT):
            return ps[:, slot, :].rearrange("p (b n) -> p b n", b=2)[:, :, 0:n]

        ident, ones = cst[:, C_ID:C_ID + P], cst[:, C_ONE:C_ONE + P]
        tri = [cst[:, C_TRI + d * P:C_TRI + (d + 1) * P] for d in range(2)]
        rot = cst[:, C_ROT:C_ROT + P]
        iota8 = cst[:, C_IOTA:C_IOTA + 8]
        eps = cst[:, C_EPS:C_EPS + 1]
        cos, sin = cossin[:, 0, :], cossin[:, 1, :]

        def chunks(base, n, width):
            return arena[:, base:base + n * width].rearrange("p (n w) -> p n w", n=n)

        xc = xT[:, :].rearrange("p (k t) -> p k t", k=KD)
        tc = tmp[:, :].rearrange("p (k t) -> p k t", k=KD)
        qkvT, zT = chunks(0, 12, T), chunks(7680, 4, T)
        qT, kT, vB = chunks(10240, H, T), chunks(12800, H, TK), chunks(15872, NT + 1, 512)
        pB, aB = chunks(18944, 4, T), chunks(21504, 2, T)
        qkraw, raw, cv = chunks(22784, 2, T), arena[:, 24064:24064 + 643], arena[:, 24708:24708 + 641]
        rtmp = std[:, 0:DEC_SEQ]
        tok = chunks(10240, NT, 1024)
        DTs, Ais = chunks(15360, NT, 1024), chunks(20480, NT, 1024)
        oS = chunks(5120, NT, 512)
        dE, dM, dC, dD, dT1 = (tmp[:, i * 1024:(i + 1) * 1024] for i in range(5))
        Sst = [hT[:, :, :].rearrange("p k t -> p (k t)")[:, i * 1024:(i + 1) * 1024] for i in range(2)]
        actT = chunks(0, FC, T)
        yacc = chunks(11 * T, NT, D)
        sg = tmp[:, 0:2 * T].rearrange("p (b t) -> p b t", b=2)
        qn, qr, kn, vC = chunks(0, HC, T), chunks(5120, 4, T), chunks(7680, HC, TK), chunks(13824, NT + 1, 1024)
        krT, ckv, cq = arena[:, 19968:19968 + TK], chunks(20736, 2, TK), chunks(22272, 3, T)
        krraw = arena[:, 24192:24192 + T]
        pC = tmp[:, 0:2 * T].rearrange("p (b t) -> p b t", b=2)
        aC = tmp[:, 2 * T:4 * T].rearrange("p (b t) -> p b t", b=2)
        qraw = tmp[:, 4 * T:6 * T].rearrange("p (b t) -> p b t", b=2)

        g_, beta, gcum, glast, eg, ed, el = (dsm[:, i, :, :, :] for i in range(7))

        w_full = [sem(f"w_full{s}") for s in range(WS)]
        ps_full = [sem(f"ps_full{s}") for s in range(4)]
        ps_free = [sem(f"ps_free{s}") for s in range(4)]
        act_step, dve_step, pool_step = sem("act_step"), sem("dve_step"), sem("pool_step")
        consts_in, x_in, caches_in, mla_caches_in, state_in = (
            sem(n) for n in ("consts_in", "x_in", "caches_in", "mla_caches_in", "state_in"))
        csilu_ready, lam_ready, lam_exp, modA_ready = (
            sem(n) for n in ("csilu_ready", "lam_ready", "lam_exp", "modA_ready"))
        sq_ready, std_ready, hs_ready, h_ready = (sem(n) for n in ("sq_ready", "std_ready", "hs_ready", "h_ready"))
        conv_ready, qkv_ready, cn_sq, cn_out = (sem(n) for n in ("conv_ready", "qkv_ready", "cn_sq", "cn_out"))
        gate_in, gate_e, gate_l, g_ready = (sem(n) for n in ("gate_in", "gate_e", "gate_l", "g_ready"))
        decay_in, decay_out = sem("decay_in"), sem("decay_out")
        mx_ready, a_ready = sem("mx_ready"), sem("a_ready")
        gb_ready, e_in, e_out, c_ready, dt_ready = (
            sem(n) for n in ("gb_ready", "e_in", "e_out", "c_ready", "dt_ready"))
        s_zero, r_ready, vd_ready = sem("s_zero"), sem("r_ready"), sem("vd_ready")
        os_ready, od_ready, on_ready = sem("os_ready"), sem("od_ready"), sem("on_ready")
        top_ready, top_exp, yacc_zero = sem("top_ready"), sem("top_exp"), sem("yacc_zero")
        kv_out, state_out, mla_out, y_out = (sem(n) for n in ("kv_out", "state_out", "mla_out", "y_out"))

        R = Ring(4)
        plan_b, plan_c = attention_plan(H, 2), attention_plan(HC, 1)
        rope_order = [("P", 0)] + [x for c in range(1, 8) for x in (("P", c), ("R", c - 1))] + [("R", 7)]
        uq_order = [("P", 0)] + [x for c in range(1, 4) for x in (("P", c), ("R", c - 1))] + [("R", 3)]
        DL = 4 + 3 * (LEVELS - 1) - 1
        SCAN = [(0, 0), (1, 4), (2, 3), (3, 2), (4, 1)]
        for stage, each, turns in (
                ("lam", 2, 1), ("mod", 2, 12), ("norm0", 1, 1), ("qkv", 12, 1), ("z", 4, 1), ("gat", 1, 1),
                ("qk", 16, 1), ("vb", NT, 1), ("l2", 8, 1), ("att0", len(plan_b), 1), ("obn", H, 1),
                ("cum", 1, 1), ("tri", DL * NT, 1), ("scan", 5 * NT, 1), ("onrm", NT, 1), ("eo", 4, 2),
                ("norm1", 1, 1), ("fgu", 2 * EC, 2), ("fdn", 2, 4),
                ("norm2", 1, 1), ("oi", 7, 1), ("mlan", 2, 1), ("uqn", HC, 1), ("uqr", 8, 1), ("kn", HC, 1),
                ("vv", NT + 1, 1), ("att1", len(plan_c), 1), ("oo", 4, 2),
                ("norm3", 1, 1), ("rt", 1, 1), ("moe", 2 * EC + 6, NE), ("yt", KD, 1), ("norm4", 1, 1)):
            R.plan(stage, each, turns)

        def take(stage, j, turn=0):
            s, n = R.use(stage, j, turn)
            if not (isinstance(n, int) and n == 0):
                nc.tensor.wait_ge(ps_free[s], n)
            return s

        def full(eng, stage, j, turn=0):
            s, n = R.use(stage, j, turn)
            eng.wait_ge(ps_full[s], n + 1)
            return s

        def done(eng, stage, j, turn=0):
            s, n = R.use(stage, j, turn)
            eng.wait_ge(ps_free[s], n + 1)

        W = Ring(WS)
        loads = {
            "mod": (I["w_mod"], WB, 4, 12, lambda j: ("mod", 0)),
            "qkv": (I["w_ev"][0:6], WB, 6, 1, lambda j: ("qkv", 2 * j + 1)),
            "z": (I["w_ev"][6:8], WB, 2, 1, lambda j: ("z", 2 * j + 1)),
            "gat": (I["w_evg"], KD * 16, 1, 1, lambda j: ("gat", 0)),
            "qk": (I["w_ev"][8:12], WB, 4, 1, lambda j: ("qk", rope_order.index(("P", 2 * j + 1)))),
            "vb": (I["w_ev"][12:14], WB, 2, 1, lambda j: ("vb", NT - 1)),
            "eo": (I["w_eo"], WB, 2, 2, lambda j: ("eo", 2 * j + 1)),
            "fgu": (I["w_gu"], WB, EC, 2, lambda j: ("fgu", 2 * j + 1)),
            "fdn": (I["w_dn"], LK * P, 4, 4, lambda j: ("fdn", j // 2)),
            "oi": (I["w_oi"], WB, 3, 1, lambda j: ("oi", 2 * j + 1)),
            "uqn": (I["w_uq"][0:2], 1536, 2, 1, lambda j: ("uqn", 4 * j + 3)),
            "uqr": (I["w_uq"][2:3], 1536, 1, 1, lambda j: ("uqr", uq_order.index(("P", 3)))),
            "kn": (I["w_ukv"][0:1], WB, 1, 1, lambda j: ("kn", HC - 1)),
            "vv": (I["w_ukv"][1:2], WB, 1, 1, lambda j: ("vv", NT)),
            "oo": (I["w_oo"], WB, 2, 2, lambda j: ("oo", 2 * j + 1)),
            "rt": (I["w_rt"], 64, 1, 1, lambda j: ("rt", 0)),
            "moe": (None, WB, EC + 6, NE, lambda j: ("moe", 2 * j + 1 if j < EC else 2 * EC + 3 * ((j - EC) // 3) + 2)),
        }
        history = [[] for _ in range(WS)]
        for stage, (_, _, each, turns, _) in loads.items():
            W.plan(stage, each, turns)
            for turn in range(turns):
                for j in range(each):
                    history[j % WS].append((stage, j, turn))

        def block(stage, j, turn=0):
            s, n = W.use(stage, j, turn)
            nc.tensor.wait_ge(w_full[s], 16 * (n + 1))
            return wring[:, s, :]

        def load(sync, stage, j, turn=0):
            dram, size, each, _, _ = loads[stage]
            s, n = W.use(stage, j, turn)
            if isinstance(turn, int):
                held = history[s][n - 1] if n else None
            elif j >= WS:
                held = (stage, j - WS, turn)
            else:
                held = (stage, max(i for i in range(each) if i % WS == s), turn - 1)
            if held:
                pstage, pj = loads[held[0]][4](held[1])
                full(sync, pstage, pj, held[2])
            if stage == "moe":
                if j < EC:
                    src = I["w_mgu"][bass.ds(turn * EC + j, 1), :, :]
                else:
                    half, part = (j - EC) // 3, (j - EC) % 3
                    size = 4 * 512 if part < 2 else 3 * 512
                    src = I["w_mdn"][bass.ds(turn * 2 + half, 1), :, part * WB:part * WB + size]
            else:
                src = dram[bass.ds(turn * each + j, 1), :, 0:size]
            sync.dma_start(wring[:, s, 0:size], src.rearrange("a p n -> p (a n)")).then_inc(w_full[s], 16)

        def load_stage(sync, stage):
            each, turns = loads[stage][2:4]
            ahead = min(WS, each)
            for j in range(ahead):
                load(sync, stage, j, 0)
            if turns > 1:
                with sync.Fori(0, turns - 1) as turn:
                    for j in range(ahead, each):
                        load(sync, stage, j, turn)
                    for j in range(ahead):
                        load(sync, stage, j, turn + 1)
            for j in range(ahead, each):
                load(sync, stage, j, turns - 1)

        def mm(out, lhsT, rhs, first, last):
            return nc.tensor.matmul(out, lhsT, rhs, start=first, stop=last)

        def pe_linear(stage, j, turn, weights, source, n=HT):
            s = take(stage, j, turn)
            out = pair(s, n)
            nk = len(weights)
            for half in range(2):
                for k in range(nk):
                    last = mm(out[:, half, :], weights[k], source(k, half * n, half * n + n), k == 0, k == nk - 1)
            last.then_inc(ps_full[s], 1)
            return s

        def from_h(k, a, b):
            return hT[:, k, a:b]

        def cols(w, nk, width, c):
            return [w[:, k * width + c * P:k * width + (c + 1) * P] for k in range(nk)]

        def pe_lam():
            nc.tensor.wait_ge(consts_in, 16 * 4)
            nc.tensor.wait_ge(lam_ready, 1)
            for i in range(2):
                s = take("lam", i)
                mm(ps[:, s, 0:1], cst[0:64, C_ONE:C_ONE + P], lam_pr[:, i:i + 1], True, True).then_inc(ps_full[s], 1)

        def pe_mod():
            nc.tensor.wait_ge(csilu_ready, 1)
            with nc.tensor.Fori(0, 12) as i:
                s = take("mod", 0, i)
                for b in range(4):
                    w = block("mod", b, i)
                    for kk in range(2):
                        k = 2 * b + kk
                        for half in range(2):
                            last = mm(ps[0:2, s, half * 512:(half + 1) * 512], csilu[:, 2 * k:2 * k + 2],
                                      w[:, kk * D + half * 512:kk * D + (half + 1) * 512], k == 0, k == KD - 1)
                last.then_inc(ps_full[s], 1)
                done(nc.tensor, "mod", 0, i)
                s = take("mod", 1, i)
                for j in range(KD):
                    last = mm(ps[:, s, 2 * j:2 * j + 2], tmp[0:2, j * P:(j + 1) * P], ident[0:2, 0:2], True, True)
                last.then_inc(ps_full[s], 1)

        def dve_mod(dve):
            with dve.Fori(0, 12) as i:
                s = full(dve, "mod", 0, i)
                nc.vector.tensor_copy(tmp[0:2, 0:D], ps[0:2, s, :]).then_inc(ps_free[s], 1)
                s = full(dve, "mod", 1, i)
                nc.vector.tensor_tensor(
                    modcol[:, bass.ds(i * 16, 16)].rearrange("p (k c) -> p k c", c=2),
                    ps[:, s, 0:16].rearrange("p (k c) -> p k c", c=2),
                    spread(wsm[:, bass.ds(i * 8 + S_MODB, 8)], 2, 2), ALU.add).then_inc(ps_free[s], 1)
            done(dve, "mod", 1, 11)
            for n, m in enumerate((1, 4, 7, 10)):
                last = nc.vector.scalar_tensor_tensor(
                    modA[:, n, :, :], modcol[:, m * 16:m * 16 + 16].rearrange("p (k c) -> p k c", c=2), 1.0,
                    spread(wsm[:, S_NORM + n * 8:S_NORM + n * 8 + 8], 2, 2), ALU.add, ALU.mult)
            last.then_inc(modA_ready, 1)

        def act_norm(act, n, x_done):
            x_done(act)
            for k in range(KD):
                nc.scalar.activation(tc[:, k, :], xc[:, k, :], ACT.Square).then_inc(sq_ready, 1)
            s = full(act, f"norm{n}", 0)
            nc.scalar.activation(std[:, :].rearrange("p (b n) -> p b n", b=2), pair(s), ACT.Sqrt,
                                 bias=eps, scale=1.0 / D).then_inc(ps_free[s], 1)
            if n < 4:
                m = (0, 3, 6, 9)[n]
                if n == 0:
                    act.wait_ge(modA_ready, 1)
                for k in range(KD):
                    act.wait_ge(hs_ready, 8 * n + k + 1)
                    for a, b, c in SEGS:
                        last = nc.scalar.activation(hT[:, k, a:b], hT[:, k, a:b], ACT.Identity,
                                                    bias=modcol[:, m * 16 + 2 * k + c:m * 16 + 2 * k + c + 1])
                    last.then_inc(h_ready, 1)

        def pe_norm(n):
            s = take(f"norm{n}", 0)
            for k in range(KD):
                nc.tensor.wait_ge(sq_ready, 8 * n + k + 1)
                for half in range(2):
                    last = nc.tensor.matmul(pair(s)[:, half, :], ones, tc[:, k, half * HT:(half + 1) * HT],
                                            start=(k == 0), stop=(k == KD - 1))
            last.then_inc(ps_full[s], 1)

        def dve_norm(dve, st, n):
            done(dve, f"norm{n}", 0)
            st.then(nc.vector.reciprocal(std[:, :], std[:, :]))
            if n == 0:
                dve.wait_ge(modA_ready, 1)
            for k in range(KD):
                for a, b, c in (SEGS if n < 4 else ((0, T, 0),)):
                    A = modA[:, n, k, c:c + 1] if n < 4 else wsm[:, S_NORM + 32 + k:S_NORM + 33 + k]
                    last = nc.vector.scalar_tensor_tensor(hT[:, k, a:b], xc[:, k, a:b], A, std[:, a:b],
                                                          ALU.mult, ALU.mult)
                last.then_inc(hs_ready, 1)

        def act_colnorm(act, stage, groups, base, scale):
            i = 0
            for group in groups:
                for src, _, _ in group:
                    nc.scalar.activation(tc[:, i, :], src, ACT.Square).then_inc(cn_sq, 1)
                    i += 1
            i = 0
            for g, group in enumerate(groups):
                s = full(act, stage, g)
                nc.scalar.activation(tc[:, i, :].rearrange("p (b n) -> p b n", b=2), pair(s), ACT.Sqrt,
                                     bias=eps, scale=scale[g]).then_inc(ps_free[s], 1)
                i += len(group)

        def pe_colnorm(stage, groups, base):
            i = 0
            for g, group in enumerate(groups):
                s = take(stage, g)
                nc.tensor.wait_ge(cn_sq, base + i + len(group))
                for half in range(2):
                    for c in range(len(group)):
                        last = mm(pair(s)[:, half, :], ones, tc[:, i + c, half * HT:(half + 1) * HT],
                                  c == 0, c == len(group) - 1)
                last.then_inc(ps_full[s], 1)
                i += len(group)

        def dve_colnorm(dve, st, stage, groups):
            i = 0
            for g, group in enumerate(groups):
                done(dve, stage, g)
                st.then(nc.vector.reciprocal(tc[:, i, :], tc[:, i, :]))
                for src, dst, w in group:
                    last = nc.vector.scalar_tensor_tensor(dst, src, w, tc[:, i, :], ALU.mult, ALU.mult)
                last.then_inc(cn_out, 1)
                i += len(group)

        l2_groups = [[(qkvT[:, c, :], qkvT[:, c, :], P ** -0.5 if c < H else 1.0)] for c in range(8)]
        obn_groups = [[(hT[:, H + h, :], hT[:, H + h, :], wsm[:, S_SUBLN:S_SUBLN + 1])] for h in range(H)]
        mla_groups = [[(cq[:, c, :], cq[:, c, :], wsm[:, S_QN + c:S_QN + c + 1]) for c in range(3)],
                      [(ckv[:, c, 0:T], ckv[:, c, 0:T], wsm[:, S_KVN + c:S_KVN + c + 1]) for c in range(2)]]

        def pe_even_in():
            nc.tensor.wait_ge(h_ready, 8)
            for c in range(12):
                if c % 2 == 0:
                    w = block("qkv", c // 2)
                pe_linear("qkv", c, 0, cols(w, KD, 256, c % 2), from_h)
            for c in range(4):
                if c % 2 == 0:
                    w = block("z", c // 2)
                pe_linear("z", c, 0, cols(w, KD, 256, c % 2), from_h)
            w, s = block("gat", 0), take("gat", 0)
            for t in range(NT):
                for k in range(KD):
                    last = mm(ps[:, s, t * 16:(t + 1) * 16], hT[:, k, t * P:(t + 1) * P], w[:, k * 16:(k + 1) * 16],
                              k == 0, k == KD - 1)
            last.then_inc(ps_full[s], 1)
            for j, (what, c) in enumerate(rope_order):
                if what == "P":
                    if c % 2 == 0:
                        w = block("qk", c // 2)
                    pe_linear("qk", j, 0, cols(w, KD, 256, c % 2), from_h)
                else:
                    done(nc.tensor, "qk", rope_order.index(("P", c)))
                    s = take("qk", j)
                    mm(ps[:, s, 0:DEC_SEQ], rot, qkraw[:, c % 2, SEQ:T], True, True).then_inc(ps_full[s], 1)
            w = [block("vb", 0), block("vb", 1)]
            for t in range(NT):
                s = take("vb", t)
                for b in range(2):
                    for k in range(KD):
                        last = mm(ps[:, s, b * 256:(b + 1) * 256], hT[:, k, t * P:(t + 1) * P],
                                  w[b][:, k * 256:(k + 1) * 256], k == 0, k == KD - 1)
                last.then_inc(ps_full[s], 1)

        def act_even_in(act):
            for c in range(12):
                s = full(act, "qkv", c)
                nc.scalar.activation(raw[:, 1:1 + SEQ], ps[:, s, 0:SEQ], ACT.Copy)
                nc.scalar.activation(raw[:, 2 + SEQ:2 + HT], ps[:, s, SEQ:HT], ACT.Copy)
                nc.scalar.activation(raw[:, 2 + HT:2 + T], ps[:, s, 512:512 + HT], ACT.Copy).then_inc(ps_free[s], 1)
                act.wait_ge(conv_ready, c + 1)
                nc.scalar.activation(qkvT[:, c, 0:SEQ], cv[:, 0:SEQ], ACT.Silu)
                nc.scalar.activation(qkvT[:, c, SEQ:T], cv[:, SEQ + 1:T + 1], ACT.Silu).then_inc(qkv_ready, 1)
            for c in range(4):
                s = full(act, "z", c)
                nc.scalar.activation(zT[:, c, :].rearrange("p (b n) -> p b n", b=2), pair(s), ACT.Silu
                                     ).then_inc(ps_free[s], 1)
            act.wait_ge(gate_in, 1)
            gr = gates_sb[:, :].rearrange("p (t c) -> p t c", c=16)
            nc.scalar.activation(gr[:, :, 8:16], gr[:, :, 8:16], ACT.Exp, scale=-1.0)
            nc.scalar.activation(dsm[:, 2, :, :, :].rearrange("p a t h -> p (a t h)"),
                                 dsm[:, 2, :, :, :].rearrange("p a t h -> p (a t h)"), ACT.Exp, scale=-1.0)
            nc.scalar.activation(wsm[:, S_ALOG:S_ALOG + 8], wsm[:, S_ALOG:S_ALOG + 8], ACT.Exp).then_inc(gate_e, 1)
            act.wait_ge(gate_e, 1)
            nc.scalar.activation(dsm[:, 2, :, :, :].rearrange("p a t h -> p (a t h)"),
                                 dsm[:, 2, :, :, :].rearrange("p a t h -> p (a t h)"), ACT.Ln,
                                 bias=ones[:, 0:1]).then_inc(gate_l, 1)
            for c in range(8):
                j = rope_order.index(("P", c))
                if c >= 2:
                    done(act, "qk", rope_order.index(("R", c - 2)))
                s = full(act, "qk", j)
                nc.scalar.activation(qkraw[:, c % 2, :].rearrange("p (b n) -> p b n", b=2), pair(s), ACT.Copy,
                                     scale=64 ** -0.5 if c < H else 1.0).then_inc(ps_free[s], 1)

        def dve_rope(st, raw_in, dst, s, prompt=True):
            nc.vector.tensor_copy(dst[:, 0:SEQ], raw_in[:, 0:SEQ])
            nc.vector.tensor_tensor(dst[:, SEQ:T], raw_in[:, SEQ:T], cos, ALU.mult)
            st.then(nc.vector.tensor_tensor(rtmp, ps[:, s, 0:DEC_SEQ], sin, ALU.mult))
            nc.vector.tensor_tensor(dst[:, SEQ:T], dst[:, SEQ:T], rtmp, ALU.add).then_inc(ps_free[s], 1)

        def dve_even_in(dve, st):
            for c in range(12):
                done(dve, "qkv", c)
                if c:
                    dve.wait_ge(qkv_ready, c)
                cw = wsm[:, S_CONV + 3 * c:S_CONV + 3 * c + 3]
                st.then(nc.vector.tensor_scalar(cv, raw[:, 0:641], cw[:, 0:1], None, ALU.mult))
                st.then(nc.vector.scalar_tensor_tensor(cv, raw[:, 1:642], cw[:, 1:2], cv, ALU.mult, ALU.add))
                nc.vector.scalar_tensor_tensor(cv, raw[:, 2:643], cw[:, 2:3], cv, ALU.mult, ALU.add
                                               ).then_inc(conv_ready, 1)
            s = full(dve, "gat", 0)
            nc.vector.tensor_copy(gates_sb[:, :], ps[:, s, 0:80]).then_inc(ps_free[s], 1)
            done(dve, "gat", 0)
            gr = gates_sb[:, :].rearrange("p (t d h) -> p t d h", d=4, h=H)
            sp = dsm[:, 2, :, :, :]
            for d in range(2):
                last = nc.vector.tensor_tensor(g_[:, d, :, :], gr[:, :, d, :],
                                               spread(wsm[:, S_DTB + d * H:S_DTB + (d + 1) * H], 1, NT), ALU.add)
            st.then(last)
            st.then(nc.vector.tensor_scalar(sp, g_, -1.0, None, ALU.mult))
            nc.vector.tensor_tensor(sp, sp, g_, ALU.max).then_inc(gate_in, 1)
            st.then(nc.vector.tensor_scalar(g_, g_, 0.0, None, ALU.max))
            dve.wait_ge(gate_e, 1)
            dve.wait_ge(gate_l, 1)
            st.then(nc.vector.tensor_tensor(g_, g_, sp, ALU.add))
            for d in range(2):
                nc.vector.scalar_tensor_tensor(g_[:, d, :, :], g_[:, d, :, :], -1.0,
                                               spread(wsm[:, S_ALOG + d * H:S_ALOG + (d + 1) * H], 1, NT),
                                               ALU.mult, ALU.mult)
                last = nc.vector.tensor_scalar(beta[:, d, :, :], gr[:, :, 2 + d, :], 1.0, None, ALU.add)
            st.then(last)
            nc.vector.reciprocal(beta, beta).then_inc(g_ready, 1)
            for c in range(8):
                s = full(dve, "qk", rope_order.index(("R", c)))
                if c:
                    done(dve, "qk", rope_order.index(("R", c - 1)))
                dve_rope(st, qkraw[:, c % 2, :], qT[:, c, :] if c < H else kT[:, c - H, 0:T], s)
            for t in range(NT):
                s = full(dve, "vb", t)
                nc.vector.tensor_copy(vB[:, t, :], ps[:, s, 0:512]).then_inc(ps_free[s], 1)

        def attention(heads, streams, stage, order, scores, values, probs, turned, item_base, stat):
            items = attention_items(heads)
            at = {x: j for j, x in enumerate(order)}
            nstat = 3 * streams

            def cells(i):
                return att[:, (i % 2) * 8:(i % 2) * 8 + 8]

            def pe():
                for j, (what, i, st_) in enumerate(order):
                    h, t = items[i]
                    blocks = (0,) if t == 0 else tuple(range(1, NT + 1))
                    if what == "scores":
                        s = take(stage, j)
                        if t == 0:
                            terms = scores(h, t, st_, 0, P)
                            for n, (q, k) in enumerate(terms):
                                last = mm(ps[:, s, 0:P], q, k, n == 0, n == len(terms) - 1)
                        else:
                            for half in range(2):
                                terms = scores(h, t, st_, P + half * HT, P + (half + 1) * HT)
                                for n, (q, k) in enumerate(terms):
                                    last = mm(pair(s)[:, half, :], q, k, n == 0, n == len(terms) - 1)
                    elif what == "turn":
                        nc.tensor.wait_ge(a_ready, item_base + i + 1)
                        s = take(stage, j)
                        for n in range(len(blocks)):
                            last = nc.tensor.transpose(ps[:, s, n * P:(n + 1) * P],
                                                       probs(i, 0)[:, n * P:(n + 1) * P], ident)
                    else:
                        done(nc.tensor, stage, at[("turn", i, 0)])
                        s = take(stage, j)
                        for n, b in enumerate(blocks):
                            last = mm(ps[:, s, 0:P], values(h, b), turned(i)[:, n * P:(n + 1) * P],
                                      n == 0, n == len(blocks) - 1)
                    last.then_inc(ps_full[s], 1)

            def view(i, ap, s):
                if items[i][1] == 0:
                    return ps[:, s, 0:P], ap[:, 0:P]
                return pair(s), ap.rearrange("p (b n) -> p b n", b=2)

            def dve(eng, st):
                for i in range(len(items) + 2):
                    if i < len(items):
                        h, t = items[i]
                        for st_ in range(streams):
                            s = full(eng, stage, at[("scores", i, st_)])
                            src, _ = view(i, probs(i, st_), s)
                            nc.vector.tensor_reduce(cells(i)[:, st_:st_ + 1], src, AX.X if t == 0 else AX.XY,
                                                    ALU.max, negate=True).then_inc(mx_ready, 1)
                        for st_ in range(streams):
                            done(eng, stage, at[("scores", i, st_)])
                        w = P if t == 0 else T
                        sums, inv = cells(i)[:, 2:2 + streams], cells(i)[:, 4:4 + streams]
                        st.then(nc.vector.reciprocal(inv, sums))
                        if streams == 1:
                            nc.vector.tensor_scalar(probs(i, 0)[:, 0:w], probs(i, 0)[:, 0:w], inv[:, 0:1], None,
                                                    ALU.mult).then_inc(a_ready, 1)
                        else:
                            nc.vector.tensor_scalar(probs(i, 0)[:, 0:w], probs(i, 0)[:, 0:w], inv[:, 0:1], None,
                                                    ALU.mult)
                            st.then(nc.vector.tensor_scalar(inv[:, 1:2], inv[:, 1:2], neglam[:, 0:1], None, ALU.mult))
                            nc.vector.scalar_tensor_tensor(probs(i, 0)[:, 0:w], probs(i, 1)[:, 0:w], inv[:, 1:2],
                                                           probs(i, 0)[:, 0:w], ALU.mult, ALU.add
                                                           ).then_inc(a_ready, 1)
                    if i >= 2:
                        h, t = items[i - 2]
                        s = full(eng, stage, at[("values", i - 2, 0)])
                        nc.vector.tensor_copy(hT[:, stat + h, t * P:(t + 1) * P], ps[:, s, 0:P]
                                              ).then_inc(ps_free[s], 1)

            def act(eng):
                for i in range(len(items) + 1):
                    if i < len(items):
                        for st_ in range(streams):
                            eng.wait_ge(mx_ready, (item_base * 2 if streams == 1 else 0) + i * streams + st_ + 1)
                            s, _ = R.use(stage, at[("scores", i, st_)])
                            src, dst = view(i, probs(i, st_), s)
                            nc.scalar.activation(dst, src, ACT.Exp, bias=cells(i)[:, st_:st_ + 1],
                                                 accum_out=cells(i)[:, 2 + st_:3 + st_]).then_inc(ps_free[s], 1)
                    if i >= 1:
                        s = full(eng, stage, at[("turn", i - 1, 0)])
                        w = P if items[i - 1][1] == 0 else T
                        nc.scalar.activation(turned(i - 1)[:, 0:w], ps[:, s, 0:w], ACT.Copy).then_inc(ps_free[s], 1)

            return pe, dve, act

        def diff_scores(h, t, st_, a, b):
            r = slice(st_ * ROPE, (st_ + 1) * ROPE)
            return [(qT[r, h, t * P:(t + 1) * P], kT[r, h, a:b])]

        def mla_scores(h, t, st_, a, b):
            r = slice((h % 2) * ROPE, (h % 2 + 1) * ROPE)
            return [(qn[:, h, t * P:(t + 1) * P], kn[:, h, a:b]), (qr[r, h // 2, t * P:(t + 1) * P], krT[r, a:b])]

        att0 = attention(H, 2, "att0", plan_b, diff_scores, lambda h, b: vB[:, b, h * P:(h + 1) * P],
                         lambda i, s: pB[:, (i % 2) * 2 + s, :], lambda i: aB[:, i % 2, :], 0, H)
        att1 = attention(HC, 1, "att1", plan_c, mla_scores, lambda h, b: vC[:, b, h * P:(h + 1) * P],
                         lambda i, s: pC[:, i % 2, :], lambda i: aC[:, i % 2, :], H * NT, 0)

        def quad(ap):
            return ap.rearrange("p (d h c) -> p d h c", d=2, h=H)

        def per_head(ap):
            return ap.rearrange("p (h c) -> p h c", h=H)

        gb = dT1
        TR = {n: i for i, n in enumerate(["tok", "gram", "grow", "C0"])}
        for lv in range(1, LEVELS):
            for n, what in enumerate(("T1", "XT", "X")):
                TR[(what, lv)] = 4 + 3 * (lv - 1) + n

        def prod(t, what):
            return DL * t + TR[what]

        def pool_delta(pool):
            for t in range(NT):
                if t == 0:
                    pool.wait_ge(g_ready, 1)
                    full(pool, "obn", H - 1)
                    pool.wait_ge(cn_out, 8 + H)
                else:
                    full(pool, "tri", prod(t - 1, ("XT", LEVELS - 1)))
                for d in range(2):
                    last = nc.gpsimd.tensor_copy(quad(gb)[:, d, :, :], spread(g_[:, d, t, :], 2, P))
                last.then_inc(gb_ready, 1)
                done(pool, "tri", prod(t, "gram"))
                for lv in range(LEVELS):
                    if lv == 1:
                        pool.wait_ge(dt_ready, t + 1)
                        full(pool, "tri", prod(t, "C0"))
                    if lv > 1:
                        full(pool, "tri", prod(t, ("T1", lv - 1)))
                    for d in range(2):
                        mask = cst[:, C_LVL + (lv * 2 + d) * P:C_LVL + (lv * 2 + d + 1) * P]
                        last = nc.gpsimd.tensor_tensor(quad(dC)[:, d, :, :], quad(dM)[:, d, :, :],
                                                       spread(mask, 1, H), ALU.mult)
                    last.then_inc(c_ready, 1)

        def pe_delta():
            nc.tensor.wait_ge(g_ready, 1)
            nc.tensor.wait_ge(cn_out, 8)
            s = take("cum", 0)
            for d in range(2):
                mm(ps[:, s, d * 20:d * 20 + 20], tri[d], g_[:, d, :, :].rearrange("p t h -> p (t h)"), True, True)
            mm(ps[:, s, 40:80], ones, g_.rearrange("p d t h -> p (d t h)"), True, True).then_inc(ps_full[s], 1)
            for t in range(NT):
                a, b = t * P, (t + 1) * P
                s = take("tri", prod(t, "tok"))
                for h in range(H):
                    nc.tensor.transpose(ps[:, s, h * P:(h + 1) * P], qkvT[:, H + h, a:b], ident)
                for h in range(H):
                    last = nc.tensor.transpose(ps[:, s, 512 + h * P:512 + (h + 1) * P], qkvT[:, 2 * H + h, a:b], ident)
                last.then_inc(ps_full[s], 1)
                s = take("tri", prod(t, "gram"))
                for h in range(H):
                    mm(ps[:, s, h * P:(h + 1) * P], qkvT[:, H + h, a:b], qkvT[:, H + h, a:b], True, True)
                for h in range(H):
                    last = mm(ps[:, s, 512 + h * P:512 + (h + 1) * P], qkvT[:, H + h, a:b], qkvT[:, h, a:b], True, True)
                last.then_inc(ps_full[s], 1)
                nc.tensor.wait_ge(gb_ready, t + 1)
                s = take("tri", prod(t, "grow"))
                for i in range(2 * H):
                    last = mm(ps[:, s, i * P:(i + 1) * P], gb[:, i * P:(i + 1) * P], tri[i // H], True, True)
                last.then_inc(ps_full[s], 1)
                nc.tensor.wait_ge(c_ready, LEVELS * t + 1)
                s = take("tri", prod(t, "C0"))
                for i in range(2 * H):
                    last = nc.tensor.transpose(ps[:, s, i * P:(i + 1) * P], dC[:, i * P:(i + 1) * P], ident)
                last.then_inc(ps_full[s], 1)
                nc.tensor.wait_ge(dt_ready, t + 1)
                for lv in range(1, LEVELS):
                    nc.tensor.wait_ge(c_ready, LEVELS * t + lv + 1)
                    done(nc.tensor, "tri", prod(t, "C0" if lv == 1 else ("X", lv - 1)))
                    s = take("tri", prod(t, ("T1", lv)))
                    for i in range(2 * H):
                        r = slice(i * P, (i + 1) * P)
                        last = mm(ps[:, s, r], dC[:, r], dD[:, r], True, True)
                    last.then_inc(ps_full[s], 1)
                    done(nc.tensor, "tri", prod(t, ("T1", lv)))
                    if lv > 1:
                        done(nc.tensor, "tri", prod(t, ("XT", lv - 1)))
                    s = take("tri", prod(t, ("XT", lv)))
                    for i in range(2 * H):
                        r = slice(i * P, (i + 1) * P)
                        last = mm(ps[:, s, r], dT1[:, r], DTs[:, t, r], True, True)
                    last.then_inc(ps_full[s], 1)
                    if lv < LEVELS - 1:
                        s = take("tri", prod(t, ("X", lv)))
                        for i in range(2 * H):
                            r = slice(i * P, (i + 1) * P)
                            last = mm(ps[:, s, r], DTs[:, t, r], dT1[:, r], True, True)
                        last.then_inc(ps_full[s], 1)

        def act_delta(act):
            act.wait_ge(decay_in, 1)
            flat = [dsm[:, i, :, :, :].rearrange("p d t h -> p (d t h)") for i in range(7)]
            nc.scalar.activation(flat[4], flat[2], ACT.Exp)
            nc.scalar.activation(flat[5], flat[5], ACT.Exp)
            nc.scalar.activation(flat[6], flat[3], ACT.Exp).then_inc(decay_out, 1)
            act.wait_ge(kv_out, 32)
            for t in range(NT):
                s = full(act, "tri", prod(t, "tok"))
                nc.scalar.activation(tok[:, t, :], ps[:, s, :], ACT.Copy).then_inc(ps_free[s], 1)
                act.wait_ge(e_in, t + 1)
                nc.scalar.activation(dE, dE, ACT.Exp).then_inc(e_out, 1)
                for lv in range(1, LEVELS):
                    s = full(act, "tri", prod(t, ("T1", lv)))
                    nc.scalar.activation(dT1, ps[:, s, :], ACT.Copy).then_inc(ps_free[s], 1)

        def dve_delta(dve, st):
            s = full(dve, "cum", 0)
            nc.vector.tensor_copy(dsm[:, 2:4, :, :, :].rearrange("p i d t h -> p (i d t h)"), ps[:, s, 0:80]
                                  ).then_inc(ps_free[s], 1)
            done(dve, "cum", 0)
            nc.vector.tensor_tensor(ed, glast, gcum, ALU.subtract).then_inc(decay_in, 1)
            dve.wait_ge(kv_out, 32)
            for t in range(NT):
                s = full(dve, "tri", prod(t, "grow"))
                if t == 0:
                    dve.wait_ge(cn_out, 8 + H)
                for d in range(2):
                    last = nc.vector.tensor_tensor(quad(dE)[:, d, :, :], quad(ps[:, s, :])[:, d, :, :],
                                                   spread(gcum[:, d, t, :], 2, P), ALU.subtract)
                last.then_inc(ps_free[s], 1)
                done(dve, "tri", prod(t, "grow"))
                for d in range(2):
                    last = nc.vector.scalar_tensor_tensor(
                        quad(dE)[:, d, :, :], quad(dE)[:, d, :, :], 0.0,
                        spread(cst[:, C_NEG + d * P:C_NEG + (d + 1) * P], 1, H), ALU.min, ALU.add)
                last.then_inc(e_in, 1)
                dve.wait_ge(e_out, t + 1)
                s = full(dve, "tri", prod(t, "gram"))
                for d in range(2):
                    nc.vector.tensor_tensor(per_head(Ais[:, t, d * 512:(d + 1) * 512]), per_head(ps[:, s, 512:1024]),
                                            quad(dE)[:, d, :, :], ALU.mult)
                    last = nc.vector.tensor_tensor(quad(dM)[:, d, :, :], quad(dE)[:, d, :, :],
                                                   spread(beta[:, d, t, :], 2, P), ALU.mult)
                st.then(last)
                for d in range(2):
                    last = nc.vector.tensor_tensor(quad(dM)[:, d, :, :], per_head(ps[:, s, 0:512]),
                                                   quad(dM)[:, d, :, :], ALU.mult)
                last.then_inc(ps_free[s], 1)
                done(dve, "tri", prod(t, "gram"))
                dve.wait_ge(c_ready, LEVELS * t + 1)
                nc.vector.tensor_tensor(DTs[:, t, :].rearrange("p (i c) -> p i c", c=P), spread(ident, 1, 2 * H),
                                        dC.rearrange("p (i c) -> p i c", c=P), ALU.subtract).then_inc(dt_ready, 1)
                s = full(dve, "tri", prod(t, "C0"))
                nc.vector.tensor_tensor(dD.rearrange("p (i c) -> p i c", c=P), spread(ident, 1, 2 * H),
                                        ps[:, s, :].rearrange("p (i c) -> p i c", c=P), ALU.subtract
                                        ).then_inc(ps_free[s], 1)
                for lv in range(1, LEVELS):
                    sx = full(dve, "tri", prod(t, ("XT", lv)))
                    if lv < LEVELS - 1:
                        s = full(dve, "tri", prod(t, ("X", lv)))
                        done(dve, "tri", prod(t, "C0" if lv == 1 else ("X", lv - 1)))
                        nc.vector.tensor_tensor(dD, dD, ps[:, s, :], ALU.subtract).then_inc(ps_free[s], 1)
                    if lv == 1:
                        dve.wait_ge(dt_ready, t + 1)
                    else:
                        done(dve, "tri", prod(t, ("XT", lv - 1)))
                    nc.vector.tensor_tensor(DTs[:, t, :], DTs[:, t, :], ps[:, sx, :], ALU.subtract
                                            ).then_inc(ps_free[sx], 1)

        sR, sV, sD, sO = dE, dM, dC, dD

        def pe_scan():
            nc.tensor.wait_ge(s_zero, 1)
            nc.tensor.wait_ge(state_in, 16)
            done(nc.tensor, "tri", prod(NT - 1, ("XT", LEVELS - 1)))
            for i, tiles in enumerate(SCAN):
                S = Sst[min(i, 1)]
                if i > 1:
                    done(nc.tensor, "scan", 5 * (i - 1) + 4)
                for n, base in ((0, H), (1, 0)):
                    s = take("scan", 5 * i + n)
                    for j in range(2 * H):
                        d, h = j // H, j % H
                        t = tiles[d]
                        last = mm(ps[:, s, j * P:(j + 1) * P], qkvT[:, base + h, t * P:(t + 1) * P],
                                  S[:, j * P:(j + 1) * P], True, True)
                    last.then_inc(ps_full[s], 1)
                nc.tensor.wait_ge(r_ready, i + 1)
                s = take("scan", 5 * i + 2)
                for j in range(2 * H):
                    r = slice(j * P, (j + 1) * P)
                    last = mm(ps[:, s, r], DTs[:, tiles[j // H], r], sR[:, r], True, True)
                last.then_inc(ps_full[s], 1)
                done(nc.tensor, "scan", 5 * i + 2)
                s = take("scan", 5 * i + 3)
                for j in range(2 * H):
                    r = slice(j * P, (j + 1) * P)
                    last = mm(ps[:, s, r], Ais[:, tiles[j // H], r], sV[:, r], True, True)
                last.then_inc(ps_full[s], 1)
                nc.tensor.wait_ge(vd_ready, i + 1)
                s = take("scan", 5 * i + 4)
                for j in range(2 * H):
                    r = slice(j * P, (j + 1) * P)
                    last = mm(ps[:, s, r], tok[:, tiles[j // H], (j % H) * P:(j % H + 1) * P], sD[:, r], True, True)
                last.then_inc(ps_full[s], 1)

        def dve_scan(dve, st):
            dve.wait_ge(decay_out, 1)
            seen = set()
            for i, tiles in enumerate(SCAN):
                S = Sst[min(i, 1)]

                def scaled(out, inp, factor):
                    for d, t in enumerate(tiles):
                        last = nc.vector.tensor_tensor(quad(out)[:, d, :, :], quad(inp)[:, d, :, :],
                                                       spread(factor[:, d, t, :], 2, P), ALU.mult)
                    return last

                s = full(dve, "scan", 5 * i)
                scaled(sR, ps[:, s, :], eg).then_inc(ps_free[s], 1)
                done(dve, "scan", 5 * i)
                for d, t in enumerate(tiles):
                    last = nc.vector.tensor_tensor(sR[:, d * 512:(d + 1) * 512], tok[:, t, 512:1024],
                                                   sR[:, d * 512:(d + 1) * 512], ALU.subtract)
                last.then_inc(r_ready, 1)
                s = full(dve, "scan", 5 * i + 1)
                scaled(sO, ps[:, s, :], eg).then_inc(ps_free[s], 1)
                st.then(scaled(S, S, el))
                s = full(dve, "scan", 5 * i + 2)
                scaled(sV, ps[:, s, :], beta).then_inc(ps_free[s], 1)
                done(dve, "scan", 5 * i + 2)
                scaled(sD, sV, ed).then_inc(vd_ready, 1)
                done(dve, "scan", 5 * i + 1)
                s = full(dve, "scan", 5 * i + 3)
                for d, t in enumerate(tiles):
                    o = oS[:, t, :] if t not in seen else sO[:, d * 512:(d + 1) * 512]
                    last = nc.vector.tensor_tensor(o, sO[:, d * 512:(d + 1) * 512], ps[:, s, d * 512:(d + 1) * 512],
                                                   ALU.add)
                    if d == 0:
                        again = [x for x in enumerate(tiles) if x[1] in seen or (x[0] == 1 and tiles[0] == tiles[1])]
                        seen.add(t)
                seen.add(tiles[1])
                last.then_inc(ps_free[s], 1)
                done(dve, "scan", 5 * i + 3)
                for d, t in again:
                    st.then(nc.vector.tensor_tensor(oS[:, t, :], oS[:, t, :], sO[:, d * 512:(d + 1) * 512], ALU.add))
                s = full(dve, "scan", 5 * i + 4)
                nc.vector.tensor_tensor(S, S, ps[:, s, :], ALU.add).then_inc(ps_free[s], 1)
                done(dve, "scan", 5 * i + 4)
            sq = tmp[:, 0:NT * 512]
            oF = oS.rearrange("p t c -> p (t c)")
            st.then(nc.vector.tensor_tensor(sq, oF, oF, ALU.mult))
            nc.vector.tensor_reduce(osd[:, :], sq.rearrange("p (i c) -> p i c", c=P), AX.X, ALU.add
                                    ).then_inc(os_ready, 1)
            dve.wait_ge(od_ready, 1)
            st.then(nc.vector.reciprocal(osd[:, :], osd[:, :]))
            nc.vector.tensor_tensor(oF.rearrange("p (i c) -> p i c", c=P), oF.rearrange("p (i c) -> p i c", c=P),
                                    spread(osd[:, :], 2, P), ALU.mult).then_inc(on_ready, 1)
            dve.wait_ge(state_out, 16)
            for t in range(NT):
                s = full(dve, "onrm", t)
                nc.vector.scalar_tensor_tensor(hT[:, 0:H, t * P:(t + 1) * P], per_head(ps[:, s, 0:512]),
                                               wsm[:, S_ONORM:S_ONORM + 1], zT[:, :, t * P:(t + 1) * P],
                                               ALU.mult, ALU.mult).then_inc(ps_free[s], 1)

        def act_onorm(act):
            act.wait_ge(os_ready, 1)
            nc.scalar.activation(osd[:, :], osd[:, :], ACT.Sqrt, bias=eps, scale=1.0 / P).then_inc(od_ready, 1)

        def pe_onorm():
            nc.tensor.wait_ge(on_ready, 1)
            for t in range(NT):
                s = take("onrm", t)
                for h in range(H):
                    last = nc.tensor.transpose(ps[:, s, h * P:(h + 1) * P], oS[:, t, h * P:(h + 1) * P], ident)
                last.then_inc(ps_full[s], 1)

        def pe_out(stage):
            with nc.tensor.Fori(0, 2) as turn:
                for j in range(4):
                    if j % 2 == 0:
                        w = block(stage, j // 2, turn)
                    pe_linear(stage, j, turn, cols(w, KD, 256, j % 2), from_h)

        def dve_residual(dve, stage, each, turns, gate):
            with dve.Fori(0, turns) as turn:
                for j in range(each):
                    s = full(dve, stage, j, turn)
                    c = turn * each + j
                    for a, b, at, grp in ((0, SEQ, 0, 0), (SEQ, HT, SEQ, 1), (HT, T, 512, 1)):
                        xs = xT[:, bass.ds(c * T + a, b - a)]
                        last = nc.vector.scalar_tensor_tensor(xs, ps[:, s, at:at + b - a],
                                                              modcol[:, bass.ds(c * 2 + (gate * 16 + grp), 1)], xs,
                                                              ALU.mult, ALU.add)
                    last.then_inc(ps_free[s], 1)

        def pe_ffn():
            nc.tensor.wait_ge(h_ready, 16)
            with nc.tensor.Fori(0, 2) as turn:
                for j in range(EC):
                    w = block("fgu", j, turn)
                    for u in range(2):
                        pe_linear("fgu", 2 * j + u, turn, cols(w, KD, 256, u), from_h)
            done(nc.tensor, "fgu", 2 * EC - 1, 1)
            with nc.tensor.Fori(0, 4) as turn:
                for j in range(2):
                    w = [block("fdn", 2 * j, turn), block("fdn", 2 * j + 1, turn)]
                    pe_linear("fdn", j, turn, [w[k // LK][:, (k % LK) * P:(k % LK + 1) * P] for k in range(FC)],
                              lambda k, a, b: actT[:, k, a:b])

        def act_gate(act, stage, j, turn):
            if j >= 2:
                done(act, stage, 2 * (j - 2) + 1, turn)
            else:
                done(act, stage, 2 * (EC - 1 - j) + 1, turn - 1)
            s = full(act, stage, 2 * j, turn)
            nc.scalar.activation(sg[:, j % 2, :].rearrange("p (b n) -> p b n", b=2), pair(s), ACT.Silu
                                 ).then_inc(ps_free[s], 1)

        def dve_up(dve, stage, j, turn, out):
            done(dve, stage, 2 * j, turn)
            s = full(dve, stage, 2 * j + 1, turn)
            nc.vector.tensor_tensor(out.rearrange("p (b n) -> p b n", b=2),
                                    sg[:, j % 2, :].rearrange("p (b n) -> p b n", b=2), pair(s), ALU.mult
                                    ).then_inc(ps_free[s], 1)

        def pe_odd_in():
            nc.tensor.wait_ge(h_ready, 24)
            for c in range(6):
                if c % 2 == 0:
                    w = block("oi", c // 2)
                pe_linear("oi", c, 0, cols(w, KD, 256, c % 2), from_h)
            pe_colnorm("mlan", mla_groups, 12)
            done(nc.tensor, "oi", 5)
            s = take("oi", 6)
            mm(ps[:, s, 0:DEC_SEQ], rot, krraw[:, SEQ:T], True, True).then_inc(ps_full[s], 1)

        def pe_odd_qkv():
            nc.tensor.wait_ge(cn_out, 13)

            def from_cq(k, a, b):
                return cq[:, k, a:b]

            for c in range(HC):
                if c % 4 == 0:
                    w = block("uqn", c // 4)
                pe_linear("uqn", c, 0, cols(w, 3, 512, c % 4), from_cq)
            w = block("uqr", 0)
            for j, (what, c) in enumerate(uq_order):
                if what == "P":
                    pe_linear("uqr", j, 0, cols(w, 3, 512, c), from_cq)
                else:
                    done(nc.tensor, "uqr", uq_order.index(("P", c)))
                    s = take("uqr", j)
                    mm(ps[:, s, 0:DEC_SEQ], rot, qraw[:, c % 2, SEQ:T], True, True).then_inc(ps_full[s], 1)
            nc.tensor.wait_ge(cn_out, 14)
            nc.tensor.wait_ge(mla_caches_in, 32)
            w = block("kn", 0)
            for c in range(HC):
                pe_linear("kn", c, 0, cols(w, 2, D, c), lambda k, a, b: ckv[:, k, a:b], TK // 2)
            w = block("vv", 0)
            for t in range(NT + 1):
                s = take("vv", t)
                for half in range(2):
                    for k in range(2):
                        last = mm(ps[:, s, half * 512:(half + 1) * 512], ckv[:, k, t * P:(t + 1) * P],
                                  w[:, k * D + half * 512:k * D + (half + 1) * 512], k == 0, k == 1)
                last.then_inc(ps_full[s], 1)

        def act_odd_in(act):
            for c in range(6):
                s = full(act, "oi", c)
                dst = cq[:, c, :] if c < 3 else ckv[:, c - 3, 0:T] if c < 5 else krraw
                nc.scalar.activation(dst.rearrange("p (b n) -> p b n", b=2), pair(s), ACT.Copy
                                     ).then_inc(ps_free[s], 1)
            done(act, "oi", 4)
            act_colnorm(act, "mlan", mla_groups, 12, [1 / 384, 1 / 256])

        def act_odd_qkv(act):
            scale = 192 ** -0.5
            act.wait_ge(cn_out, 14)
            for c in range(HC):
                s = full(act, "uqn", c)
                nc.scalar.activation(qn[:, c, :].rearrange("p (b n) -> p b n", b=2), pair(s), ACT.Copy, scale=scale
                                     ).then_inc(ps_free[s], 1)
            for c in range(4):
                if c >= 2:
                    done(act, "uqr", uq_order.index(("R", c - 2)))
                s = full(act, "uqr", uq_order.index(("P", c)))
                nc.scalar.activation(qraw[:, c % 2, :].rearrange("p (b n) -> p b n", b=2), pair(s), ACT.Copy,
                                     scale=scale).then_inc(ps_free[s], 1)
            for c in range(HC):
                s = full(act, "kn", c)
                nc.scalar.activation(kn[:, c, :].rearrange("p (b n) -> p b n", b=2), pair(s, TK // 2), ACT.Copy
                                     ).then_inc(ps_free[s], 1)

        def dve_odd(dve, st):
            dve_colnorm(dve, st, "mlan", mla_groups)
            s = full(dve, "oi", 6)
            dve_rope(st, krraw, krT[:, 0:T], s)
            for c in range(4):
                s = full(dve, "uqr", uq_order.index(("R", c)))
                if c == 0:
                    done(dve, "oi", 6)
                else:
                    done(dve, "uqr", uq_order.index(("R", c - 1)))
                dve_rope(st, qraw[:, c % 2, :], qr[:, c, :], s)
            for t in range(NT + 1):
                s = full(dve, "vv", t)
                nc.vector.tensor_copy(vC[:, t, :], ps[:, s, :]).then_inc(ps_free[s], 1)

        rt = gates_sb[:, 0:NT * NE].rearrange("p (t e) -> p t e", e=NE)
        top = tmp[:, 2 * T:2 * T + NT * 8].rearrange("p (t e) -> p t e", e=8)
        topi = tmp[:, 2 * T + 64:2 * T + 64 + NT * 8].bitcast(U32).rearrange("p (t e) -> p t e", e=8)
        topf = tmp[:, 2 * T + 128:2 * T + 128 + NT * 8].rearrange("p (t e) -> p t e", e=8)
        tw = tmp[:, 2 * T + 192:2 * T + 192 + 3 * NT].rearrange("p (i t) -> p i t", i=3)
        oh = tmp[:, 2 * T + 256:2 * T + 256 + NT * NE].rearrange("p (t e) -> p t e", e=NE)

        def pe_router():
            nc.tensor.wait_ge(h_ready, 32)
            w, s = block("rt", 0), take("rt", 0)
            for t in range(NT):
                for k in range(KD):
                    last = mm(ps[:, s, t * NE:(t + 1) * NE], hT[:, k, t * P:(t + 1) * P], w[:, k * NE:(k + 1) * NE],
                              k == 0, k == KD - 1)
            last.then_inc(ps_full[s], 1)

        def dve_router(dve, st):
            nc.vector.memset(yacc, 0.0).then_inc(yacc_zero, 1)
            s = full(dve, "rt", 0)
            nc.vector.tensor_copy(gates_sb[:, 0:NT * NE], ps[:, s, 0:NT * NE]).then_inc(ps_free[s], 1)
            done(dve, "rt", 0)
            for t in range(NT):
                last = nc.vector.max(top[:, t, :], rt[:, t, :])
            st.then(last)
            for t in range(NT):
                st.then(nc.vector.max_index(topi[:, t, :], top[:, t, :], rt[:, t, :]))
            nc.vector.tensor_copy(topf, topi)
            nc.vector.tensor_tensor(tw[:, 0, :], top[:, :, 1], top[:, :, 0], ALU.subtract).then_inc(top_ready, 1)
            dve.wait_ge(top_exp, 1)
            st.then(nc.vector.tensor_scalar(tw[:, 1, :], tw[:, 0, :], 1.0, None, ALU.add))
            st.then(nc.vector.reciprocal(tw[:, 1, :], tw[:, 1, :]))
            st.then(nc.vector.tensor_tensor(tw[:, 2, :], tw[:, 0, :], tw[:, 1, :], ALU.mult))
            for t in range(NT):
                nc.vector.tensor_scalar(rt[:, t, :], iota8, topf[:, t, 0:1], tw[:, 1, t:t + 1], ALU.is_equal, ALU.mult)
                last = nc.vector.tensor_scalar(oh[:, t, :], iota8, topf[:, t, 1:2], tw[:, 2, t:t + 1],
                                               ALU.is_equal, ALU.mult)
            st.then(last)
            st.then(nc.vector.tensor_tensor(rt, rt, oh, ALU.add))

        def pe_moe():
            with nc.tensor.Fori(0, NE) as e:
                for j in range(EC):
                    w = block("moe", j, e)
                    for u in range(2):
                        pe_linear("moe", 2 * j + u, e, cols(w, KD, 256, u), from_h)
                done(nc.tensor, "moe", 2 * EC - 1, e)
                for half in range(2):
                    w = [block("moe", EC + 3 * half + i, e) for i in range(3)]
                    for q, tiles in enumerate(((0, 1), (2, 3), (4,))):
                        j = 2 * EC + 3 * half + q
                        s = take("moe", j, e)
                        for n, t in enumerate(tiles):
                            for k in range(EC):
                                last = mm(ps[:, s, n * 512:(n + 1) * 512], actT[:, k, t * P:(t + 1) * P],
                                          w[k // 4][:, (k % 4) * 512:(k % 4 + 1) * 512], k == 0, k == EC - 1)
                        last.then_inc(ps_full[s], 1)

        def dve_moe(dve):
            dve.wait_ge(yacc_zero, 1)
            with dve.Fori(0, NE) as e:
                for j in range(EC):
                    dve_up(dve, "moe", j, e, actT[:, j, :])
                for half in range(2):
                    for q, tiles in enumerate(((0, 1), (2, 3), (4,))):
                        s = full(dve, "moe", 2 * EC + 3 * half + q, e)
                        for n, t in enumerate(tiles):
                            y = yacc[:, t, half * 512:(half + 1) * 512]
                            last = nc.vector.scalar_tensor_tensor(
                                y, ps[:, s, n * 512:(n + 1) * 512], gates_sb[:, bass.ds(e + t * NE, 1)], y,
                                ALU.mult, ALU.add)
                        last.then_inc(ps_free[s], 1)

        def pe_moe_out():
            done(nc.tensor, "moe", 2 * EC + 5, NE - 1)
            for c in range(KD):
                s = take("yt", c)
                for t in range(NT):
                    last = nc.tensor.transpose(ps[:, s, t * P:(t + 1) * P], yacc[:, t, c * P:(c + 1) * P], ident)
                last.then_inc(ps_full[s], 1)

        def dve_moe_out(dve):
            for c in range(KD):
                s = full(dve, "yt", c)
                for a, b, grp in SEGS:
                    last = nc.vector.scalar_tensor_tensor(xc[:, c, a:b], ps[:, s, a:b],
                                                          modcol[:, 11 * 16 + 2 * c + grp:11 * 16 + 2 * c + grp + 1],
                                                          xc[:, c, a:b], ALU.mult, ALU.add)
                last.then_inc(ps_free[s], 1)

        block_ = ctx.enter_context(nc.Block())

        @block_.sync
        def _(sync):
            sync.dma_start(wsm[:, :], I["wsm"]).then_inc(consts_in, 16)
            sync.dma_start(cst[:, :], I["cst"]).then_inc(consts_in, 16)
            sync.dma_start(lam_in[:, :], I["lam"]).then_inc(consts_in, 16)
            sync.dma_start(cossin[:, :, :], I["cossin"]).then_inc(consts_in, 16)
            for stage in loads:
                load_stage(sync, stage)
                if stage == "mod":
                    sync.dma_start(xT[:, :], I["x"]).then_inc(x_in, 16)
            sync.wait_ge(hs_ready, 8 * 5)
            sync.dma_start(O["y"], hT[:, :, :].rearrange("p k t -> p (k t)")).then_inc(y_out, 16)
            sync.wait_ge(y_out, 16)

        @block_.gpsimd
        def _(pool):
            pool.dma_start(kT[:, :, T:TK], I["ck"]).then_inc(caches_in, 16)
            pool.dma_start(vB[:, NT, :], I["cv"]).then_inc(caches_in, 16)
            done(pool, "qk", 15)
            pool.dma_start(O["dk"], kT[:, :, 0:SEQ]).then_inc(kv_out, 16)
            done(pool, "vb", 0)
            pool.dma_start(O["dv"], vB[:, 0, :]).then_inc(kv_out, 16)
            full(pool, "vb", NT - 1)
            pool.dma_start(Sst[1], I["state"]).then_inc(state_in, 16)
            pool_delta(pool)
            done(pool, "scan", 4)
            pool.dma_start(O["state"], Sst[0]).then_inc(state_out, 16)
            full(pool, "fdn", 1, 3)
            pool.dma_start(ckv[:, :, T:TK], I["cckv"]).then_inc(mla_caches_in, 16)
            pool.dma_start(krT[:, T:TK], I["ckr"]).then_inc(mla_caches_in, 16)
            done(pool, "oi", 6)
            pool.dma_start(O["kr"], krT[0:ROPE, 0:SEQ]).then_inc(mla_out, 16)
            pool.wait_ge(cn_out, 14)
            pool.dma_start(O["ckv"], ckv[:, :, 0:SEQ]).then_inc(mla_out, 16)
            pool.wait_ge(kv_out, 32)
            pool.wait_ge(state_out, 16)
            pool.wait_ge(mla_out, 32)

        @block_.scalar
        def _(act):
            act.wait_ge(consts_in, 16 * 4)
            nc.scalar.activation(csilu[:, :], wsm[:, S_C:S_C + 16], ACT.Silu).then_inc(csilu_ready, 1)
            for i in range(2):
                s = full(act, "lam", i)
                nc.scalar.activation(lam_e[:, i:i + 1], ps[:, s, 0:1], ACT.Exp).then_inc(ps_free[s], 1)
            act_norm(act, 0, lambda a: (a.wait_ge(x_in, 16), full(a, "mod", 1, 11)))
            act_even_in(act)
            act.wait_ge(qkv_ready, 12)
            act_colnorm(act, "l2", l2_groups, 0, [1.0] * 8)
            att0[2](act)
            done(act, "att0", len(plan_b) - 1)
            act.wait_ge(cn_out, 8)
            act_colnorm(act, "obn", obn_groups, 8, [1 / P] * H)
            act_delta(act)
            act_onorm(act)
            act_norm(act, 1, lambda a: done(a, "eo", 3, 1))
            with act.Fori(0, 2) as turn:
                for j in range(EC):
                    act_gate(act, "fgu", j, turn)
            act_norm(act, 2, lambda a: done(a, "fdn", 1, 3))
            act_odd_in(act)
            act_odd_qkv(act)
            att1[2](act)
            act_norm(act, 3, lambda a: done(a, "oo", 3, 1))
            act.wait_ge(top_ready, 1)
            nc.scalar.activation(tw[:, 0, :], tw[:, 0, :], ACT.Exp).then_inc(top_exp, 1)
            with act.Fori(0, NE) as e:
                for j in range(EC):
                    act_gate(act, "moe", j, e)
            act_norm(act, 4, lambda a: done(a, "yt", KD - 1))

        @block_.vector
        def _(dve):
            st = Steps(dve, dve_step)
            dve.wait_ge(consts_in, 16 * 4)
            for i in range(2):
                last = nc.vector.tensor_tensor(lam_pr[:, i:i + 1], lam_in[:, 2 * i:2 * i + 1],
                                               lam_in[:, 2 * i + 1:2 * i + 2], ALU.mult)
            last.then_inc(lam_ready, 1)
            for col in (0, 1 + SEQ, 2 + T):
                last = nc.vector.memset(raw[:, col:col + 1], 0.0)
            st.then(last)
            done(dve, "lam", 0)
            done(dve, "lam", 1)
            st.then(nc.vector.tensor_tensor(neglam[:, :], lam_e[:, 1:2], lam_e[:, 0:1], ALU.subtract))
            st.then(nc.vector.tensor_scalar(neglam[:, :], neglam[:, :], -LAM_INIT, None, ALU.add))
            st.then(nc.vector.tensor_scalar(wsm[:, S_SUBLN:S_SUBLN + 1], wsm[:, S_SUBLN:S_SUBLN + 1],
                                            1.0 - LAM_INIT, None, ALU.mult))
            dve_mod(dve)
            dve_norm(dve, st, 0)
            dve_even_in(dve, st)
            dve_colnorm(dve, st, "l2", l2_groups)
            dve.wait_ge(caches_in, 32)
            att0[1](dve, st)
            dve_colnorm(dve, st, "obn", obn_groups)
            nc.vector.memset(Sst[0], 0.0).then_inc(s_zero, 1)
            dve_delta(dve, st)
            dve_scan(dve, st)
            dve_residual(dve, "eo", 4, 2, 2)
            dve_norm(dve, st, 1)
            with dve.Fori(0, 2) as turn:
                for j in range(EC):
                    dve_up(dve, "fgu", j, turn, arena[:, bass.ds((turn * EC + j) * T, T)])
            dve_residual(dve, "fdn", 2, 4, 5)
            dve_norm(dve, st, 2)
            dve_odd(dve, st)
            att1[1](dve, st)
            dve_residual(dve, "oo", 4, 2, 8)
            dve_norm(dve, st, 3)
            dve_router(dve, st)
            dve_moe(dve)
            dve_moe_out(dve)
            dve_norm(dve, st, 4)

        @block_.tensor
        def _(pe):
            pe_lam()
            pe_mod()
            pe_norm(0)
            pe_even_in()
            pe_colnorm("l2", l2_groups, 0)
            pe.wait_ge(caches_in, 32)
            att0[0]()
            pe_colnorm("obn", obn_groups, 8)
            pe_delta()
            pe_scan()
            pe_onorm()
            done(pe, "onrm", NT - 1)
            pe.wait_ge(cn_out, 12)
            pe_out("eo")
            pe_norm(1)
            pe_ffn()
            pe_norm(2)
            pe_odd_in()
            pe_odd_qkv()
            done(pe, "vv", NT)
            done(pe, "uqr", 7)
            att1[0]()
            done(pe, "att1", len(plan_c) - 1)
            pe_out("oo")
            pe_norm(3)
            pe_router()
            pe_moe()
            pe_moe_out()
            pe_norm(4)


def kernel(**inputs):
    import numpy as _np
    import concourse.bacc as _bacc
    from concourse.bass_utils import run_bass_kernel_spmd as _run

    v = {k: _np.asarray(a) for k, a in inputs.items()}

    def cut(w, ncols):
        k, n = w.shape
        return w.reshape(k // P, P, n // ncols, ncols).transpose(2, 1, 0, 3).reshape(n // ncols, P, -1)

    def col(w):
        return w.reshape(-1, P).T

    def rows(w):
        return _np.broadcast_to(w.reshape(1, -1), (P, w.size))

    def gate_up(w, nf):
        return w.reshape(KD, P, 2, nf, P).transpose(3, 1, 0, 2, 4).reshape(nf, P, KD * 256)

    i = _np.arange(P)
    ident = _np.eye(P)
    before = (i[:, None] <= i[None, :]).astype(_np.float64)
    masks = [before, before.T]
    levels = []
    for lv in range(LEVELS):
        w = 2 ** lv
        same = (i[:, None] // (2 * w)) == (i[None, :] // (2 * w))
        fwd = same & (i[None, :] % (2 * w) >= w) & (i[:, None] % (2 * w) < w)
        levels += [fwd, fwd.T]
    rot = _np.zeros((P, P))
    for b in range(0, P, 32):
        for j in range(16):
            rot[b + 16 + j, b + j] = -1.0
            rot[b + j, b + 16 + j] = 1.0
    table = _np.concatenate(
        [ident, _np.ones((P, P)), *masks, *[_np.where(m > 0, 0.0, NEG) for m in masks], *levels, rot,
         _np.broadcast_to(_np.arange(8.0), (P, 8)), _np.full((P, 1), EPS)], axis=1).astype(_np.float32)
    half = ROPE // 2
    inv = (_np.float32(10000.0) ** (-_np.arange(0, half, 2, dtype=_np.float32) / _np.float32(half))).astype(_np.float32)
    tokens = _np.arange(DEC_SEQ)
    ar = (tokens // 64).astype(_np.float32)[:, None] * inv[None, :]
    ac = (tokens % 64).astype(_np.float32)[:, None] * inv[None, :]
    ang = _np.concatenate([ar, ar, ac, ac, ar, ar, ac, ac], axis=1).astype(_np.float32).T
    cossin = _np.stack([_np.cos(ang), _np.sin(ang)], axis=1).astype(_np.float32)

    w_in = v["ev_w_in"][0]
    main = _np.concatenate([w_in[:, 0:2048], w_in[:, 2064:3600]], axis=1)
    od_in = _np.concatenate([v["od_w_in"][0], v["od_w_in"][0][:, 640:704]], axis=1)
    uq = v["od_w_uq"][0].reshape(384, HC, 192)
    ukv = v["od_w_ukv"][0].reshape(256, HC, 256)
    arrays = {
        "wsm": _np.concatenate(
            [col(w) for w in (v["norm_mix"][0], v["norm_ffn"][0], v["norm_mix"][1], v["norm_ffn"][1],
                              v["final_norm"], v["mod_b"])]
            + [v["ev_conv_w"][0].reshape(3, 12, P).transpose(2, 1, 0).reshape(P, 36),
               col(v["ev_onorm"][0]), col(v["ev_subln"][0]), col(v["od_q_norm"][0]), col(v["od_kv_norm"][0]),
               rows(v["ev_dt_bias"][0]), rows(v["ev_a_log"][0]),
               _np.stack([col(v["c_ctx"]), col(v["c"][0])], axis=2).reshape(P, 16)], axis=1),
        "cst": table,
        "lam": v["ev_lambda"][0].T,
        "cossin": cossin,
        "x": _np.concatenate([v["x_prompt"][0], v["x_sample"][0]], axis=0).T.reshape(KD, P, T)
             .transpose(1, 0, 2).reshape(P, KD * T),
        "ck": v["cache_diff_k"][0, 0].transpose(2, 0, 1),
        "cv": v["cache_diff_v"][0, 0].transpose(1, 0, 2).reshape(P, 512),
        "cckv": v["cache_mla_ckv"][0, 0].T.reshape(2, P, PAST).transpose(1, 0, 2),
        "ckr": _np.concatenate([v["cache_mla_krope"][0, 0].T] * 2, axis=0),
        "state": v["state_delta"][0, 0].transpose(2, 0, 1, 3).reshape(P, 1024),
        "w_mod": v["mod_w"].reshape(2, 4, 2, P, 6, D).transpose(0, 4, 1, 3, 2, 5).reshape(48, P, WB),
        "w_ev": cut(main, 256),
        "w_evg": cut(w_in[:, 2048:2064], 16),
        "w_eo": cut(v["ev_w_out"][0], 256),
        "w_gu": gate_up(v["ffn_w_gu"][0], FC),
        "w_dn": v["ffn_w_down"][0].reshape(2, LK, P, KD, P).transpose(3, 0, 2, 1, 4).reshape(16, P, LK * P),
        "w_oi": cut(od_in, 256),
        "w_uq": _np.concatenate([cut(uq[:, :, 0:128].reshape(384, 1024), 512),
                                 cut(uq[:, :, 128:192].reshape(384, 512), 512)], axis=0),
        "w_ukv": _np.stack([cut(ukv[:, :, 0:128].reshape(256, D), D)[0], cut(ukv[:, :, 128:].reshape(256, D), D)[0]]),
        "w_oo": cut(v["od_w_out"][0], 256),
        "w_rt": cut(v["moe_router"][0], NE),
        "w_mgu": _np.concatenate([gate_up(v["moe_w_gu"][0, e], EC) for e in range(NE)], axis=0),
        "w_mdn": v["moe_w_down"][0].reshape(NE, EC, P, 2, 512).transpose(0, 3, 2, 1, 4).reshape(2 * NE, P, EC * 512),
    }
    outs = {"y": (P, KD * T), "state": (P, 1024), "dk": (P, H, SEQ), "dv": (SEQ, 512),
            "ckv": (P, 2, SEQ), "kr": (ROPE, SEQ)}
    nc = _bacc.Bacc("TRN2", target_bir_lowering=False, num_devices=1, dynamic_dma_scratch_size=2048)
    arrays = {f"in_{n}": _np.ascontiguousarray(a) for n, a in arrays.items()}
    I = {n[3:]: nc.dram_tensor(n, a.shape, F32, kind="ExternalInput").ap() for n, a in arrays.items()}
    O = {n: nc.dram_tensor(f"out_{n}", s, F32, kind="ExternalOutput").ap() for n, s in outs.items()}
    program(nc, I, O)
    r = _run(nc, [arrays], core_ids=[0]).results[0]
    y = r["out_y"].reshape(P, KD, T).transpose(2, 1, 0).reshape(T, D)
    return (
        y[0:SEQ].reshape(1, SEQ, D), y[SEQ:T].reshape(1, DEC_SEQ, D),
        r["out_state"].reshape(P, 2, H, P).transpose(1, 2, 0, 3).reshape(1, 1, 2, H, P, P),
        r["out_dk"].transpose(1, 2, 0).reshape(1, 1, H, SEQ, P),
        r["out_dv"].reshape(SEQ, H, P).transpose(1, 0, 2).reshape(1, 1, H, SEQ, P),
        r["out_ckv"].transpose(2, 1, 0).reshape(1, 1, SEQ, 256),
        r["out_kr"].T.reshape(1, 1, SEQ, ROPE),
    )
```

```python
from contextlib import ExitStack

import numpy as np
import concourse.bass as bass
from concourse import mybir

ALU = mybir.AluOpType
ACT = mybir.ActivationFunctionType
AX = mybir.AxisListType
F32 = mybir.dt.float32
U32 = mybir.dt.uint32
I32 = mybir.dt.int32
F32R = mybir.dt.float32r

P = 128
D = 1024
KD = D // P
SEQ, DEC_SEQ, PAST = 128, 512, 128
T = SEQ + DEC_SEQ
NT = T // P
HT = T // 2
TK = T + PAST
SEGS = ((0, SEQ, 0), (SEQ, T, 1))
H = 4
HC = 8
ROPE = 64
FC = 2816 // P
NE = 8
EC = 1408 // P
WS = 5
WB = 2048
LEVELS = 7
NEG = -30000.0
EPS = 1e-6
LAM_INIT = 0.8 - 0.6
ITEMS = (2 * T + NE * (P - 1)) // P
LK = 11

C_ID, C_ONE, C_TRI, C_NEG, C_LVL, C_ROT = 0, 128, 256, 512, 768, 768 + LEVELS * 256
C_IOTA = C_ROT + 128
C_EPS = C_IOTA + P
C_COLS = C_EPS + 1
S_NORM, S_MODB, S_CONV = 0, 40, 136
S_ONORM, S_SUBLN, S_QN, S_KVN, S_DTB, S_ALOG, S_C = 172, 173, 174, 177, 179, 187, 195
S_COLS = S_C + 16


class Ring:

    def __init__(self, slots):
        self.slots, self.used, self.stages = slots, [0] * slots, {}

    def plan(self, stage, each, turns=1):
        per = [(each - s + self.slots - 1) // self.slots for s in range(self.slots)]
        self.stages[stage] = (list(self.used), per, each, turns)
        self.used = [u + turns * p for u, p in zip(self.used, per)]

    def use(self, stage, j, turn=0):
        before, per, _, _ = self.stages[stage]
        s = j % self.slots
        return s, turn * per[s] + before[s] + j // self.slots


class Steps:

    def __init__(self, eng, sem):
        self.eng, self.sem, self.n, self.off = eng, sem, 0, 0

    def did(self, ins):
        ins.then_inc(self.sem, 1)
        self.n += 1

    def sync(self):
        self.eng.wait_ge(self.sem, self.n + self.off)

    def then(self, ins):
        self.did(ins)
        self.sync()

    def loop(self, turn, each):
        self.start, self.off = self.n, turn * each

    def end(self, each, turns):
        assert self.n - self.start == each, (self.n - self.start, each)
        self.n, self.off = self.start + each * turns, 0


def spread(ap, axis, n):
    v = ap.unsqueeze(axis)
    shape = list(v.shape)
    shape[axis] = n
    return v.broadcast_to(shape)


def attention_items(heads):
    return [(h, t) for h in range(heads) for t in range(NT)]


def attention_plan(heads, streams):
    items = attention_items(heads)
    plan = []
    for i in range(len(items) + 2):
        if i < len(items):
            plan += [("scores", i, s) for s in range(streams)]
        if 1 <= i <= len(items):
            plan.append(("turn", i - 1, 0))
        if i >= 2:
            plan.append(("values", i - 2, 0))
    return plan


def program(nc, I, O):
    with ExitStack() as ctx:
        def sb(name, shape, dt=F32):
            return ctx.enter_context(nc.sbuf_tensor(name, shape, dt))

        def sem(name):
            return ctx.enter_context(nc.semaphore(name))

        wring = sb("wring", [P, WS, WB])
        xT = sb("xT", [P, KD * T])
        hT = sb("hT", [P, KD, T])
        tmp = sb("tmp", [P, KD * T])
        with ExitStack() as mixers:
            arena = mixers.enter_context(nc.sbuf_tensor("arena", [P, 25600], F32))
        expf = sb("expf", [P, 8576])
        expr = sb("expr", [P, 25600 - 8576], F32R)
        cst = sb("cst", [P, C_COLS])
        cossin = sb("cossin", [P, 2, DEC_SEQ])
        wsm = sb("wsm", [P, S_COLS])
        lam_in = sb("lam_in", [64, 4])
        lam_pr = sb("lam_pr", [64, 2])
        lam_e = sb("lam_e", [P, 2])
        neglam = sb("neglam", [P, 1])
        csilu = sb("csilu", [P, KD * 2])
        modcol = sb("modcol", [P, 12 * 16])
        modA = sb("modA", [P, 4, KD, 2])
        std = sb("std", [P, T])
        gates_sb = sb("gates_sb", [P, 5 * 16])
        dsm = sb("dsm", [P, 7, 2, NT, H])
        att = sb("att", [P, 16])
        osd = sb("osd", [P, NT * H])
        item_expert = sb("item_expert", [1, ITEMS + 1], I32)
        slot_of = sb("slot_of", [P, 2, NT])
        tokw = sb("tokw", [P, 2, NT])
        inw = sb("inw", [P, 3, NT])

        ps = ctx.enter_context(nc.psum_tensor("ps", [P, 4, 1024], F32))

        def pair(slot, n=HT):
            return ps[:, slot, :].rearrange("p (b n) -> p b n", b=2)[:, :, 0:n]

        ident, ones = cst[:, C_ID:C_ID + P], cst[:, C_ONE:C_ONE + P]
        tri = [cst[:, C_TRI + d * P:C_TRI + (d + 1) * P] for d in range(2)]
        rot = cst[:, C_ROT:C_ROT + P]
        iota = cst[:, C_IOTA:C_IOTA + P]
        eps = cst[:, C_EPS:C_EPS + 1]
        cos, sin = cossin[:, 0, :], cossin[:, 1, :]

        def chunks(base, n, width):
            return arena[:, base:base + n * width].rearrange("p (n w) -> p n w", n=n)

        xc = xT[:, :].rearrange("p (k t) -> p k t", k=KD)
        tc = tmp[:, :].rearrange("p (k t) -> p k t", k=KD)
        qkvT, zT = chunks(0, 12, T), chunks(7680, 4, T)
        qT, kT, vB = chunks(10240, H, T), chunks(12800, H, TK), chunks(15872, NT + 1, 512)
        pB, aB = chunks(18944, 4, T), chunks(21504, 2, T)
        qkraw, raw, cv = chunks(22784, 2, T), arena[:, 24064:24064 + 643], arena[:, 24708:24708 + 641]
        rtmp = std[:, 0:DEC_SEQ]
        tok = chunks(10240, NT, 1024)
        DTs, Ais = chunks(15360, NT, 1024), chunks(20480, NT, 1024)
        oS = chunks(5120, NT, 512)
        dE, dM, dC, dD, dT1 = (tmp[:, i * 1024:(i + 1) * 1024] for i in range(5))
        Sst = [hT[:, :, :].rearrange("p k t -> p (k t)")[:, i * 1024:(i + 1) * 1024] for i in range(2)]
        actT = chunks(0, FC, T)
        yacc = expf[:, 0:NT * D].rearrange("p (t n) -> p t n", t=NT)
        xs, xe = expf[:, 5120:6144], expf[:, 6144:7168]
        actE = expf[:, 7168:8576].rearrange("p (k s) -> p k s", k=EC)
        hhi, hlo = (expr[:, i * 5120:(i + 1) * 5120].rearrange("p (t n) -> p t n", t=NT) for i in range(2))
        sel = expr[:, 10240:10880].rearrange("p (t s) -> p t s", t=NT)
        selT = expr[:, 10880:11520]
        yhi, ylo = expr[:, 11520:12544], expr[:, 12544:13568]
        sg = tmp[:, 0:2 * T].rearrange("p (b t) -> p b t", b=2)
        qn, qr, kn, vC = chunks(0, HC, T), chunks(5120, 4, T), chunks(7680, HC, TK), chunks(13824, NT + 1, 1024)
        krT, ckv, cq = arena[:, 19968:19968 + TK], chunks(20736, 2, TK), chunks(22272, 3, T)
        krraw = arena[:, 24192:24192 + T]
        pC = tmp[:, 0:2 * T].rearrange("p (b t) -> p b t", b=2)
        aC = tmp[:, 2 * T:4 * T].rearrange("p (b t) -> p b t", b=2)
        qraw = tmp[:, 4 * T:6 * T].rearrange("p (b t) -> p b t", b=2)

        g_, beta, gcum, glast, eg, ed, el = (dsm[:, i, :, :, :] for i in range(7))

        w_full = [sem(f"w_full{s}") for s in range(WS)]
        ps_full = [sem(f"ps_full{s}") for s in range(4)]
        ps_free = [sem(f"ps_free{s}") for s in range(4)]
        act_step, dve_step, pool_step = sem("act_step"), sem("dve_step"), sem("pool_step")
        consts_in, x_in, caches_in, mla_caches_in, state_in = (
            sem(n) for n in ("consts_in", "x_in", "caches_in", "mla_caches_in", "state_in"))
        csilu_ready, lam_ready, lam_exp, modA_ready = (
            sem(n) for n in ("csilu_ready", "lam_ready", "lam_exp", "modA_ready"))
        sq_ready, std_ready, hs_ready, h_ready = (sem(n) for n in ("sq_ready", "std_ready", "hs_ready", "h_ready"))
        conv_ready, qkv_ready, cn_sq, cn_out = (sem(n) for n in ("conv_ready", "qkv_ready", "cn_sq", "cn_out"))
        gate_in, gate_e, gate_l, g_ready = (sem(n) for n in ("gate_in", "gate_e", "gate_l", "g_ready"))
        decay_in, decay_out = sem("decay_in"), sem("decay_out")
        mx_ready, a_ready = sem("mx_ready"), sem("a_ready")
        gb_ready, e_in, e_out, c_ready, dt_ready = (
            sem(n) for n in ("gb_ready", "e_in", "e_out", "c_ready", "dt_ready"))
        s_zero, r_ready, vd_ready = sem("s_zero"), sem("r_ready"), sem("vd_ready")
        os_ready, od_ready, on_ready = sem("os_ready"), sem("od_ready"), sem("on_ready")
        top_ready, top_exp, exp_zero = sem("top_ready"), sem("top_exp"), sem("exp_zero")
        hhi_ready, oh_ready, items_ready, sel_ready, yhi_ready, silu_ready = (
            sem(n) for n in ("hhi_ready", "oh_ready", "items_ready", "sel_ready", "yhi_ready", "silu_ready"))
        kv_out, state_out, mla_out, y_out = (sem(n) for n in ("kv_out", "state_out", "mla_out", "y_out"))

        R = Ring(4)
        plan_b, plan_c = attention_plan(H, 2), attention_plan(HC, 1)
        rope_order = [("P", 0)] + [x for c in range(1, 8) for x in (("P", c), ("R", c - 1))] + [("R", 7)]
        uq_order = [("P", 0)] + [x for c in range(1, 4) for x in (("P", c), ("R", c - 1))] + [("R", 3)]
        DL = 4 + 3 * (LEVELS - 1) - 1
        SCAN = [(0, 0), (1, 4), (2, 3), (3, 2), (4, 1)]
        ITEM = (["gu0", "gu1"] + [f"sc{t}" for t in range(NT)] + ["turnP"] + [f"gu{j}" for j in range(2, EC)]
                + ["gather", "dn0", "turnX", "dn1"])
        for stage, each, turns in (
                ("lam", 2, 1), ("mod", 2, 12), ("norm0", 1, 1), ("qkv", 12, 1), ("z", 4, 1), ("gat", 1, 1),
                ("qk", 16, 1), ("vb", NT, 1), ("l2", 8, 1), ("att0", len(plan_b), 1), ("obn", H, 1),
                ("cum", 1, 1), ("tri", DL * NT, 1), ("scan", 5 * NT, 1), ("onrm", NT, 1), ("eo", 4, 2),
                ("norm1", 1, 1), ("fgu", 2 * EC, 2), ("fdn", 2, 4),
                ("norm2", 1, 1), ("oi", 7, 1), ("mlan", 2, 1), ("uqn", HC, 1), ("uqr", 8, 1), ("kn", HC, 1),
                ("vv", NT + 1, 1), ("att1", len(plan_c), 1), ("oo", 4, 2),
                ("norm3", 1, 1), ("rt", 1, 1), ("ht", NT, 1), ("cnt", 1, 1), ("moe0", 2, 1),
                ("moe", len(ITEM), ITEMS), ("moe1", NT, 1), ("yt", KD, 1), ("norm4", 1, 1)):
            R.plan(stage, each, turns)

        def take(stage, j, turn=0):
            s, n = R.use(stage, j, turn)
            if not (isinstance(n, int) and n == 0):
                nc.tensor.wait_ge(ps_free[s], n)
            return s

        def full(eng, stage, j, turn=0):
            s, n = R.use(stage, j, turn)
            eng.wait_ge(ps_full[s], n + 1)
            return s

        def done(eng, stage, j, turn=0):
            s, n = R.use(stage, j, turn)
            eng.wait_ge(ps_free[s], n + 1)

        W = Ring(WS)
        loads = {
            "mod": (I["w_mod"], WB, 4, 12, lambda j: ("mod", 0)),
            "qkv": (I["w_ev"][0:6], WB, 6, 1, lambda j: ("qkv", 2 * j + 1)),
            "z": (I["w_ev"][6:8], WB, 2, 1, lambda j: ("z", 2 * j + 1)),
            "gat": (I["w_evg"], KD * 16, 1, 1, lambda j: ("gat", 0)),
            "qk": (I["w_ev"][8:12], WB, 4, 1, lambda j: ("qk", rope_order.index(("P", 2 * j + 1)))),
            "vb": (I["w_ev"][12:14], WB, 2, 1, lambda j: ("vb", NT - 1)),
            "eo": (I["w_eo"], WB, 2, 2, lambda j: ("eo", 2 * j + 1)),
            "fgu": (I["w_gu"], WB, EC, 2, lambda j: ("fgu", 2 * j + 1)),
            "fdn": (I["w_dn"], LK * P, 4, 4, lambda j: ("fdn", j // 2)),
            "oi": (I["w_oi"], WB, 3, 1, lambda j: ("oi", 2 * j + 1)),
            "uqn": (I["w_uq"][0:2], 1536, 2, 1, lambda j: ("uqn", 4 * j + 3)),
            "uqr": (I["w_uq"][2:3], 1536, 1, 1, lambda j: ("uqr", uq_order.index(("P", 3)))),
            "kn": (I["w_ukv"][0:1], WB, 1, 1, lambda j: ("kn", HC - 1)),
            "vv": (I["w_ukv"][1:2], WB, 1, 1, lambda j: ("vv", NT)),
            "oo": (I["w_oo"], WB, 2, 2, lambda j: ("oo", 2 * j + 1)),
            "rt": (I["w_rt"], 64, 1, 1, lambda j: ("rt", 0)),
            "moe": (None, WB, EC + 6, ITEMS, lambda j: ("moe", ITEM.index(f"gu{j}" if j < EC else f"dn{(j - EC) // 3}"))),
        }
        history = [[] for _ in range(WS)]
        for stage, (_, _, each, turns, _) in loads.items():
            W.plan(stage, each, turns)
            for turn in range(turns):
                for j in range(each):
                    history[j % WS].append((stage, j, turn))

        def block(stage, j, turn=0):
            s, n = W.use(stage, j, turn)
            nc.tensor.wait_ge(w_full[s], 16 * (n + 1))
            return wring[:, s, :]

        def load(sync, stage, j, turn=0, expert=0):
            dram, size, each, _, _ = loads[stage]
            s, n = W.use(stage, j, turn)
            if isinstance(turn, int):
                held = history[s][n - 1] if n else None
            elif j >= WS:
                held = (stage, j - WS, turn)
            else:
                held = (stage, max(i for i in range(each) if i % WS == s), turn - 1)
            if held:
                pstage, pj = loads[held[0]][4](held[1])
                full(sync, pstage, pj, held[2])
            if stage == "moe":
                if j < EC:
                    src = I["w_mgu"][bass.ds(expert * EC + j, 1), :, :]
                else:
                    half, part = (j - EC) // 3, (j - EC) % 3
                    size = 4 * 512 if part < 2 else 3 * 512
                    src = I["w_mdn"][bass.ds(expert * 2 + half, 1), :, part * WB:part * WB + size]
            else:
                src = dram[bass.ds(turn * each + j, 1), :, 0:size]
            sync.dma_start(wring[:, s, 0:size], src.rearrange("a p n -> p (a n)")).then_inc(w_full[s], 16)

        def load_stage(sync, stage):
            each, turns = loads[stage][2:4]
            ahead = min(WS, each)
            who = expert_of if stage == "moe" else lambda sync, turn: 0
            e = who(sync, 0)
            for j in range(ahead):
                load(sync, stage, j, 0, e)
            if turns > 1:
                with sync.Fori(0, turns - 1) as turn:
                    e = who(sync, turn)
                    for j in range(ahead, each):
                        load(sync, stage, j, turn, e)
                    e = who(sync, turn + 1)
                    for j in range(ahead):
                        load(sync, stage, j, turn + 1, e)
            e = who(sync, turns - 1)
            for j in range(ahead, each):
                load(sync, stage, j, turns - 1, e)

        def expert_of(sync, item):
            if isinstance(item, int) and item == 0:
                sync.wait_ge(items_ready, 1)
            return sync.value_load(item_expert[0:1, bass.ds(item, 1)], min_val=0, max_val=NE - 1)

        def mm(out, lhsT, rhs, first, last):
            return nc.tensor.matmul(out, lhsT, rhs, start=first, stop=last)

        def pe_linear(stage, j, turn, weights, source, n=HT):
            s = take(stage, j, turn)
            out = pair(s, n)
            nk = len(weights)
            for half in range(2):
                for k in range(nk):
                    last = mm(out[:, half, :], weights[k], source(k, half * n, half * n + n), k == 0, k == nk - 1)
            last.then_inc(ps_full[s], 1)
            return s

        def from_h(k, a, b):
            return hT[:, k, a:b]

        def cols(w, nk, width, c):
            return [w[:, k * width + c * P:k * width + (c + 1) * P] for k in range(nk)]

        def pe_lam():
            nc.tensor.wait_ge(consts_in, 16 * 4)
            nc.tensor.wait_ge(lam_ready, 1)
            for i in range(2):
                s = take("lam", i)
                mm(ps[:, s, 0:1], cst[0:64, C_ONE:C_ONE + P], lam_pr[:, i:i + 1], True, True).then_inc(ps_full[s], 1)

        def pe_mod():
            nc.tensor.wait_ge(csilu_ready, 1)
            with nc.tensor.Fori(0, 12) as i:
                s = take("mod", 0, i)
                for b in range(4):
                    w = block("mod", b, i)
                    for kk in range(2):
                        k = 2 * b + kk
                        for half in range(2):
                            last = mm(ps[0:2, s, half * 512:(half + 1) * 512], csilu[:, 2 * k:2 * k + 2],
                                      w[:, kk * D + half * 512:kk * D + (half + 1) * 512], k == 0, k == KD - 1)
                last.then_inc(ps_full[s], 1)
                done(nc.tensor, "mod", 0, i)
                s = take("mod", 1, i)
                for j in range(KD):
                    last = mm(ps[:, s, 2 * j:2 * j + 2], tmp[0:2, j * P:(j + 1) * P], ident[0:2, 0:2], True, True)
                last.then_inc(ps_full[s], 1)

        def dve_mod(dve):
            with dve.Fori(0, 12) as i:
                s = full(dve, "mod", 0, i)
                nc.vector.tensor_copy(tmp[0:2, 0:D], ps[0:2, s, :]).then_inc(ps_free[s], 1)
                s = full(dve, "mod", 1, i)
                nc.vector.tensor_tensor(
                    modcol[:, bass.ds(i * 16, 16)].rearrange("p (k c) -> p k c", c=2),
                    ps[:, s, 0:16].rearrange("p (k c) -> p k c", c=2),
                    spread(wsm[:, bass.ds(i * 8 + S_MODB, 8)], 2, 2), ALU.add).then_inc(ps_free[s], 1)
            done(dve, "mod", 1, 11)
            for n, m in enumerate((1, 4, 7, 10)):
                last = nc.vector.scalar_tensor_tensor(
                    modA[:, n, :, :], modcol[:, m * 16:m * 16 + 16].rearrange("p (k c) -> p k c", c=2), 1.0,
                    spread(wsm[:, S_NORM + n * 8:S_NORM + n * 8 + 8], 2, 2), ALU.add, ALU.mult)
            last.then_inc(modA_ready, 1)

        def act_norm(act, n, x_done):
            x_done(act)
            for k in range(KD):
                nc.scalar.activation(tc[:, k, :], xc[:, k, :], ACT.Square).then_inc(sq_ready, 1)
            s = full(act, f"norm{n}", 0)
            nc.scalar.activation(std[:, :].rearrange("p (b n) -> p b n", b=2), pair(s), ACT.Sqrt,
                                 bias=eps, scale=1.0 / D).then_inc(ps_free[s], 1)
            if n < 4:
                m = (0, 3, 6, 9)[n]
                if n == 0:
                    act.wait_ge(modA_ready, 1)
                for k in range(KD):
                    act.wait_ge(hs_ready, 8 * n + k + 1)
                    for a, b, c in SEGS:
                        last = nc.scalar.activation(hT[:, k, a:b], hT[:, k, a:b], ACT.Identity,
                                                    bias=modcol[:, m * 16 + 2 * k + c:m * 16 + 2 * k + c + 1])
                    last.then_inc(h_ready, 1)

        def pe_norm(n):
            s = take(f"norm{n}", 0)
            for k in range(KD):
                nc.tensor.wait_ge(sq_ready, 8 * n + k + 1)
                for half in range(2):
                    last = nc.tensor.matmul(pair(s)[:, half, :], ones, tc[:, k, half * HT:(half + 1) * HT],
                                            start=(k == 0), stop=(k == KD - 1))
            last.then_inc(ps_full[s], 1)

        def dve_norm(dve, st, n):
            done(dve, f"norm{n}", 0)
            st.then(nc.vector.reciprocal(std[:, :], std[:, :]))
            if n == 0:
                dve.wait_ge(modA_ready, 1)
            for k in range(KD):
                for a, b, c in (SEGS if n < 4 else ((0, T, 0),)):
                    A = modA[:, n, k, c:c + 1] if n < 4 else wsm[:, S_NORM + 32 + k:S_NORM + 33 + k]
                    last = nc.vector.scalar_tensor_tensor(hT[:, k, a:b], xc[:, k, a:b], A, std[:, a:b],
                                                          ALU.mult, ALU.mult)
                last.then_inc(hs_ready, 1)

        def act_colnorm(act, stage, groups, base, scale):
            i = 0
            for group in groups:
                for src, _, _ in group:
                    nc.scalar.activation(tc[:, i, :], src, ACT.Square).then_inc(cn_sq, 1)
                    i += 1
            i = 0
            for g, group in enumerate(groups):
                s = full(act, stage, g)
                nc.scalar.activation(tc[:, i, :].rearrange("p (b n) -> p b n", b=2), pair(s), ACT.Sqrt,
                                     bias=eps, scale=scale[g]).then_inc(ps_free[s], 1)
                i += len(group)

        def pe_colnorm(stage, groups, base):
            i = 0
            for g, group in enumerate(groups):
                s = take(stage, g)
                nc.tensor.wait_ge(cn_sq, base + i + len(group))
                for half in range(2):
                    for c in range(len(group)):
                        last = mm(pair(s)[:, half, :], ones, tc[:, i + c, half * HT:(half + 1) * HT],
                                  c == 0, c == len(group) - 1)
                last.then_inc(ps_full[s], 1)
                i += len(group)

        def dve_colnorm(dve, st, stage, groups):
            i = 0
            for g, group in enumerate(groups):
                done(dve, stage, g)
                st.then(nc.vector.reciprocal(tc[:, i, :], tc[:, i, :]))
                for src, dst, w in group:
                    last = nc.vector.scalar_tensor_tensor(dst, src, w, tc[:, i, :], ALU.mult, ALU.mult)
                last.then_inc(cn_out, 1)
                i += len(group)

        l2_groups = [[(qkvT[:, c, :], qkvT[:, c, :], P ** -0.5 if c < H else 1.0)] for c in range(8)]
        obn_groups = [[(hT[:, H + h, :], hT[:, H + h, :], wsm[:, S_SUBLN:S_SUBLN + 1])] for h in range(H)]
        mla_groups = [[(cq[:, c, :], cq[:, c, :], wsm[:, S_QN + c:S_QN + c + 1]) for c in range(3)],
                      [(ckv[:, c, 0:T], ckv[:, c, 0:T], wsm[:, S_KVN + c:S_KVN + c + 1]) for c in range(2)]]

        def pe_even_in():
            nc.tensor.wait_ge(h_ready, 8)
            for c in range(12):
                if c % 2 == 0:
                    w = block("qkv", c // 2)
                pe_linear("qkv", c, 0, cols(w, KD, 256, c % 2), from_h)
            for c in range(4):
                if c % 2 == 0:
                    w = block("z", c // 2)
                pe_linear("z", c, 0, cols(w, KD, 256, c % 2), from_h)
            w, s = block("gat", 0), take("gat", 0)
            for t in range(NT):
                for k in range(KD):
                    last = mm(ps[:, s, t * 16:(t + 1) * 16], hT[:, k, t * P:(t + 1) * P], w[:, k * 16:(k + 1) * 16],
                              k == 0, k == KD - 1)
            last.then_inc(ps_full[s], 1)
            for j, (what, c) in enumerate(rope_order):
                if what == "P":
                    if c % 2 == 0:
                        w = block("qk", c // 2)
                    pe_linear("qk", j, 0, cols(w, KD, 256, c % 2), from_h)
                else:
                    done(nc.tensor, "qk", rope_order.index(("P", c)))
                    s = take("qk", j)
                    mm(ps[:, s, 0:DEC_SEQ], rot, qkraw[:, c % 2, SEQ:T], True, True).then_inc(ps_full[s], 1)
            w = [block("vb", 0), block("vb", 1)]
            for t in range(NT):
                s = take("vb", t)
                for b in range(2):
                    for k in range(KD):
                        last = mm(ps[:, s, b * 256:(b + 1) * 256], hT[:, k, t * P:(t + 1) * P],
                                  w[b][:, k * 256:(k + 1) * 256], k == 0, k == KD - 1)
                last.then_inc(ps_full[s], 1)

        def act_even_in(act):
            for c in range(12):
                s = full(act, "qkv", c)
                nc.scalar.activation(raw[:, 1:1 + SEQ], ps[:, s, 0:SEQ], ACT.Copy)
                nc.scalar.activation(raw[:, 2 + SEQ:2 + HT], ps[:, s, SEQ:HT], ACT.Copy)
                nc.scalar.activation(raw[:, 2 + HT:2 + T], ps[:, s, 512:512 + HT], ACT.Copy).then_inc(ps_free[s], 1)
                act.wait_ge(conv_ready, c + 1)
                nc.scalar.activation(qkvT[:, c, 0:SEQ], cv[:, 0:SEQ], ACT.Silu)
                nc.scalar.activation(qkvT[:, c, SEQ:T], cv[:, SEQ + 1:T + 1], ACT.Silu).then_inc(qkv_ready, 1)
            for c in range(4):
                s = full(act, "z", c)
                nc.scalar.activation(zT[:, c, :].rearrange("p (b n) -> p b n", b=2), pair(s), ACT.Silu
                                     ).then_inc(ps_free[s], 1)
            act.wait_ge(gate_in, 1)
            gr = gates_sb[:, :].rearrange("p (t c) -> p t c", c=16)
            nc.scalar.activation(gr[:, :, 8:16], gr[:, :, 8:16], ACT.Exp, scale=-1.0)
            nc.scalar.activation(dsm[:, 2, :, :, :].rearrange("p a t h -> p (a t h)"),
                                 dsm[:, 2, :, :, :].rearrange("p a t h -> p (a t h)"), ACT.Exp, scale=-1.0)
            nc.scalar.activation(wsm[:, S_ALOG:S_ALOG + 8], wsm[:, S_ALOG:S_ALOG + 8], ACT.Exp).then_inc(gate_e, 1)
            act.wait_ge(gate_e, 1)
            nc.scalar.activation(dsm[:, 2, :, :, :].rearrange("p a t h -> p (a t h)"),
                                 dsm[:, 2, :, :, :].rearrange("p a t h -> p (a t h)"), ACT.Ln,
                                 bias=ones[:, 0:1]).then_inc(gate_l, 1)
            for c in range(8):
                j = rope_order.index(("P", c))
                if c >= 2:
                    done(act, "qk", rope_order.index(("R", c - 2)))
                s = full(act, "qk", j)
                nc.scalar.activation(qkraw[:, c % 2, :].rearrange("p (b n) -> p b n", b=2), pair(s), ACT.Copy,
                                     scale=64 ** -0.5 if c < H else 1.0).then_inc(ps_free[s], 1)

        def dve_rope(st, raw_in, dst, s, prompt=True):
            nc.vector.tensor_copy(dst[:, 0:SEQ], raw_in[:, 0:SEQ])
            nc.vector.tensor_tensor(dst[:, SEQ:T], raw_in[:, SEQ:T], cos, ALU.mult)
            st.then(nc.vector.tensor_tensor(rtmp, ps[:, s, 0:DEC_SEQ], sin, ALU.mult))
            nc.vector.tensor_tensor(dst[:, SEQ:T], dst[:, SEQ:T], rtmp, ALU.add).then_inc(ps_free[s], 1)

        def dve_even_in(dve, st):
            for c in range(12):
                done(dve, "qkv", c)
                if c:
                    dve.wait_ge(qkv_ready, c)
                cw = wsm[:, S_CONV + 3 * c:S_CONV + 3 * c + 3]
                st.then(nc.vector.tensor_scalar(cv, raw[:, 0:641], cw[:, 0:1], None, ALU.mult))
                st.then(nc.vector.scalar_tensor_tensor(cv, raw[:, 1:642], cw[:, 1:2], cv, ALU.mult, ALU.add))
                nc.vector.scalar_tensor_tensor(cv, raw[:, 2:643], cw[:, 2:3], cv, ALU.mult, ALU.add
                                               ).then_inc(conv_ready, 1)
            s = full(dve, "gat", 0)
            nc.vector.tensor_copy(gates_sb[:, :], ps[:, s, 0:80]).then_inc(ps_free[s], 1)
            done(dve, "gat", 0)
            gr = gates_sb[:, :].rearrange("p (t d h) -> p t d h", d=4, h=H)
            sp = dsm[:, 2, :, :, :]
            for d in range(2):
                last = nc.vector.tensor_tensor(g_[:, d, :, :], gr[:, :, d, :],
                                               spread(wsm[:, S_DTB + d * H:S_DTB + (d + 1) * H], 1, NT), ALU.add)
            st.then(last)
            st.then(nc.vector.tensor_scalar(sp, g_, -1.0, None, ALU.mult))
            nc.vector.tensor_tensor(sp, sp, g_, ALU.max).then_inc(gate_in, 1)
            st.then(nc.vector.tensor_scalar(g_, g_, 0.0, None, ALU.max))
            dve.wait_ge(gate_e, 1)
            dve.wait_ge(gate_l, 1)
            st.then(nc.vector.tensor_tensor(g_, g_, sp, ALU.add))
            for d in range(2):
                nc.vector.scalar_tensor_tensor(g_[:, d, :, :], g_[:, d, :, :], -1.0,
                                               spread(wsm[:, S_ALOG + d * H:S_ALOG + (d + 1) * H], 1, NT),
                                               ALU.mult, ALU.mult)
                last = nc.vector.tensor_scalar(beta[:, d, :, :], gr[:, :, 2 + d, :], 1.0, None, ALU.add)
            st.then(last)
            nc.vector.reciprocal(beta, beta).then_inc(g_ready, 1)
            for c in range(8):
                s = full(dve, "qk", rope_order.index(("R", c)))
                if c:
                    done(dve, "qk", rope_order.index(("R", c - 1)))
                dve_rope(st, qkraw[:, c % 2, :], qT[:, c, :] if c < H else kT[:, c - H, 0:T], s)
            for t in range(NT):
                s = full(dve, "vb", t)
                nc.vector.tensor_copy(vB[:, t, :], ps[:, s, 0:512]).then_inc(ps_free[s], 1)

        def attention(heads, streams, stage, order, scores, values, probs, turned, item_base, stat):
            items = attention_items(heads)
            at = {x: j for j, x in enumerate(order)}
            nstat = 3 * streams

            def cells(i):
                return att[:, (i % 2) * 8:(i % 2) * 8 + 8]

            def pe():
                for j, (what, i, st_) in enumerate(order):
                    h, t = items[i]
                    blocks = (0,) if t == 0 else tuple(range(1, NT + 1))
                    if what == "scores":
                        s = take(stage, j)
                        if t == 0:
                            terms = scores(h, t, st_, 0, P)
                            for n, (q, k) in enumerate(terms):
                                last = mm(ps[:, s, 0:P], q, k, n == 0, n == len(terms) - 1)
                        else:
                            for half in range(2):
                                terms = scores(h, t, st_, P + half * HT, P + (half + 1) * HT)
                                for n, (q, k) in enumerate(terms):
                                    last = mm(pair(s)[:, half, :], q, k, n == 0, n == len(terms) - 1)
                    elif what == "turn":
                        nc.tensor.wait_ge(a_ready, item_base + i + 1)
                        s = take(stage, j)
                        for n in range(len(blocks)):
                            last = nc.tensor.transpose(ps[:, s, n * P:(n + 1) * P],
                                                       probs(i, 0)[:, n * P:(n + 1) * P], ident)
                    else:
                        done(nc.tensor, stage, at[("turn", i, 0)])
                        s = take(stage, j)
                        for n, b in enumerate(blocks):
                            last = mm(ps[:, s, 0:P], values(h, b), turned(i)[:, n * P:(n + 1) * P],
                                      n == 0, n == len(blocks) - 1)
                    last.then_inc(ps_full[s], 1)

            def view(i, ap, s):
                if items[i][1] == 0:
                    return ps[:, s, 0:P], ap[:, 0:P]
                return pair(s), ap.rearrange("p (b n) -> p b n", b=2)

            def dve(eng, st):
                for i in range(len(items) + 2):
                    if i < len(items):
                        h, t = items[i]
                        for st_ in range(streams):
                            s = full(eng, stage, at[("scores", i, st_)])
                            src, _ = view(i, probs(i, st_), s)
                            nc.vector.tensor_reduce(cells(i)[:, st_:st_ + 1], src, AX.X if t == 0 else AX.XY,
                                                    ALU.max, negate=True).then_inc(mx_ready, 1)
                        for st_ in range(streams):
                            done(eng, stage, at[("scores", i, st_)])
                        w = P if t == 0 else T
                        sums, inv = cells(i)[:, 2:2 + streams], cells(i)[:, 4:4 + streams]
                        st.then(nc.vector.reciprocal(inv, sums))
                        if streams == 1:
                            nc.vector.tensor_scalar(probs(i, 0)[:, 0:w], probs(i, 0)[:, 0:w], inv[:, 0:1], None,
                                                    ALU.mult).then_inc(a_ready, 1)
                        else:
                            nc.vector.tensor_scalar(probs(i, 0)[:, 0:w], probs(i, 0)[:, 0:w], inv[:, 0:1], None,
                                                    ALU.mult)
                            st.then(nc.vector.tensor_scalar(inv[:, 1:2], inv[:, 1:2], neglam[:, 0:1], None, ALU.mult))
                            nc.vector.scalar_tensor_tensor(probs(i, 0)[:, 0:w], probs(i, 1)[:, 0:w], inv[:, 1:2],
                                                           probs(i, 0)[:, 0:w], ALU.mult, ALU.add
                                                           ).then_inc(a_ready, 1)
                    if i >= 2:
                        h, t = items[i - 2]
                        s = full(eng, stage, at[("values", i - 2, 0)])
                        nc.vector.tensor_copy(hT[:, stat + h, t * P:(t + 1) * P], ps[:, s, 0:P]
                                              ).then_inc(ps_free[s], 1)

            def act(eng):
                for i in range(len(items) + 1):
                    if i < len(items):
                        for st_ in range(streams):
                            eng.wait_ge(mx_ready, (item_base * 2 if streams == 1 else 0) + i * streams + st_ + 1)
                            s, _ = R.use(stage, at[("scores", i, st_)])
                            src, dst = view(i, probs(i, st_), s)
                            nc.scalar.activation(dst, src, ACT.Exp, bias=cells(i)[:, st_:st_ + 1],
                                                 accum_out=cells(i)[:, 2 + st_:3 + st_]).then_inc(ps_free[s], 1)
                    if i >= 1:
                        s = full(eng, stage, at[("turn", i - 1, 0)])
                        w = P if items[i - 1][1] == 0 else T
                        nc.scalar.activation(turned(i - 1)[:, 0:w], ps[:, s, 0:w], ACT.Copy).then_inc(ps_free[s], 1)

            return pe, dve, act

        def diff_scores(h, t, st_, a, b):
            r = slice(st_ * ROPE, (st_ + 1) * ROPE)
            return [(qT[r, h, t * P:(t + 1) * P], kT[r, h, a:b])]

        def mla_scores(h, t, st_, a, b):
            r = slice((h % 2) * ROPE, (h % 2 + 1) * ROPE)
            return [(qn[:, h, t * P:(t + 1) * P], kn[:, h, a:b]), (qr[r, h // 2, t * P:(t + 1) * P], krT[r, a:b])]

        att0 = attention(H, 2, "att0", plan_b, diff_scores, lambda h, b: vB[:, b, h * P:(h + 1) * P],
                         lambda i, s: pB[:, (i % 2) * 2 + s, :], lambda i: aB[:, i % 2, :], 0, H)
        att1 = attention(HC, 1, "att1", plan_c, mla_scores, lambda h, b: vC[:, b, h * P:(h + 1) * P],
                         lambda i, s: pC[:, i % 2, :], lambda i: aC[:, i % 2, :], H * NT, 0)

        def quad(ap):
            return ap.rearrange("p (d h c) -> p d h c", d=2, h=H)

        def per_head(ap):
            return ap.rearrange("p (h c) -> p h c", h=H)

        gb = dT1
        TR = {n: i for i, n in enumerate(["tok", "gram", "grow", "C0"])}
        for lv in range(1, LEVELS):
            for n, what in enumerate(("T1", "XT", "X")):
                TR[(what, lv)] = 4 + 3 * (lv - 1) + n

        def prod(t, what):
            return DL * t + TR[what]

        def pool_delta(pool):
            for t in range(NT):
                if t == 0:
                    pool.wait_ge(g_ready, 1)
                    full(pool, "obn", H - 1)
                    pool.wait_ge(cn_out, 8 + H)
                else:
                    full(pool, "tri", prod(t - 1, ("XT", LEVELS - 1)))
                for d in range(2):
                    last = nc.gpsimd.tensor_copy(quad(gb)[:, d, :, :], spread(g_[:, d, t, :], 2, P))
                last.then_inc(gb_ready, 1)
                done(pool, "tri", prod(t, "gram"))
                for lv in range(LEVELS):
                    if lv == 1:
                        pool.wait_ge(dt_ready, t + 1)
                        full(pool, "tri", prod(t, "C0"))
                    if lv > 1:
                        full(pool, "tri", prod(t, ("T1", lv - 1)))
                    for d in range(2):
                        mask = cst[:, C_LVL + (lv * 2 + d) * P:C_LVL + (lv * 2 + d + 1) * P]
                        last = nc.gpsimd.tensor_tensor(quad(dC)[:, d, :, :], quad(dM)[:, d, :, :],
                                                       spread(mask, 1, H), ALU.mult)
                    last.then_inc(c_ready, 1)

        def pe_delta():
            nc.tensor.wait_ge(g_ready, 1)
            nc.tensor.wait_ge(cn_out, 8)
            s = take("cum", 0)
            for d in range(2):
                mm(ps[:, s, d * 20:d * 20 + 20], tri[d], g_[:, d, :, :].rearrange("p t h -> p (t h)"), True, True)
            mm(ps[:, s, 40:80], ones, g_.rearrange("p d t h -> p (d t h)"), True, True).then_inc(ps_full[s], 1)
            for t in range(NT):
                a, b = t * P, (t + 1) * P
                s = take("tri", prod(t, "tok"))
                for h in range(H):
                    nc.tensor.transpose(ps[:, s, h * P:(h + 1) * P], qkvT[:, H + h, a:b], ident)
                for h in range(H):
                    last = nc.tensor.transpose(ps[:, s, 512 + h * P:512 + (h + 1) * P], qkvT[:, 2 * H + h, a:b], ident)
                last.then_inc(ps_full[s], 1)
                s = take("tri", prod(t, "gram"))
                for h in range(H):
                    mm(ps[:, s, h * P:(h + 1) * P], qkvT[:, H + h, a:b], qkvT[:, H + h, a:b], True, True)
                for h in range(H):
                    last = mm(ps[:, s, 512 + h * P:512 + (h + 1) * P], qkvT[:, H + h, a:b], qkvT[:, h, a:b], True, True)
                last.then_inc(ps_full[s], 1)
                nc.tensor.wait_ge(gb_ready, t + 1)
                s = take("tri", prod(t, "grow"))
                for i in range(2 * H):
                    last = mm(ps[:, s, i * P:(i + 1) * P], gb[:, i * P:(i + 1) * P], tri[i // H], True, True)
                last.then_inc(ps_full[s], 1)
                nc.tensor.wait_ge(c_ready, LEVELS * t + 1)
                s = take("tri", prod(t, "C0"))
                for i in range(2 * H):
                    last = nc.tensor.transpose(ps[:, s, i * P:(i + 1) * P], dC[:, i * P:(i + 1) * P], ident)
                last.then_inc(ps_full[s], 1)
                nc.tensor.wait_ge(dt_ready, t + 1)
                for lv in range(1, LEVELS):
                    nc.tensor.wait_ge(c_ready, LEVELS * t + lv + 1)
                    done(nc.tensor, "tri", prod(t, "C0" if lv == 1 else ("X", lv - 1)))
                    s = take("tri", prod(t, ("T1", lv)))
                    for i in range(2 * H):
                        r = slice(i * P, (i + 1) * P)
                        last = mm(ps[:, s, r], dC[:, r], dD[:, r], True, True)
                    last.then_inc(ps_full[s], 1)
                    done(nc.tensor, "tri", prod(t, ("T1", lv)))
                    if lv > 1:
                        done(nc.tensor, "tri", prod(t, ("XT", lv - 1)))
                    s = take("tri", prod(t, ("XT", lv)))
                    for i in range(2 * H):
                        r = slice(i * P, (i + 1) * P)
                        last = mm(ps[:, s, r], dT1[:, r], DTs[:, t, r], True, True)
                    last.then_inc(ps_full[s], 1)
                    if lv < LEVELS - 1:
                        s = take("tri", prod(t, ("X", lv)))
                        for i in range(2 * H):
                            r = slice(i * P, (i + 1) * P)
                            last = mm(ps[:, s, r], DTs[:, t, r], dT1[:, r], True, True)
                        last.then_inc(ps_full[s], 1)

        def act_delta(act):
            act.wait_ge(decay_in, 1)
            flat = [dsm[:, i, :, :, :].rearrange("p d t h -> p (d t h)") for i in range(7)]
            nc.scalar.activation(flat[4], flat[2], ACT.Exp)
            nc.scalar.activation(flat[5], flat[5], ACT.Exp)
            nc.scalar.activation(flat[6], flat[3], ACT.Exp).then_inc(decay_out, 1)
            act.wait_ge(kv_out, 32)
            for t in range(NT):
                s = full(act, "tri", prod(t, "tok"))
                nc.scalar.activation(tok[:, t, :], ps[:, s, :], ACT.Copy).then_inc(ps_free[s], 1)
                act.wait_ge(e_in, t + 1)
                nc.scalar.activation(dE, dE, ACT.Exp).then_inc(e_out, 1)
                for lv in range(1, LEVELS):
                    s = full(act, "tri", prod(t, ("T1", lv)))
                    nc.scalar.activation(dT1, ps[:, s, :], ACT.Copy).then_inc(ps_free[s], 1)

        def dve_delta(dve, st):
            s = full(dve, "cum", 0)
            nc.vector.tensor_copy(dsm[:, 2:4, :, :, :].rearrange("p i d t h -> p (i d t h)"), ps[:, s, 0:80]
                                  ).then_inc(ps_free[s], 1)
            done(dve, "cum", 0)
            nc.vector.tensor_tensor(ed, glast, gcum, ALU.subtract).then_inc(decay_in, 1)
            dve.wait_ge(kv_out, 32)
            for t in range(NT):
                s = full(dve, "tri", prod(t, "grow"))
                if t == 0:
                    dve.wait_ge(cn_out, 8 + H)
                for d in range(2):
                    last = nc.vector.tensor_tensor(quad(dE)[:, d, :, :], quad(ps[:, s, :])[:, d, :, :],
                                                   spread(gcum[:, d, t, :], 2, P), ALU.subtract)
                last.then_inc(ps_free[s], 1)
                done(dve, "tri", prod(t, "grow"))
                for d in range(2):
                    last = nc.vector.scalar_tensor_tensor(
                        quad(dE)[:, d, :, :], quad(dE)[:, d, :, :], 0.0,
                        spread(cst[:, C_NEG + d * P:C_NEG + (d + 1) * P], 1, H), ALU.min, ALU.add)
                last.then_inc(e_in, 1)
                dve.wait_ge(e_out, t + 1)
                s = full(dve, "tri", prod(t, "gram"))
                for d in range(2):
                    nc.vector.tensor_tensor(per_head(Ais[:, t, d * 512:(d + 1) * 512]), per_head(ps[:, s, 512:1024]),
                                            quad(dE)[:, d, :, :], ALU.mult)
                    last = nc.vector.tensor_tensor(quad(dM)[:, d, :, :], quad(dE)[:, d, :, :],
                                                   spread(beta[:, d, t, :], 2, P), ALU.mult)
                st.then(last)
                for d in range(2):
                    last = nc.vector.tensor_tensor(quad(dM)[:, d, :, :], per_head(ps[:, s, 0:512]),
                                                   quad(dM)[:, d, :, :], ALU.mult)
                last.then_inc(ps_free[s], 1)
                done(dve, "tri", prod(t, "gram"))
                dve.wait_ge(c_ready, LEVELS * t + 1)
                nc.vector.tensor_tensor(DTs[:, t, :].rearrange("p (i c) -> p i c", c=P), spread(ident, 1, 2 * H),
                                        dC.rearrange("p (i c) -> p i c", c=P), ALU.subtract).then_inc(dt_ready, 1)
                s = full(dve, "tri", prod(t, "C0"))
                nc.vector.tensor_tensor(dD.rearrange("p (i c) -> p i c", c=P), spread(ident, 1, 2 * H),
                                        ps[:, s, :].rearrange("p (i c) -> p i c", c=P), ALU.subtract
                                        ).then_inc(ps_free[s], 1)
                for lv in range(1, LEVELS):
                    sx = full(dve, "tri", prod(t, ("XT", lv)))
                    if lv < LEVELS - 1:
                        s = full(dve, "tri", prod(t, ("X", lv)))
                        done(dve, "tri", prod(t, "C0" if lv == 1 else ("X", lv - 1)))
                        nc.vector.tensor_tensor(dD, dD, ps[:, s, :], ALU.subtract).then_inc(ps_free[s], 1)
                    if lv == 1:
                        dve.wait_ge(dt_ready, t + 1)
                    else:
                        done(dve, "tri", prod(t, ("XT", lv - 1)))
                    nc.vector.tensor_tensor(DTs[:, t, :], DTs[:, t, :], ps[:, sx, :], ALU.subtract
                                            ).then_inc(ps_free[sx], 1)

        sR, sV, sD, sO = dE, dM, dC, dD

        def pe_scan():
            nc.tensor.wait_ge(s_zero, 1)
            nc.tensor.wait_ge(state_in, 16)
            done(nc.tensor, "tri", prod(NT - 1, ("XT", LEVELS - 1)))
            for i, tiles in enumerate(SCAN):
                S = Sst[min(i, 1)]
                if i > 1:
                    done(nc.tensor, "scan", 5 * (i - 1) + 4)
                for n, base in ((0, H), (1, 0)):
                    s = take("scan", 5 * i + n)
                    for j in range(2 * H):
                        d, h = j // H, j % H
                        t = tiles[d]
                        last = mm(ps[:, s, j * P:(j + 1) * P], qkvT[:, base + h, t * P:(t + 1) * P],
                                  S[:, j * P:(j + 1) * P], True, True)
                    last.then_inc(ps_full[s], 1)
                nc.tensor.wait_ge(r_ready, i + 1)
                s = take("scan", 5 * i + 2)
                for j in range(2 * H):
                    r = slice(j * P, (j + 1) * P)
                    last = mm(ps[:, s, r], DTs[:, tiles[j // H], r], sR[:, r], True, True)
                last.then_inc(ps_full[s], 1)
                done(nc.tensor, "scan", 5 * i + 2)
                s = take("scan", 5 * i + 3)
                for j in range(2 * H):
                    r = slice(j * P, (j + 1) * P)
                    last = mm(ps[:, s, r], Ais[:, tiles[j // H], r], sV[:, r], True, True)
                last.then_inc(ps_full[s], 1)
                nc.tensor.wait_ge(vd_ready, i + 1)
                s = take("scan", 5 * i + 4)
                for j in range(2 * H):
                    r = slice(j * P, (j + 1) * P)
                    last = mm(ps[:, s, r], tok[:, tiles[j // H], (j % H) * P:(j % H + 1) * P], sD[:, r], True, True)
                last.then_inc(ps_full[s], 1)

        def dve_scan(dve, st):
            dve.wait_ge(decay_out, 1)
            seen = set()
            for i, tiles in enumerate(SCAN):
                S = Sst[min(i, 1)]

                def scaled(out, inp, factor):
                    for d, t in enumerate(tiles):
                        last = nc.vector.tensor_tensor(quad(out)[:, d, :, :], quad(inp)[:, d, :, :],
                                                       spread(factor[:, d, t, :], 2, P), ALU.mult)
                    return last

                s = full(dve, "scan", 5 * i)
                scaled(sR, ps[:, s, :], eg).then_inc(ps_free[s], 1)
                done(dve, "scan", 5 * i)
                for d, t in enumerate(tiles):
                    last = nc.vector.tensor_tensor(sR[:, d * 512:(d + 1) * 512], tok[:, t, 512:1024],
                                                   sR[:, d * 512:(d + 1) * 512], ALU.subtract)
                last.then_inc(r_ready, 1)
                s = full(dve, "scan", 5 * i + 1)
                scaled(sO, ps[:, s, :], eg).then_inc(ps_free[s], 1)
                st.then(scaled(S, S, el))
                s = full(dve, "scan", 5 * i + 2)
                scaled(sV, ps[:, s, :], beta).then_inc(ps_free[s], 1)
                done(dve, "scan", 5 * i + 2)
                scaled(sD, sV, ed).then_inc(vd_ready, 1)
                done(dve, "scan", 5 * i + 1)
                s = full(dve, "scan", 5 * i + 3)
                for d, t in enumerate(tiles):
                    o = oS[:, t, :] if t not in seen else sO[:, d * 512:(d + 1) * 512]
                    last = nc.vector.tensor_tensor(o, sO[:, d * 512:(d + 1) * 512], ps[:, s, d * 512:(d + 1) * 512],
                                                   ALU.add)
                    if d == 0:
                        again = [x for x in enumerate(tiles) if x[1] in seen or (x[0] == 1 and tiles[0] == tiles[1])]
                        seen.add(t)
                seen.add(tiles[1])
                last.then_inc(ps_free[s], 1)
                done(dve, "scan", 5 * i + 3)
                for d, t in again:
                    st.then(nc.vector.tensor_tensor(oS[:, t, :], oS[:, t, :], sO[:, d * 512:(d + 1) * 512], ALU.add))
                s = full(dve, "scan", 5 * i + 4)
                nc.vector.tensor_tensor(S, S, ps[:, s, :], ALU.add).then_inc(ps_free[s], 1)
                done(dve, "scan", 5 * i + 4)
            sq = tmp[:, 0:NT * 512]
            oF = oS.rearrange("p t c -> p (t c)")
            st.then(nc.vector.tensor_tensor(sq, oF, oF, ALU.mult))
            nc.vector.tensor_reduce(osd[:, :], sq.rearrange("p (i c) -> p i c", c=P), AX.X, ALU.add
                                    ).then_inc(os_ready, 1)
            dve.wait_ge(od_ready, 1)
            st.then(nc.vector.reciprocal(osd[:, :], osd[:, :]))
            nc.vector.tensor_tensor(oF.rearrange("p (i c) -> p i c", c=P), oF.rearrange("p (i c) -> p i c", c=P),
                                    spread(osd[:, :], 2, P), ALU.mult).then_inc(on_ready, 1)
            dve.wait_ge(state_out, 16)
            for t in range(NT):
                s = full(dve, "onrm", t)
                nc.vector.scalar_tensor_tensor(hT[:, 0:H, t * P:(t + 1) * P], per_head(ps[:, s, 0:512]),
                                               wsm[:, S_ONORM:S_ONORM + 1], zT[:, :, t * P:(t + 1) * P],
                                               ALU.mult, ALU.mult).then_inc(ps_free[s], 1)

        def act_onorm(act):
            act.wait_ge(os_ready, 1)
            nc.scalar.activation(osd[:, :], osd[:, :], ACT.Sqrt, bias=eps, scale=1.0 / P).then_inc(od_ready, 1)

        def pe_onorm():
            nc.tensor.wait_ge(on_ready, 1)
            for t in range(NT):
                s = take("onrm", t)
                for h in range(H):
                    last = nc.tensor.transpose(ps[:, s, h * P:(h + 1) * P], oS[:, t, h * P:(h + 1) * P], ident)
                last.then_inc(ps_full[s], 1)

        def pe_out(stage):
            with nc.tensor.Fori(0, 2) as turn:
                for j in range(4):
                    if j % 2 == 0:
                        w = block(stage, j // 2, turn)
                    pe_linear(stage, j, turn, cols(w, KD, 256, j % 2), from_h)

        def dve_residual(dve, stage, each, turns, gate):
            with dve.Fori(0, turns) as turn:
                for j in range(each):
                    s = full(dve, stage, j, turn)
                    c = turn * each + j
                    for a, b, at, grp in ((0, SEQ, 0, 0), (SEQ, HT, SEQ, 1), (HT, T, 512, 1)):
                        xs = xT[:, bass.ds(c * T + a, b - a)]
                        last = nc.vector.scalar_tensor_tensor(xs, ps[:, s, at:at + b - a],
                                                              modcol[:, bass.ds(c * 2 + (gate * 16 + grp), 1)], xs,
                                                              ALU.mult, ALU.add)
                    last.then_inc(ps_free[s], 1)

        def pe_ffn():
            nc.tensor.wait_ge(h_ready, 16)
            with nc.tensor.Fori(0, 2) as turn:
                for j in range(EC):
                    w = block("fgu", j, turn)
                    for u in range(2):
                        pe_linear("fgu", 2 * j + u, turn, cols(w, KD, 256, u), from_h)
            done(nc.tensor, "fgu", 2 * EC - 1, 1)
            with nc.tensor.Fori(0, 4) as turn:
                for j in range(2):
                    w = [block("fdn", 2 * j, turn), block("fdn", 2 * j + 1, turn)]
                    pe_linear("fdn", j, turn, [w[k // LK][:, (k % LK) * P:(k % LK + 1) * P] for k in range(FC)],
                              lambda k, a, b: actT[:, k, a:b])

        def act_gate(act, stage, j, turn):
            if j >= 2:
                done(act, stage, 2 * (j - 2) + 1, turn)
            else:
                done(act, stage, 2 * (EC - 1 - j) + 1, turn - 1)
            s = full(act, stage, 2 * j, turn)
            nc.scalar.activation(sg[:, j % 2, :].rearrange("p (b n) -> p b n", b=2), pair(s), ACT.Silu
                                 ).then_inc(ps_free[s], 1)

        def dve_up(dve, stage, j, turn, out):
            done(dve, stage, 2 * j, turn)
            s = full(dve, stage, 2 * j + 1, turn)
            nc.vector.tensor_tensor(out.rearrange("p (b n) -> p b n", b=2),
                                    sg[:, j % 2, :].rearrange("p (b n) -> p b n", b=2), pair(s), ALU.mult
                                    ).then_inc(ps_free[s], 1)

        def pe_odd_in():
            nc.tensor.wait_ge(h_ready, 24)
            for c in range(6):
                if c % 2 == 0:
                    w = block("oi", c // 2)
                pe_linear("oi", c, 0, cols(w, KD, 256, c % 2), from_h)
            pe_colnorm("mlan", mla_groups, 12)
            done(nc.tensor, "oi", 5)
            s = take("oi", 6)
            mm(ps[:, s, 0:DEC_SEQ], rot, krraw[:, SEQ:T], True, True).then_inc(ps_full[s], 1)

        def pe_odd_qkv():
            nc.tensor.wait_ge(cn_out, 13)

            def from_cq(k, a, b):
                return cq[:, k, a:b]

            for c in range(HC):
                if c % 4 == 0:
                    w = block("uqn", c // 4)
                pe_linear("uqn", c, 0, cols(w, 3, 512, c % 4), from_cq)
            w = block("uqr", 0)
            for j, (what, c) in enumerate(uq_order):
                if what == "P":
                    pe_linear("uqr", j, 0, cols(w, 3, 512, c), from_cq)
                else:
                    done(nc.tensor, "uqr", uq_order.index(("P", c)))
                    s = take("uqr", j)
                    mm(ps[:, s, 0:DEC_SEQ], rot, qraw[:, c % 2, SEQ:T], True, True).then_inc(ps_full[s], 1)
            nc.tensor.wait_ge(cn_out, 14)
            nc.tensor.wait_ge(mla_caches_in, 32)
            w = block("kn", 0)
            for c in range(HC):
                pe_linear("kn", c, 0, cols(w, 2, D, c), lambda k, a, b: ckv[:, k, a:b], TK // 2)
            w = block("vv", 0)
            for t in range(NT + 1):
                s = take("vv", t)
                for half in range(2):
                    for k in range(2):
                        last = mm(ps[:, s, half * 512:(half + 1) * 512], ckv[:, k, t * P:(t + 1) * P],
                                  w[:, k * D + half * 512:k * D + (half + 1) * 512], k == 0, k == 1)
                last.then_inc(ps_full[s], 1)

        def act_odd_in(act):
            for c in range(6):
                s = full(act, "oi", c)
                dst = cq[:, c, :] if c < 3 else ckv[:, c - 3, 0:T] if c < 5 else krraw
                nc.scalar.activation(dst.rearrange("p (b n) -> p b n", b=2), pair(s), ACT.Copy
                                     ).then_inc(ps_free[s], 1)
            done(act, "oi", 4)
            act_colnorm(act, "mlan", mla_groups, 12, [1 / 384, 1 / 256])

        def act_odd_qkv(act):
            scale = 192 ** -0.5
            act.wait_ge(cn_out, 14)
            for c in range(HC):
                s = full(act, "uqn", c)
                nc.scalar.activation(qn[:, c, :].rearrange("p (b n) -> p b n", b=2), pair(s), ACT.Copy, scale=scale
                                     ).then_inc(ps_free[s], 1)
            for c in range(4):
                if c >= 2:
                    done(act, "uqr", uq_order.index(("R", c - 2)))
                s = full(act, "uqr", uq_order.index(("P", c)))
                nc.scalar.activation(qraw[:, c % 2, :].rearrange("p (b n) -> p b n", b=2), pair(s), ACT.Copy,
                                     scale=scale).then_inc(ps_free[s], 1)
            for c in range(HC):
                s = full(act, "kn", c)
                nc.scalar.activation(kn[:, c, :].rearrange("p (b n) -> p b n", b=2), pair(s, TK // 2), ACT.Copy
                                     ).then_inc(ps_free[s], 1)

        def dve_odd(dve, st):
            dve_colnorm(dve, st, "mlan", mla_groups)
            s = full(dve, "oi", 6)
            dve_rope(st, krraw, krT[:, 0:T], s)
            for c in range(4):
                s = full(dve, "uqr", uq_order.index(("R", c)))
                if c == 0:
                    done(dve, "oi", 6)
                else:
                    done(dve, "uqr", uq_order.index(("R", c - 1)))
                dve_rope(st, qraw[:, c % 2, :], qr[:, c, :], s)
            for t in range(NT + 1):
                s = full(dve, "vv", t)
                nc.vector.tensor_copy(vC[:, t, :], ps[:, s, :]).then_inc(ps_free[s], 1)

        def rows8(k, n=NE):
            return tmp[:, 2 * T + 64 * k:2 * T + 64 * k + NT * n].rearrange("p (t e) -> p t e", e=n)

        rt = gates_sb[:, 0:NT * NE].rearrange("p (t e) -> p t e", e=NE)
        top, topi, topf, oh1, oh2, oh, pos, prd = (rows8(k) for k in range(8))
        topi = topi.bitcast(U32)
        tw = tmp[:, 2 * T + 512:2 * T + 512 + NT]
        cnt, tiles_e, last_e, first_e = (tmp[:, 2 * T + 528 + 8 * i:2 * T + 536 + 8 * i] for i in range(4))
        cmp = tmp[:, 2 * T + 576:2 * T + 576 + (ITEMS + 1) * NE].rearrange("p (i e) -> p i e", e=NE)
        sgE = tmp[:, 0:2 * P].rearrange("p (b s) -> p b s", b=2)
        sel1 = tmp[:, T:2 * T].rearrange("p (t s) -> p t s", t=NT)
        whof = tmp[:, 2 * T + 800:2 * T + 800 + ITEMS + 1]

        def pe_router():
            nc.tensor.wait_ge(h_ready, 32)
            w, s = block("rt", 0), take("rt", 0)
            for t in range(NT):
                for k in range(KD):
                    last = mm(ps[:, s, t * NE:(t + 1) * NE], hT[:, k, t * P:(t + 1) * P], w[:, k * NE:(k + 1) * NE],
                              k == 0, k == KD - 1)
            last.then_inc(ps_full[s], 1)
            for t in range(NT):
                s = take("ht", t)
                for k in range(KD):
                    last = nc.tensor.transpose(ps[:, s, k * P:(k + 1) * P], hT[:, k, t * P:(t + 1) * P], ident)
                last.then_inc(ps_full[s], 1)
            nc.tensor.wait_ge(oh_ready, 1)
            s = take("cnt", 0)
            for t in range(NT):
                for u in range(t + 1):
                    mm(ps[:, s, t * NE:(t + 1) * NE], tri[0] if u == t else ones, oh[:, u, :], u == 0, u == t)
            for u in range(NT):
                last = mm(ps[:, s, NT * NE:(NT + 1) * NE], ones, oh[:, u, :], u == 0, u == NT - 1)
            last.then_inc(ps_full[s], 1)

        def dve_router(dve, st):
            dve.wait_ge(mla_out, 32)
            nc.vector.memset(yacc, 0.0)
            nc.vector.memset(expr[:, 10880:13568].bitcast(F32), 0.0)
            nc.vector.memset(inw[:, :, :], 0.0).then_inc(exp_zero, 1)
            s = full(dve, "rt", 0)
            nc.vector.tensor_copy(gates_sb[:, 0:NT * NE], ps[:, s, 0:NT * NE]).then_inc(ps_free[s], 1)
            done(dve, "rt", 0)
            for t in range(NT):
                last = nc.vector.max(top[:, t, :], rt[:, t, :])
            st.then(last)
            for t in range(NT):
                st.then(nc.vector.max_index(topi[:, t, :], top[:, t, :], rt[:, t, :]))
            nc.vector.tensor_copy(topf, topi)
            nc.vector.tensor_tensor(tw, top[:, :, 1], top[:, :, 0], ALU.subtract).then_inc(top_ready, 1)
            dve.wait_ge(top_ready, 1)
            for t in range(NT):
                for i, o in enumerate((oh1, oh2)):
                    last = nc.vector.tensor_scalar(o[:, t, :], iota[:, 0:NE], topf[:, t, i:i + 1], None, ALU.is_equal)
            st.then(last)
            nc.vector.tensor_tensor(oh, oh1, oh2, ALU.add).then_inc(oh_ready, 1)
            dve.wait_ge(top_exp, 1)
            st.then(nc.vector.tensor_scalar(tokw[:, 1, :], tw, 1.0, None, ALU.add))
            st.then(nc.vector.reciprocal(tokw[:, 0, :], tokw[:, 1, :]))
            st.then(nc.vector.tensor_tensor(tokw[:, 1, :], tw, tokw[:, 0, :], ALU.mult))
            for t in range(NT):
                dve.wait_ge(hhi_ready, t + 1)
                s, _ = R.use("ht", t)
                nc.vector.tensor_tensor(hlo[:, t, :], ps[:, s, :], hhi[:, t, :].bitcast(F32), ALU.subtract
                                        ).then_inc(ps_free[s], 1)
            s = full(dve, "cnt", 0)
            nc.vector.tensor_copy(pos, ps[:, s, 0:NT * NE].rearrange("p (t e) -> p t e", e=NE))
            nc.vector.tensor_copy(cnt, ps[:, s, NT * NE:(NT + 1) * NE]).then_inc(ps_free[s], 1)
            done(dve, "cnt", 0)
            st.then(nc.vector.tensor_scalar(tiles_e, cnt, 0.0, None, ALU.is_gt))
            for m in range(1, NT):
                st.then(nc.vector.scalar_tensor_tensor(tiles_e, cnt, float(m * P), tiles_e, ALU.is_gt, ALU.add))
            st.then(nc.vector.tensor_tensor_scan(last_e, ones[:, 0:NE], tiles_e, 0.0, ALU.mult, ALU.add))
            nc.vector.tensor_tensor(cmp, spread(last_e, 1, ITEMS + 1), spread(iota[:, 0:ITEMS + 1], 2, NE), ALU.is_le)
            st.then(nc.vector.tensor_tensor(first_e, last_e, tiles_e, ALU.subtract))
            nc.vector.tensor_reduce(whof, cmp, AX.X, ALU.add)
            st.then(nc.vector.tensor_scalar(first_e, first_e, float(P), -1.0, ALU.mult, ALU.add))
            st.then(nc.vector.tensor_scalar(whof, whof, float(NE - 1), None, ALU.min))
            nc.vector.tensor_copy(item_expert[0:1, :], whof[0:1, :]).then_inc(items_ready, 1)
            st.then(nc.vector.tensor_tensor(pos, pos, spread(first_e, 1, NT), ALU.add))
            for i, o in enumerate((oh1, oh2)):
                st.then(nc.vector.tensor_tensor(prd, pos, o, ALU.mult))
                st.then(nc.vector.tensor_reduce(slot_of[:, i, :], prd, AX.X, ALU.add))
            dve_select(st)

        def dve_select(st):
            for t in range(NT):
                last = nc.vector.tensor_scalar(sel1[:, t, :], iota, slot_of[:, 0, t:t + 1], None, ALU.is_equal)
            st.then(last)
            for t in range(NT):
                last = nc.vector.scalar_tensor_tensor(sel[:, t, :], iota, slot_of[:, 1, t:t + 1], sel1[:, t, :],
                                                      ALU.is_equal, ALU.add)
            last.then_inc(sel_ready, 1)

        def pe_gather(stage, i, turn, item):
            nc.tensor.wait_ge(sel_ready, item + 1)
            s = take(stage, i, turn)
            for half in range(2):
                c = slice(half * 512, (half + 1) * 512)
                for t in range(NT):
                    for part, x in enumerate((hhi, hlo)):
                        last = mm(ps[:, s, c], sel[:, t, :], x[:, t, c], t == 0 and part == 0,
                                  t == NT - 1 and part == 1)
            last.then_inc(ps_full[s], 1)

        def pe_turn_rows(stage, i, turn, src):
            done(nc.tensor, stage, src, turn)
            s = take(stage, i, turn)
            for k in range(KD):
                last = nc.tensor.transpose(ps[:, s, k * P:(k + 1) * P], xs[:, k * P:(k + 1) * P], ident)
            last.then_inc(ps_full[s], 1)

        def pe_scatter(stage, base, turn):
            for t in range(NT):
                s = take(stage, base + t, turn)
                for half in range(2):
                    c = slice(half * 512, (half + 1) * 512)
                    for part, y in enumerate((yhi, ylo)):
                        last = mm(ps[:, s, c], selT[:, t * P:(t + 1) * P], y[:, c], part == 0, part == 1)
                last.then_inc(ps_full[s], 1)

        def pe_moe():
            done(nc.tensor, "ht", NT - 1)
            nc.tensor.wait_ge(exp_zero, 1)
            pe_gather("moe0", 0, 0, 0)
            pe_turn_rows("moe0", 1, 0, 0)
            done(nc.tensor, "moe0", 1)
            at = ITEM.index
            with nc.tensor.Fori(0, ITEMS) as i:
                for j in range(EC):
                    if j == 0:
                        done(nc.tensor, "moe", at("turnX"), i - 1)
                    if j == 2:
                        for what in ("dn0", "dn1", "turnP"):
                            done(nc.tensor, "moe", at(what), i - 1)
                        pe_scatter("moe", at("sc0"), i)
                        s = take("moe", at("turnP"), i)
                        for t in range(NT):
                            last = nc.tensor.transpose(ps[:, s, t * P:(t + 1) * P], sel[:, t, :].bitcast(F32), ident)
                        last.then_inc(ps_full[s], 1)
                    w, s = block("moe", j, i), take("moe", at(f"gu{j}"), i)
                    for u in range(2):
                        for k in range(KD):
                            last = mm(ps[:, s, u * 512:u * 512 + P], w[:, k * 256 + u * P:k * 256 + (u + 1) * P],
                                      xe[:, k * P:(k + 1) * P], k == 0, k == KD - 1)
                    last.then_inc(ps_full[s], 1)
                pe_gather("moe", at("gather"), i, i + 1)
                for half in range(2):
                    if half == 0:
                        done(nc.tensor, "moe", at(f"gu{EC - 1}"), i)
                    else:
                        pe_turn_rows("moe", at("turnX"), i, at("gather"))
                    w = [block("moe", EC + 3 * half + n, i) for n in range(3)]
                    s = take("moe", at(f"dn{half}"), i)
                    for k in range(EC):
                        last = mm(ps[:, s, 0:512], actE[:, k, :], w[k // 4][:, (k % 4) * 512:(k % 4 + 1) * 512],
                                  k == 0, k == EC - 1)
                    last.then_inc(ps_full[s], 1)
            for half in range(2):
                done(nc.tensor, "moe", at(f"dn{half}"), ITEMS - 1)
            done(nc.tensor, "moe", at("turnP"), ITEMS - 1)
            pe_scatter("moe1", 0, 0)

        def act_moe(act):
            at = ITEM.index
            act.wait_ge(mla_out, 32)
            for t in range(NT):
                s = full(act, "ht", t)
                nc.scalar.activation(hhi[:, t, :], ps[:, s, :], ACT.Copy).then_inc(hhi_ready, 1)
            s = full(act, "moe0", 0)
            nc.scalar.activation(xs, ps[:, s, :], ACT.Copy).then_inc(ps_free[s], 1)
            s = full(act, "moe0", 1)
            nc.scalar.activation(xe, ps[:, s, :], ACT.Copy).then_inc(ps_free[s], 1)
            with act.Fori(0, ITEMS) as i:
                for j in range(EC):
                    done(act, "moe", at(f"gu{j - 2 if j >= 2 else EC - 1 - j}"), i if j >= 2 else i - 1)
                    s = full(act, "moe", at(f"gu{j}"), i)
                    nc.scalar.activation(sgE[:, j % 2, :], ps[:, s, 0:P], ACT.Silu).then_inc(silu_ready, 1)
                s = full(act, "moe", at("gather"), i)
                nc.scalar.activation(xs, ps[:, s, :], ACT.Copy).then_inc(ps_free[s], 1)
                s = full(act, "moe", at("dn0"), i)
                nc.scalar.activation(yhi[:, 0:512], ps[:, s, 0:512], ACT.Copy).then_inc(yhi_ready, 1)
                s = full(act, "moe", at("turnX"), i)
                nc.scalar.activation(xe, ps[:, s, :], ACT.Copy).then_inc(ps_free[s], 1)
                s = full(act, "moe", at("dn1"), i)
                nc.scalar.activation(yhi[:, 512:1024], ps[:, s, 0:512], ACT.Copy).then_inc(yhi_ready, 1)

        def dve_scattered(stage, j, turn, t):
            s = full(nc.vector, stage, j, turn)
            nc.vector.scalar_tensor_tensor(yacc[:, t, :], ps[:, s, :], inw[:, 0, t:t + 1], yacc[:, t, :],
                                           ALU.mult, ALU.add).then_inc(ps_free[s], 1)

        def dve_moe(dve, st):
            at = ITEM.index
            dve.wait_ge(exp_zero, 1)
            with dve.Fori(0, ITEMS) as i:
                st.loop(i, 5)
                for j in range(EC):
                    if j == 2:
                        for t in range(NT):
                            dve_scattered("moe", at(f"sc{t}"), i, t)
                        s = full(dve, "moe", at("turnP"), i)
                        nc.vector.tensor_copy(selT, ps[:, s, 0:T]).then_inc(ps_free[s], 1)
                        done(dve, "moe", at(f"sc{NT - 1}"), i)
                        w2 = inw[:, 1:3, :]
                        st.then(nc.vector.tensor_scalar(w2, slot_of[:, :, :], 0.0, None, ALU.is_ge))
                        st.then(nc.vector.scalar_tensor_tensor(w2, slot_of[:, :, :], float(P), w2, ALU.is_lt, ALU.mult))
                        st.then(nc.vector.tensor_tensor(w2, w2, tokw[:, :, :], ALU.mult))
                        nc.vector.tensor_scalar(slot_of[:, :, :], slot_of[:, :, :], float(-P), None, ALU.add)
                        st.then(nc.vector.tensor_tensor(inw[:, 0, :], inw[:, 1, :], inw[:, 2, :], ALU.add))
                        dve_select(st)
                    dve.wait_ge(silu_ready, i * EC + (j + 1))
                    s, _ = R.use("moe", at(f"gu{j}"), i)
                    nc.vector.tensor_tensor(actE[:, j, :], sgE[:, j % 2, :], ps[:, s, 512:512 + P], ALU.mult
                                            ).then_inc(ps_free[s], 1)
                for half in range(2):
                    dve.wait_ge(yhi_ready, i * 2 + (half + 1))
                    s, _ = R.use("moe", at(f"dn{half}"), i)
                    c = slice(half * 512, (half + 1) * 512)
                    nc.vector.tensor_tensor(ylo[:, c], ps[:, s, 0:512], yhi[:, c].bitcast(F32), ALU.subtract
                                            ).then_inc(ps_free[s], 1)
            st.end(5, ITEMS)
            for t in range(NT):
                dve_scattered("moe1", t, 0, t)

        def pe_moe_out():
            done(nc.tensor, "moe1", NT - 1)
            for c in range(KD):
                s = take("yt", c)
                for t in range(NT):
                    last = nc.tensor.transpose(ps[:, s, t * P:(t + 1) * P], yacc[:, t, c * P:(c + 1) * P], ident)
                last.then_inc(ps_full[s], 1)

        def dve_moe_out(dve):
            for c in range(KD):
                s = full(dve, "yt", c)
                for a, b, grp in SEGS:
                    last = nc.vector.scalar_tensor_tensor(xc[:, c, a:b], ps[:, s, a:b],
                                                          modcol[:, 11 * 16 + 2 * c + grp:11 * 16 + 2 * c + grp + 1],
                                                          xc[:, c, a:b], ALU.mult, ALU.add)
                last.then_inc(ps_free[s], 1)

        block_ = ctx.enter_context(nc.Block())

        @block_.sync
        def _(sync):
            sync.dma_start(wsm[:, :], I["wsm"]).then_inc(consts_in, 16)
            sync.dma_start(cst[:, :], I["cst"]).then_inc(consts_in, 16)
            sync.dma_start(lam_in[:, :], I["lam"]).then_inc(consts_in, 16)
            sync.dma_start(cossin[:, :, :], I["cossin"]).then_inc(consts_in, 16)
            for stage in loads:
                load_stage(sync, stage)
                if stage == "mod":
                    sync.dma_start(xT[:, :], I["x"]).then_inc(x_in, 16)
            sync.wait_ge(hs_ready, 8 * 5)
            sync.dma_start(O["y"], hT[:, :, :].rearrange("p k t -> p (k t)")).then_inc(y_out, 16)
            sync.wait_ge(y_out, 16)

        @block_.gpsimd
        def _(pool):
            pool.dma_start(kT[:, :, T:TK], I["ck"]).then_inc(caches_in, 16)
            pool.dma_start(vB[:, NT, :], I["cv"]).then_inc(caches_in, 16)
            done(pool, "qk", 15)
            pool.dma_start(O["dk"], kT[:, :, 0:SEQ]).then_inc(kv_out, 16)
            done(pool, "vb", 0)
            pool.dma_start(O["dv"], vB[:, 0, :]).then_inc(kv_out, 16)
            full(pool, "vb", NT - 1)
            pool.dma_start(Sst[1], I["state"]).then_inc(state_in, 16)
            pool_delta(pool)
            done(pool, "scan", 4)
            pool.dma_start(O["state"], Sst[0]).then_inc(state_out, 16)
            full(pool, "fdn", 1, 3)
            pool.dma_start(ckv[:, :, T:TK], I["cckv"]).then_inc(mla_caches_in, 16)
            pool.dma_start(krT[:, T:TK], I["ckr"]).then_inc(mla_caches_in, 16)
            done(pool, "oi", 6)
            pool.dma_start(O["kr"], krT[0:ROPE, 0:SEQ]).then_inc(mla_out, 16)
            pool.wait_ge(cn_out, 14)
            pool.dma_start(O["ckv"], ckv[:, :, 0:SEQ]).then_inc(mla_out, 16)
            pool.wait_ge(kv_out, 32)
            pool.wait_ge(state_out, 16)
            pool.wait_ge(mla_out, 32)

        @block_.scalar
        def _(act):
            act.wait_ge(consts_in, 16 * 4)
            nc.scalar.activation(csilu[:, :], wsm[:, S_C:S_C + 16], ACT.Silu).then_inc(csilu_ready, 1)
            for i in range(2):
                s = full(act, "lam", i)
                nc.scalar.activation(lam_e[:, i:i + 1], ps[:, s, 0:1], ACT.Exp).then_inc(ps_free[s], 1)
            act_norm(act, 0, lambda a: (a.wait_ge(x_in, 16), full(a, "mod", 1, 11)))
            act_even_in(act)
            act.wait_ge(qkv_ready, 12)
            act_colnorm(act, "l2", l2_groups, 0, [1.0] * 8)
            att0[2](act)
            done(act, "att0", len(plan_b) - 1)
            act.wait_ge(cn_out, 8)
            act_colnorm(act, "obn", obn_groups, 8, [1 / P] * H)
            act_delta(act)
            act_onorm(act)
            act_norm(act, 1, lambda a: done(a, "eo", 3, 1))
            with act.Fori(0, 2) as turn:
                for j in range(EC):
                    act_gate(act, "fgu", j, turn)
            act_norm(act, 2, lambda a: done(a, "fdn", 1, 3))
            act_odd_in(act)
            act_odd_qkv(act)
            att1[2](act)
            act_norm(act, 3, lambda a: done(a, "oo", 3, 1))
            act.wait_ge(top_ready, 1)
            nc.scalar.activation(tw, tw, ACT.Exp).then_inc(top_exp, 1)
            act_moe(act)
            act_norm(act, 4, lambda a: done(a, "yt", KD - 1))

        @block_.vector
        def _(dve):
            st = Steps(dve, dve_step)
            dve.wait_ge(consts_in, 16 * 4)
            for i in range(2):
                last = nc.vector.tensor_tensor(lam_pr[:, i:i + 1], lam_in[:, 2 * i:2 * i + 1],
                                               lam_in[:, 2 * i + 1:2 * i + 2], ALU.mult)
            last.then_inc(lam_ready, 1)
            for col in (0, 1 + SEQ, 2 + T):
                last = nc.vector.memset(raw[:, col:col + 1], 0.0)
            st.then(last)
            done(dve, "lam", 0)
            done(dve, "lam", 1)
            st.then(nc.vector.tensor_tensor(neglam[:, :], lam_e[:, 1:2], lam_e[:, 0:1], ALU.subtract))
            st.then(nc.vector.tensor_scalar(neglam[:, :], neglam[:, :], -LAM_INIT, None, ALU.add))
            st.then(nc.vector.tensor_scalar(wsm[:, S_SUBLN:S_SUBLN + 1], wsm[:, S_SUBLN:S_SUBLN + 1],
                                            1.0 - LAM_INIT, None, ALU.mult))
            dve_mod(dve)
            dve_norm(dve, st, 0)
            dve_even_in(dve, st)
            dve_colnorm(dve, st, "l2", l2_groups)
            dve.wait_ge(caches_in, 32)
            att0[1](dve, st)
            dve_colnorm(dve, st, "obn", obn_groups)
            nc.vector.memset(Sst[0], 0.0).then_inc(s_zero, 1)
            dve_delta(dve, st)
            dve_scan(dve, st)
            dve_residual(dve, "eo", 4, 2, 2)
            dve_norm(dve, st, 1)
            with dve.Fori(0, 2) as turn:
                for j in range(EC):
                    dve_up(dve, "fgu", j, turn, arena[:, bass.ds((turn * EC + j) * T, T)])
            dve_residual(dve, "fdn", 2, 4, 5)
            dve_norm(dve, st, 2)
            dve_odd(dve, st)
            att1[1](dve, st)
            dve_residual(dve, "oo", 4, 2, 8)
            dve_norm(dve, st, 3)
            dve_router(dve, st)
            dve_moe(dve, st)
            dve_moe_out(dve)
            dve_norm(dve, st, 4)

        @block_.tensor
        def _(pe):
            pe_lam()
            pe_mod()
            pe_norm(0)
            pe_even_in()
            pe_colnorm("l2", l2_groups, 0)
            pe.wait_ge(caches_in, 32)
            att0[0]()
            pe_colnorm("obn", obn_groups, 8)
            pe_delta()
            pe_scan()
            pe_onorm()
            done(pe, "onrm", NT - 1)
            pe.wait_ge(cn_out, 12)
            pe_out("eo")
            pe_norm(1)
            pe_ffn()
            pe_norm(2)
            pe_odd_in()
            pe_odd_qkv()
            done(pe, "vv", NT)
            done(pe, "uqr", 7)
            att1[0]()
            done(pe, "att1", len(plan_c) - 1)
            pe_out("oo")
            pe_norm(3)
            pe_router()
            pe_moe()
            pe_moe_out()
            pe_norm(4)


def kernel(**inputs):
    import numpy as _np
    import concourse.bacc as _bacc
    from concourse.bass_utils import run_bass_kernel_spmd as _run

    v = {k: _np.asarray(a) for k, a in inputs.items()}

    def cut(w, ncols):
        k, n = w.shape
        return w.reshape(k // P, P, n // ncols, ncols).transpose(2, 1, 0, 3).reshape(n // ncols, P, -1)

    def col(w):
        return w.reshape(-1, P).T

    def rows(w):
        return _np.broadcast_to(w.reshape(1, -1), (P, w.size))

    def gate_up(w, nf):
        return w.reshape(KD, P, 2, nf, P).transpose(3, 1, 0, 2, 4).reshape(nf, P, KD * 256)

    i = _np.arange(P)
    ident = _np.eye(P)
    before = (i[:, None] <= i[None, :]).astype(_np.float64)
    masks = [before, before.T]
    levels = []
    for lv in range(LEVELS):
        w = 2 ** lv
        same = (i[:, None] // (2 * w)) == (i[None, :] // (2 * w))
        fwd = same & (i[None, :] % (2 * w) >= w) & (i[:, None] % (2 * w) < w)
        levels += [fwd, fwd.T]
    rot = _np.zeros((P, P))
    for b in range(0, P, 32):
        for j in range(16):
            rot[b + 16 + j, b + j] = -1.0
            rot[b + j, b + 16 + j] = 1.0
    table = _np.concatenate(
        [ident, _np.ones((P, P)), *masks, *[_np.where(m > 0, 0.0, NEG) for m in masks], *levels, rot,
         _np.broadcast_to(_np.arange(float(P)), (P, P)), _np.full((P, 1), EPS)], axis=1).astype(_np.float32)
    half = ROPE // 2
    inv = (_np.float32(10000.0) ** (-_np.arange(0, half, 2, dtype=_np.float32) / _np.float32(half))).astype(_np.float32)
    tokens = _np.arange(DEC_SEQ)
    ar = (tokens // 64).astype(_np.float32)[:, None] * inv[None, :]
    ac = (tokens % 64).astype(_np.float32)[:, None] * inv[None, :]
    ang = _np.concatenate([ar, ar, ac, ac, ar, ar, ac, ac], axis=1).astype(_np.float32).T
    cossin = _np.stack([_np.cos(ang), _np.sin(ang)], axis=1).astype(_np.float32)

    w_in = v["ev_w_in"][0]
    main = _np.concatenate([w_in[:, 0:2048], w_in[:, 2064:3600]], axis=1)
    od_in = _np.concatenate([v["od_w_in"][0], v["od_w_in"][0][:, 640:704]], axis=1)
    uq = v["od_w_uq"][0].reshape(384, HC, 192)
    ukv = v["od_w_ukv"][0].reshape(256, HC, 256)
    arrays = {
        "wsm": _np.concatenate(
            [col(w) for w in (v["norm_mix"][0], v["norm_ffn"][0], v["norm_mix"][1], v["norm_ffn"][1],
                              v["final_norm"], v["mod_b"])]
            + [v["ev_conv_w"][0].reshape(3, 12, P).transpose(2, 1, 0).reshape(P, 36),
               col(v["ev_onorm"][0]), col(v["ev_subln"][0]), col(v["od_q_norm"][0]), col(v["od_kv_norm"][0]),
               rows(v["ev_dt_bias"][0]), rows(v["ev_a_log"][0]),
               _np.stack([col(v["c_ctx"]), col(v["c"][0])], axis=2).reshape(P, 16)], axis=1),
        "cst": table,
        "lam": v["ev_lambda"][0].T,
        "cossin": cossin,
        "x": _np.concatenate([v["x_prompt"][0], v["x_sample"][0]], axis=0).T.reshape(KD, P, T)
             .transpose(1, 0, 2).reshape(P, KD * T),
        "ck": v["cache_diff_k"][0, 0].transpose(2, 0, 1),
        "cv": v["cache_diff_v"][0, 0].transpose(1, 0, 2).reshape(P, 512),
        "cckv": v["cache_mla_ckv"][0, 0].T.reshape(2, P, PAST).transpose(1, 0, 2),
        "ckr": _np.concatenate([v["cache_mla_krope"][0, 0].T] * 2, axis=0),
        "state": v["state_delta"][0, 0].transpose(2, 0, 1, 3).reshape(P, 1024),
        "w_mod": v["mod_w"].reshape(2, 4, 2, P, 6, D).transpose(0, 4, 1, 3, 2, 5).reshape(48, P, WB),
        "w_ev": cut(main, 256),
        "w_evg": cut(w_in[:, 2048:2064], 16),
        "w_eo": cut(v["ev_w_out"][0], 256),
        "w_gu": gate_up(v["ffn_w_gu"][0], FC),
        "w_dn": v["ffn_w_down"][0].reshape(2, LK, P, KD, P).transpose(3, 0, 2, 1, 4).reshape(16, P, LK * P),
        "w_oi": cut(od_in, 256),
        "w_uq": _np.concatenate([cut(uq[:, :, 0:128].reshape(384, 1024), 512),
                                 cut(uq[:, :, 128:192].reshape(384, 512), 512)], axis=0),
        "w_ukv": _np.stack([cut(ukv[:, :, 0:128].reshape(256, D), D)[0], cut(ukv[:, :, 128:].reshape(256, D), D)[0]]),
        "w_oo": cut(v["od_w_out"][0], 256),
        "w_rt": cut(v["moe_router"][0], NE),
        "w_mgu": _np.concatenate([gate_up(v["moe_w_gu"][0, e], EC) for e in range(NE)], axis=0),
        "w_mdn": v["moe_w_down"][0].reshape(NE, EC, P, 2, 512).transpose(0, 3, 2, 1, 4).reshape(2 * NE, P, EC * 512),
    }
    outs = {"y": (P, KD * T), "state": (P, 1024), "dk": (P, H, SEQ), "dv": (SEQ, 512),
            "ckv": (P, 2, SEQ), "kr": (ROPE, SEQ)}
    nc = _bacc.Bacc("TRN2", target_bir_lowering=False, num_devices=1, dynamic_dma_scratch_size=2048)
    arrays = {f"in_{n}": _np.ascontiguousarray(a) for n, a in arrays.items()}
    I = {n[3:]: nc.dram_tensor(n, a.shape, F32, kind="ExternalInput").ap() for n, a in arrays.items()}
    O = {n: nc.dram_tensor(f"out_{n}", s, F32, kind="ExternalOutput").ap() for n, s in outs.items()}
    program(nc, I, O)
    r = _run(nc, [arrays], core_ids=[0]).results[0]
    y = r["out_y"].reshape(P, KD, T).transpose(2, 1, 0).reshape(T, D)
    return (
        y[0:SEQ].reshape(1, SEQ, D), y[SEQ:T].reshape(1, DEC_SEQ, D),
        r["out_state"].reshape(P, 2, H, P).transpose(1, 2, 0, 3).reshape(1, 1, 2, H, P, P),
        r["out_dk"].transpose(1, 2, 0).reshape(1, 1, H, SEQ, P),
        r["out_dv"].reshape(SEQ, H, P).transpose(1, 0, 2).reshape(1, 1, H, SEQ, P),
        r["out_ckv"].transpose(2, 1, 0).reshape(1, 1, SEQ, 256),
        r["out_kr"].T.reshape(1, 1, SEQ, ROPE),
    )
```

```python
from contextlib import ExitStack

import numpy as np
import concourse.bass as bass
from concourse import mybir

ALU = mybir.AluOpType
ACT = mybir.ActivationFunctionType
AX = mybir.AxisListType
F32 = mybir.dt.float32
U32 = mybir.dt.uint32
I32 = mybir.dt.int32
F32R = mybir.dt.float32r

P = 128
D = 1024
KD = D // P
MODS = 2 * 6 * D // 256
MOD_FIRST = 2 * D // 256
SEQ, DEC_SEQ, PAST = 128, 512, 128
T = SEQ + DEC_SEQ
NT = T // P
HT = T // 2
TK = T + PAST
SEGS = ((0, SEQ, 0), (SEQ, T, 1))
H = 4
HC = 8
ROPE = 64
FC = 2816 // P
NE = 8
EC = 1408 // P
WS = 5
WB = 2048
LEVELS = 7
NEG = -30000.0
EPS = 1e-6
LAM_INIT = 0.8 - 0.6
IT = 2 * P
ITEMS = (2 * T + NE * (IT - 1)) // IT
LK = 11

C_ID, C_ONE, C_TRI, C_NEG, C_LVL, C_ROT = 0, 128, 256, 512, 768, 768 + LEVELS * 256
C_IOTA = C_ROT + 128
C_EPS = C_IOTA + IT
C_FOLD = C_EPS + 1
C_COLS = C_FOLD + 2
CST = -(-C_COLS // 8) * 8
assert C_ROT - C_NEG == WB
S_NORM, S_MODB, S_CONV = 0, 40, 136
S_ONORM, S_SUBLN, S_QN, S_KVN, S_DTB, S_ALOG, S_C = 172, 173, 174, 177, 179, 187, 195
S_COLS = S_C + 16


class Ring:

    def __init__(self, slots):
        self.slots, self.used, self.stages = slots, [0] * slots, {}

    def plan(self, stage, each, turns=1):
        per = [(each - s + self.slots - 1) // self.slots for s in range(self.slots)]
        self.stages[stage] = (list(self.used), per, each, turns)
        self.used = [u + turns * p for u, p in zip(self.used, per)]

    def use(self, stage, j, turn=0):
        before, per, _, _ = self.stages[stage]
        s = j % self.slots
        return s, turn * per[s] + before[s] + j // self.slots


class Steps:

    def __init__(self, eng, sem):
        self.eng, self.sem, self.n, self.off = eng, sem, 0, 0

    def did(self, ins):
        ins.then_inc(self.sem, 1)
        self.n += 1

    def sync(self):
        self.eng.wait_ge(self.sem, self.n + self.off)

    def then(self, ins):
        self.did(ins)
        self.sync()

    def loop(self, turn, each):
        self.start, self.off = self.n, turn * each

    def end(self, each, turns):
        assert self.n - self.start == each, (self.n - self.start, each)
        self.n, self.off = self.start + each * turns, 0


def spread(ap, axis, n):
    v = ap.unsqueeze(axis)
    shape = list(v.shape)
    shape[axis] = n
    return v.broadcast_to(shape)


def attention_items(heads):
    return [(h, t) for h in range(heads) for t in range(NT)]


def attention_plan(heads, streams):
    items = attention_items(heads)
    plan = []
    for i in range(len(items) + 2):
        if i < len(items):
            plan += [("scores", i, s) for s in range(streams)]
        if 1 <= i <= len(items):
            plan.append(("turn", i - 1, 0))
        if i >= 2:
            plan.append(("values", i - 2, 0))
    return plan


def program(nc, I, O):
    with ExitStack() as ctx:
        def sb(name, shape, dt=F32):
            return ctx.enter_context(nc.sbuf_tensor(name, shape, dt))

        def sem(name):
            return ctx.enter_context(nc.semaphore(name))

        with ExitStack() as plain:
            cst = plain.enter_context(nc.sbuf_tensor("cst", [P, CST], F32))
            wring = plain.enter_context(nc.sbuf_tensor("wring", [P, WS, WB], F32))
            hT = plain.enter_context(nc.sbuf_tensor("hT", [P, KD, T], F32))
            tmp = plain.enter_context(nc.sbuf_tensor("tmp", [P, KD * T], F32))
            arena = plain.enter_context(nc.sbuf_tensor("arena", [P, 25600], F32))
        cst_x = sb("cst_x", [P, CST], F32R)
        wring_x = sb("wring_x", [P, WS, WB], F32R)
        hT_x, tmp_x = sb("hT_x", [P, KD * T], F32R), sb("tmp_x", [P, KD * T], F32R)
        arena_x = sb("arena_x", [P, 25600 - 1024], F32R)
        wslot = [wring[:, s, :] for s in range(WS)] + [cst[:, C_NEG:C_ROT]]
        wslot_x = [wring_x[:, s, :] for s in range(WS)] + [cst_x[:, C_NEG:C_ROT]]
        expf = sb("expf", [P, 1024])
        xT = sb("xT", [P, KD * T])
        cossin = sb("cossin", [P, 2, DEC_SEQ])
        wsm = sb("wsm", [P, S_COLS])
        lam_in = sb("lam_in", [64, 4])
        lam_pr = sb("lam_pr", [64, 2])
        lam_e = sb("lam_e", [P, 2])
        neglam = sb("neglam", [P, 1])
        csilu = sb("csilu", [P, KD * 2])
        modcol = sb("modcol", [P, 12 * 16])
        modA = sb("modA", [P, 4, KD, 2])
        rstd = sb("rstd", [P, T])
        gates_sb = sb("gates_sb", [P, 5 * 16])
        dsm = sb("dsm", [P, 7, 2, NT, H])
        att = sb("att", [P, 16])
        gslot = att[:, 0:2]
        osd = sb("osd", [P, NT * H])
        item_expert = sb("item_expert", [1, 2 * ITEMS + 3], I32)
        slot_of = sb("slot_of", [P, 2, NT])
        tokw = dsm[:, 0, :, :, 0]
        inw = osd[:, 0:3 * NT].rearrange("p (a t) -> p a t", a=3)

        ps = ctx.enter_context(nc.psum_tensor("ps", [P, 4, 1024], F32))

        def pair(slot, n=HT):
            return ps[:, slot, :].rearrange("p (b n) -> p b n", b=2)[:, :, 0:n]

        ident, ones = cst[:, C_ID:C_ID + P], cst[:, C_ONE:C_ONE + P]
        tri = [cst[:, C_TRI + d * P:C_TRI + (d + 1) * P] for d in range(2)]
        rot = cst[:, C_ROT:C_ROT + P]
        iota = cst[:, C_IOTA:C_IOTA + IT]
        eps = cst[:, C_EPS:C_EPS + 1]
        cos, sin = cossin[:, 0, :], cossin[:, 1, :]

        def chunks(base, n, width):
            return arena[:, base:base + n * width].rearrange("p (n w) -> p n w", n=n)

        def exact(base, *shape):
            names = "abc"[:len(shape)]
            return arena_x[:, base:base + int(np.prod(shape))].rearrange(
                f"p ({' '.join(names)}) -> p {' '.join(names)}", **dict(zip(names, shape)))

        xc = xT[:, :].rearrange("p (k t) -> p k t", k=KD)
        tc = tmp[:, :].rearrange("p (k t) -> p k t", k=KD)
        qkvT, zT = chunks(0, 12, T), chunks(7680, 4, T)
        qT, kT, vB = chunks(10240, H, T), chunks(12800, H, TK), chunks(15872, NT + 1, 512)
        pB, aB = chunks(18944, 4, T), chunks(21504, 2, T)
        qkraw, raw, cv = chunks(22784, 2, T), arena[:, 24064:24064 + 643], arena[:, 24708:24708 + 641]
        rtmp = rstd[:, 0:DEC_SEQ]
        tok = chunks(10240, NT, 1024)
        DTs, Ais = chunks(15360, NT, 1024), chunks(20480, NT, 1024)
        oS = chunks(5120, NT, 512)
        dE, dM, dC, dD, dT1 = (tmp[:, i * 1024:(i + 1) * 1024] for i in range(5))
        Sst = [hT[:, :, :].rearrange("p k t -> p (k t)")[:, i * 1024:(i + 1) * 1024] for i in range(2)]
        crow = rstd[:, 0:KD * 32]
        mrow = hT[:, 3, P:T]
        fh = [v.rearrange("p (k t) -> p k t", k=KD) for v in (tmp_x[:, :], hT_x[:, :])]
        actT = chunks(0, FC, T)
        hhi, hlo = exact(0, NT, D), exact(5120, NT, D)
        whi = exact(10240, 3, WB)
        ahi, alo = exact(16384, EC, IT), exact(19200, EC, IT)
        sel, selT = exact(22016, NT, IT), exact(23296, 2, T)
        xg = hT_x[:, 0:4096].rearrange("p (q r n) -> p q r n", q=4, r=2)
        yhi, ylo = (tmp_x[:, i * 2048:(i + 1) * 2048].rearrange("p (m n) -> p m n", m=2) for i in range(2))
        act_x = exact(0, FC, T)
        act_lead = ([fh[i][:, k, :] for i in range(2) for k in range(KD)] + [exact(21504, 4, T)[:, k, :] for k in range(4)]
                    + [exact(FC * T, 2, T)[:, k, :] for k in range(2)])
        dhi = exact((FC + 2) * T, 4, LK * P)
        sg = arena[:, FC * T:(FC + 2) * T].rearrange("p (b t) -> p b t", b=2)
        fhi = exact((FC + 2) * T, 3, WB)
        qn, qr, kn, vC = chunks(0, HC, T), chunks(5120, 4, T), chunks(7680, HC, TK), chunks(13824, NT + 1, 1024)
        krT, ckv, cq = arena[:, 19968:19968 + TK], chunks(20736, 2, TK), chunks(22272, 3, T)
        krraw = arena[:, 24192:24192 + T]
        pC = tmp[:, 0:2 * T].rearrange("p (b t) -> p b t", b=2)
        aC = tmp[:, 2 * T:4 * T].rearrange("p (b t) -> p b t", b=2)
        qraw = tmp[:, 4 * T:6 * T].rearrange("p (b t) -> p b t", b=2)

        g_, beta, gcum, glast, eg, ed, el = (dsm[:, i, :, :, :] for i in range(7))

        w_full = [sem(f"w_full{s}") for s in range(WS + 1)]
        ps_full = [sem(f"ps_full{s}") for s in range(4)]
        ps_free = [sem(f"ps_free{s}") for s in range(4)]
        end_full = [sem(f"end_full{s}") for s in range(4)]
        end_free = [sem(f"end_free{s}") for s in range(4)]
        act_step = sem("act_step")
        dve_step, dve_end_step = sem("dve_step"), sem("dve_end_step")
        consts_in, x_in, caches_in, mla_caches_in, state_in = (
            sem(n) for n in ("consts_in", "x_in", "caches_in", "mla_caches_in", "state_in"))
        csilu_ready, crow_ready, lam_ready, modA_ready = (
            sem(n) for n in ("csilu_ready", "crow_ready", "lam_ready", "modA_ready"))
        sq_ready, hs_ready, h_ready = (sem(n) for n in ("sq_ready", "hs_ready", "h_ready"))
        conv_ready, qkv_ready, cn_sq, cn_out = (sem(n) for n in ("conv_ready", "qkv_ready", "cn_sq", "cn_out"))
        gate_in, gate_e, gate_l, g_ready = (sem(n) for n in ("gate_in", "gate_e", "gate_l", "g_ready"))
        decay_in, decay_out = sem("decay_in"), sem("decay_out")
        mx_ready, a_ready = sem("mx_ready"), sem("a_ready")
        gb_ready, e_in, e_out, c_ready, dt_ready = (
            sem(n) for n in ("gb_ready", "e_in", "e_out", "c_ready", "dt_ready"))
        s_zero, r_ready, vd_ready = sem("s_zero"), sem("r_ready"), sem("vd_ready")
        os_ready, od_ready, on_ready = sem("os_ready"), sem("od_ready"), sem("on_ready")
        top_ready, top_exp = sem("top_ready"), sem("top_exp")
        hhi_ready, oh_ready, items_ready, sel_ready, silu_ready = (
            sem(n) for n in ("hhi_ready", "oh_ready", "items_ready", "sel_ready", "silu_ready"))
        dhi_ready, dlo_ready, lead_ready, left_ready, left_pool_ready = (
            sem(n) for n in ("dhi_ready", "dlo_ready", "lead_ready", "left_ready", "left_pool_ready"))
        hlo_ready, fhi_ready, flo_ready = sem("hlo_ready"), sem("fhi_ready"), sem("flo_ready")
        ahi_ready = sem("ahi_ready")
        whi_ready, wlo_ready, wlo_pool_ready = sem("whi_ready"), sem("wlo_ready"), sem("wlo_pool_ready")
        kv_out, state_out, mla_out, y_out = (sem(n) for n in ("kv_out", "state_out", "mla_out", "y_out"))

        astep = Steps(nc.scalar, act_step)

        R = Ring(4)
        plan_b, plan_c = attention_plan(H, 2), attention_plan(HC, 1)
        rope_order = [("P", 0)] + [x for c in range(1, 8) for x in (("P", c), ("R", c - 1))] + [("R", 7)]
        uq_order = [("P", 0)] + [x for c in range(1, 4) for x in (("P", c), ("R", c - 1))] + [("R", 3)]
        TRI = ["tok", "gram", "grow", ("mA", 0), ("mA", 1), ("mB", 0), ("mB", 1), "C0"]
        for lv in range(1, LEVELS):
            TRI += [("T1", lv, 0), ("T1", lv, 1), ("mA", lv + 1)]
            for d in range(2):
                TRI += [("XT", lv, d)] + [("X", lv, d)] * (lv < LEVELS - 1) + [("mB", lv + 1)] * (d == 0)
        DL = len(TRI)
        SCAN = [(0, 0), (1, 4), (2, 3), (3, 2), (4, 1)]
        ITEM = (["gu0"] + [x for j in range(1, EC) for x in (f"gu{j}", f"tr{j - 1}")]
                + ["turnP0", "turnP1", "gs", f"tr{EC - 1}", "dn0"] + [f"ga{q}" for q in range(4)]
                + ["dn1"] + [f"sc{c}" for c in range(KD)])
        for stage, each, turns in (
                ("lam", 2, 1), ("mod", 4, MOD_FIRST // 2), ("norm0", 1, 1), ("qkv", 12, 1), ("z", 4, 1), ("gat", 1, 1),
                ("qk", 16, 1), ("l2", 8, 1), ("vb", NT, 1), ("att0", len(plan_b), 1), ("obn", H, 1),
                ("cum", 1, 1), ("tri", DL * NT, 1), ("scan", 5 * NT, 1), ("onrm", NT, 1), ("eo", 4, 2),
                ("norm1", 1, 1), ("fgu", 2 * EC, 2), ("fdn", 2, 4),
                ("norm2", 1, 1), ("oi", 7, 1), ("mlan", 2, 1), ("uqn", HC, 1), ("uqr", 8, 1), ("kn", HC, 1),
                ("vv", NT + 1, 1), ("att1", len(plan_c), 1), ("oo", 4, 2),
                ("norm3", 1, 1), ("rt", 1, 1), ("ht", NT, 1), ("cnt", 1, 1), ("moe0", 4, 1),
                ("moe", len(ITEM), ITEMS)):
            R.plan(stage, each, turns)
        R_end = Ring(4)
        R_end.plan("norm4", 1)

        def slot_use(stage, j, turn=0):
            if stage in R_end.stages:
                return *R_end.use(stage, j, turn), end_full, end_free
            return *R.use(stage, j, turn), ps_full, ps_free

        def filled(last, stage, j, turn=0):
            s, _, written, _ = slot_use(stage, j, turn)
            last.then_inc(written[s], 1)

        def freed(last, stage, j, turn=0):
            s, _, _, free = slot_use(stage, j, turn)
            last.then_inc(free[s], 1)

        def take(stage, j, turn=0):
            s, n, _, free = slot_use(stage, j, turn)
            if not (isinstance(n, int) and n == 0):
                nc.tensor.wait_ge(free[s], n)
            return s

        def full(eng, stage, j, turn=0):
            s, n, written, _ = slot_use(stage, j, turn)
            eng.wait_ge(written[s], n + 1)
            return s

        def done(eng, stage, j, turn=0):
            s, n, _, free = slot_use(stage, j, turn)
            eng.wait_ge(free[s], n + 1)

        W = Ring(WS)
        loads = {
            "mod": (I["w_mod"][0:MOD_FIRST], WB, 2, MOD_FIRST // 2, lambda j: ("mod", j)),
            "qkv": (I["w_ev"][0:6], WB, 6, 1, lambda j: ("qkv", 2 * j + 1)),
            "z": (I["w_ev"][6:8], WB, 2, 1, lambda j: ("z", 2 * j + 1)),
            "gat": (I["w_evg"], KD * 16, 1, 1, lambda j: ("gat", 0)),
            "qk": (I["w_ev"][8:12], WB, 4, 1, lambda j: ("qk", rope_order.index(("P", 2 * j + 1)))),
            "vb": (I["w_ev"][12:14], WB, 2, 1, lambda j: ("vb", NT - 1)),
            "mod2": (I["w_mod"][MOD_FIRST:MODS], WB, MODS - MOD_FIRST, 1,
                     lambda j: ("tri", DL * (j // 8) + TRI.index(("mA", j % 8)))),
            "eo": (I["w_eo"], WB, 2, 2, lambda j: ("eo", 2 * j + 1)),
            "fgu": (I["w_gu"], WB, EC, 2, lambda j: ("fgu", 2 * j + 1)),
            "fdn": (I["w_dn"], LK * P, 4, 4, lambda j: ("fdn", j // 2)),
            "oi": (I["w_oi"], WB, 3, 1, lambda j: ("oi", 2 * j + 1)),
            "uqn": (I["w_uq"][0:2], 1536, 2, 1, lambda j: ("uqn", 4 * j + 3)),
            "uqr": (I["w_uq"][2:3], 1536, 1, 1, lambda j: ("uqr", uq_order.index(("P", 3)))),
            "kn": (I["w_ukv"][0:1], WB, 1, 1, lambda j: ("kn", HC - 1)),
            "vv": (I["w_ukv"][1:2], WB, 1, 1, lambda j: ("vv", NT)),
            "oo": (I["w_oo"], WB, 2, 2, lambda j: ("oo", 2 * j + 1)),
            "rt": (I["w_rt"], 64, 1, 1, lambda j: ("rt", 0)),
            "moe": (None, WB, EC + 6, ITEMS, lambda j: ("moe", ITEM.index(f"gu{j}" if j < EC else f"dn{(j - EC) // 3}"))),
        }
        history = [[] for _ in range(WS + 1)]
        for stage, (_, _, each, turns, _) in loads.items():
            if stage == "moe":
                W.slots, W.used = WS + 1, W.used + [0]
            W.plan(stage, each, turns)
            for turn in range(turns):
                for j in range(each):
                    history[j % W.slots].append((stage, j, turn))

        def wslots(stage):
            return WS + (stage == "moe")

        def wuse(stage, j, turn=0):
            before, per, _, _ = W.stages[stage]
            s = j % wslots(stage)
            return s, turn * per[s] + before[s] + j // wslots(stage)

        def block(stage, j, turn=0):
            s, n = wuse(stage, j, turn)
            nc.tensor.wait_ge(w_full[s], 16 * (n + 1))
            return wring[:, s, :]

        def load(sync, stage, j, turn=0, expert=0):
            dram, size, each, _, _ = loads[stage]
            s, n = wuse(stage, j, turn)
            if isinstance(turn, int):
                held = history[s][n - 1] if n else None
            elif j >= wslots(stage):
                held = (stage, j - wslots(stage), turn)
            else:
                held = (stage, max(i for i in range(each) if i % wslots(stage) == s), turn - 1)
            if held:
                pstage, pj = loads[held[0]][4](held[1])
                full(sync, pstage, pj, held[2])
            if stage == "moe":
                if j < EC:
                    src = I["w_mgu"][bass.ds(expert * EC + j, 1), :, :]
                else:
                    half, part = (j - EC) // 3, (j - EC) % 3
                    size = 4 * 512 if part < 2 else 3 * 512
                    src = I["w_mdn"][bass.ds(expert * 2 + half, 1), :, part * WB:part * WB + size]
            else:
                src = dram[bass.ds(turn * each + j, 1), :, 0:size]
            sync.dma_start(wslot[s][:, 0:size], src.rearrange("a p n -> p (a n)")).then_inc(w_full[s], 16)

        def load_stage(sync, stage):
            each, turns = loads[stage][2:4]
            ahead = min(WS, each)
            for j in range(ahead):
                load(sync, stage, j, 0)
            if turns > 1:
                with sync.Fori(0, turns - 1) as turn:
                    for j in range(ahead, each):
                        load(sync, stage, j, turn)
                    for j in range(ahead):
                        load(sync, stage, j, turn + 1)
            for j in range(ahead, each):
                load(sync, stage, j, turns - 1)

        def items_of(eng):
            eng.wait_ge(items_ready, 1)
            return eng.value_load(item_expert[0:1, ITEMS + 1:ITEMS + 2], min_val=2 * T // IT, max_val=ITEMS)

        def load_items(sync):
            n = items_of(sync)
            e = expert_of(sync, 0)
            for j in range(WS + 1):
                load(sync, "moe", j, 0, e)
            with sync.Fori(0, ITEMS) as turn:
                with sync.If(turn < n):
                    e = expert_of(sync, turn)
                    for j in range(WS + 1, EC + 6):
                        load(sync, "moe", j, turn, e)
                with sync.If(turn + 1 < n):
                    e = expert_of(sync, turn + 1)
                    for j in range(WS + 1):
                        load(sync, "moe", j, turn + 1, e)

        def expert_of(sync, item):
            return sync.value_load(item_expert[0:1, bass.ds(item, 1)], min_val=0, max_val=NE - 1)

        def mm(out, lhsT, rhs, first, last):
            return nc.tensor.matmul(out, lhsT, rhs, start=first, stop=last)

        def pe_linear(stage, j, turn, weights, source, n=HT, h_base=None):
            s = take(stage, j, turn)
            out = pair(s, n)
            nk = len(weights)
            for half in range(2):
                for k in range(nk):
                    if half == 0 and h_base is not None:
                        nc.tensor.wait_ge(h_ready, h_base + k + 1)
                    last = mm(out[:, half, :], weights[k], source(k, half * n, half * n + n), k == 0, k == nk - 1)
            last.then_inc(ps_full[s], 1)
            return s

        def from_h(k, a, b):
            return hT[:, k, a:b]

        def cols(w, nk, width, c):
            return [w[:, k * width + c * P:k * width + (c + 1) * P] for k in range(nk)]

        def pe_lam():
            nc.tensor.wait_ge(consts_in, 16 * 4)
            nc.tensor.wait_ge(lam_ready, 1)
            for i in range(2):
                s = take("lam", i)
                mm(ps[:, s, 0:1], cst[0:64, C_ONE:C_ONE + P], lam_pr[:, i:i + 1], True, True).then_inc(ps_full[s], 1)

        def pe_mod_rows(w, s):
            for r in range(2):
                for g in range(4):
                    k = 4 * r + g
                    last = mm(ps[32 * g:32 * g + 32, s, 0:256], crow[:, k * 32:(k + 1) * 32],
                              w[:, k * 256:(k + 1) * 256], r == 0, r == 1)
            return last

        def pe_mod_cols(buf, s):
            for j in range(2):
                last = mm(ps[:, s, 2 * j:2 * j + 2], mrow[:, buf * 256 + j * P:buf * 256 + (j + 1) * P],
                          cst[:, C_FOLD:C_FOLD + 2], True, True)
            return last

        def dve_mod_cols(s, n):
            return nc.vector.tensor_tensor(
                modcol[:, bass.ds(n * 4, 4)].rearrange("p (k c) -> p k c", c=2),
                ps[:, s, 0:4].rearrange("p (k c) -> p k c", c=2),
                spread(wsm[:, bass.ds(n * 2 + S_MODB, 2)], 2, 2), ALU.add)

        def pe_mod():
            nc.tensor.wait_ge(crow_ready, 1)
            with nc.tensor.Fori(0, MOD_FIRST // 2) as i:
                for j in range(2):
                    w, s = block("mod", j, i), take("mod", j, i)
                    filled(pe_mod_rows(w, s), "mod", j, i)
                for j in range(2):
                    done(nc.tensor, "mod", j, i)
                    s = take("mod", 2 + j, i)
                    filled(pe_mod_cols(j, s), "mod", 2 + j, i)

        def dve_crow(dve, st):
            st.then(nc.vector.memset(crow, 0.0))
            nc.vector.tensor_copy(crow.rearrange("p (k c) -> p k c", c=32)[:, :, 0:2],
                                  csilu[:, :].rearrange("p (k c) -> p k c", c=2)).then_inc(crow_ready, 1)

        def dve_modA(norms):
            for n in norms:
                m = (1, 4, 7, 10)[n]
                nc.vector.scalar_tensor_tensor(
                    modA[:, n, :, :], modcol[:, m * 16:m * 16 + 16].rearrange("p (k c) -> p k c", c=2), 1.0,
                    spread(wsm[:, S_NORM + n * 8:S_NORM + n * 8 + 8], 2, 2), ALU.add, ALU.mult
                    ).then_inc(modA_ready, 1)

        def dve_mod(dve, st):
            dve.wait_ge(csilu_ready, 1)
            dve_crow(dve, st)
            with dve.Fori(0, MOD_FIRST // 2) as i:
                for j in range(2):
                    s = full(dve, "mod", j, i)
                    freed(nc.vector.tensor_copy(mrow[:, j * 256:(j + 1) * 256], ps[:, s, 0:256]), "mod", j, i)
                for j in range(2):
                    s = full(dve, "mod", 2 + j, i)
                    freed(dve_mod_cols(s, i * 2 + j), "mod", 2 + j, i)
            done(dve, "mod", 3, MOD_FIRST // 2 - 1)
            dve_modA([0])

        def act_norm(act, n, x_done, meanwhile=lambda: None):
            for k in range(KD):
                x_done(act, k)
                nc.scalar.activation(tc[:, k, :], xc[:, k, :], ACT.Square).then_inc(sq_ready, 1)
            meanwhile()
            s = full(act, f"norm{n}", 0)
            astep.then(nc.scalar.activation(rstd[:, :].rearrange("p (b n) -> p b n", b=2), pair(s), ACT.Ln,
                                            bias=eps, scale=1.0 / D))
            freed(nc.scalar.activation(rstd[:, :], rstd[:, :], ACT.Exp, scale=-0.5), f"norm{n}", 0)
            if n < 4:
                m = (0, 3, 6, 9)[n]
                act.wait_ge(modA_ready, n + 1)
                for k in range(KD):
                    act.wait_ge(hs_ready, 8 * n + k + 1)
                    if n == 1:
                        for a, b, c in SEGS:
                            nc.scalar.activation(fh[0][:, k, a:b], hT[:, k, a:b], ACT.Identity,
                                                 bias=modcol[:, m * 16 + 2 * k + c:m * 16 + 2 * k + c + 1])
                    for a, b, c in SEGS:
                        last = nc.scalar.activation(hT[:, k, a:b], hT[:, k, a:b], ACT.Identity,
                                                    bias=modcol[:, m * 16 + 2 * k + c:m * 16 + 2 * k + c + 1])
                    last.then_inc(h_ready, 1)

        def pe_norm(n):
            s = take(f"norm{n}", 0)
            for k in range(KD):
                nc.tensor.wait_ge(sq_ready, 8 * n + k + 1)
                for half in range(2):
                    last = nc.tensor.matmul(pair(s)[:, half, :], ones, tc[:, k, half * HT:(half + 1) * HT],
                                            start=(k == 0), stop=(k == KD - 1))
            filled(last, f"norm{n}", 0)

        def dve_norm(dve, st, n):
            done(dve, f"norm{n}", 0)
            if n < 4:
                dve.wait_ge(modA_ready, n + 1)
            for k in range(KD):
                for a, b, c in (SEGS if n < 4 else ((0, T, 0),)):
                    A = modA[:, n, k, c:c + 1] if n < 4 else wsm[:, S_NORM + 32 + k:S_NORM + 33 + k]
                    last = nc.vector.scalar_tensor_tensor(hT[:, k, a:b], xc[:, k, a:b], A, rstd[:, a:b],
                                                          ALU.mult, ALU.mult)
                last.then_inc(hs_ready, 1)

        def act_colsquares(groups):
            i = 0
            for group in groups:
                for src, _, _ in group:
                    nc.scalar.activation(tc[:, i, :], src, ACT.Square).then_inc(cn_sq, 1)
                    i += 1

        def act_colnorm(act, stage, groups, base, scale, squared=False):
            if not squared:
                act_colsquares(groups)
            first = [sum(len(group) for group in groups[:g]) for g in range(len(groups))]
            for four in range(0, len(groups), 4):
                gs = range(four, min(four + 4, len(groups)))
                for g in gs:
                    s = full(act, stage, g)
                    last = nc.scalar.activation(tc[:, first[g], :].rearrange("p (b n) -> p b n", b=2), pair(s), ACT.Ln,
                                                bias=eps, scale=scale[g])
                    if g == gs[-1]:
                        astep.then(last)
                for g in gs:
                    s, _ = R.use(stage, g)
                    nc.scalar.activation(tc[:, first[g], :], tc[:, first[g], :], ACT.Exp, scale=-0.5
                                         ).then_inc(ps_free[s], 1)

        def pe_colnorm(stage, groups, base):
            i = 0
            for g, group in enumerate(groups):
                s = take(stage, g)
                nc.tensor.wait_ge(cn_sq, base + i + len(group))
                for half in range(2):
                    for c in range(len(group)):
                        last = mm(pair(s)[:, half, :], ones, tc[:, i + c, half * HT:(half + 1) * HT],
                                  c == 0, c == len(group) - 1)
                last.then_inc(ps_full[s], 1)
                i += len(group)

        def dve_colnorm(dve, st, stage, groups):
            i = 0
            for g, group in enumerate(groups):
                done(dve, stage, g)
                for src, dst, w in group:
                    last = nc.vector.scalar_tensor_tensor(dst, src, w, tc[:, i, :], ALU.mult, ALU.mult)
                last.then_inc(cn_out, 1)
                i += len(group)

        l2_groups = [[(qkvT[:, c, :], qkvT[:, c, :], P ** -0.5 if c < H else 1.0)] for c in range(8)]
        obn_groups = [[(hT[:, H + h, :], hT[:, H + h, :], wsm[:, S_SUBLN:S_SUBLN + 1])] for h in range(H)]
        mla_groups = [[(cq[:, c, :], cq[:, c, :], wsm[:, S_QN + c:S_QN + c + 1]) for c in range(3)],
                      [(ckv[:, c, 0:T], ckv[:, c, 0:T], wsm[:, S_KVN + c:S_KVN + c + 1]) for c in range(2)]]

        def pe_even_in():
            for c in range(12):
                if c % 2 == 0:
                    w = block("qkv", c // 2)
                pe_linear("qkv", c, 0, cols(w, KD, 256, c % 2), from_h, h_base=None if c else 0)
            for c in range(4):
                if c % 2 == 0:
                    w = block("z", c // 2)
                pe_linear("z", c, 0, cols(w, KD, 256, c % 2), from_h)
            w, s = block("gat", 0), take("gat", 0)
            for t in range(NT):
                for k in range(KD):
                    last = mm(ps[:, s, t * 16:(t + 1) * 16], hT[:, k, t * P:(t + 1) * P], w[:, k * 16:(k + 1) * 16],
                              k == 0, k == KD - 1)
            last.then_inc(ps_full[s], 1)
            for j, (what, c) in enumerate(rope_order):
                if what == "P":
                    if c % 2 == 0:
                        w = block("qk", c // 2)
                    pe_linear("qk", j, 0, cols(w, KD, 256, c % 2), from_h)
                else:
                    done(nc.tensor, "qk", rope_order.index(("P", c)))
                    s = take("qk", j)
                    mm(ps[:, s, 0:DEC_SEQ], rot, qkraw[:, c % 2, SEQ:T], True, True).then_inc(ps_full[s], 1)
            pe_colnorm("l2", l2_groups, 0)
            w = [block("vb", 0), block("vb", 1)]
            for t in range(NT):
                s = take("vb", t)
                for b in range(2):
                    for k in range(KD):
                        last = mm(ps[:, s, b * 256:(b + 1) * 256], hT[:, k, t * P:(t + 1) * P],
                                  w[b][:, k * 256:(k + 1) * 256], k == 0, k == KD - 1)
                last.then_inc(ps_full[s], 1)

        def act_even_in(act):
            for c in range(12):
                s = full(act, "qkv", c)
                nc.scalar.activation(raw[:, 1:1 + SEQ], ps[:, s, 0:SEQ], ACT.Copy)
                nc.scalar.activation(raw[:, 2 + SEQ:2 + HT], ps[:, s, SEQ:HT], ACT.Copy)
                nc.scalar.activation(raw[:, 2 + HT:2 + T], ps[:, s, 512:512 + HT], ACT.Copy).then_inc(ps_free[s], 1)
                act.wait_ge(conv_ready, c + 1)
                nc.scalar.activation(qkvT[:, c, 0:SEQ], cv[:, 0:SEQ], ACT.Silu)
                nc.scalar.activation(qkvT[:, c, SEQ:T], cv[:, SEQ + 1:T + 1], ACT.Silu).then_inc(qkv_ready, 1)
            for c in range(4):
                s = full(act, "z", c)
                nc.scalar.activation(zT[:, c, :].rearrange("p (b n) -> p b n", b=2), pair(s), ACT.Silu
                                     ).then_inc(ps_free[s], 1)
            act.wait_ge(gate_in, 1)
            gr = gates_sb[:, :].rearrange("p (t c) -> p t c", c=16)
            nc.scalar.activation(gr[:, :, 8:16], gr[:, :, 8:16], ACT.Exp, scale=-1.0)
            nc.scalar.activation(dsm[:, 2, :, :, :].rearrange("p a t h -> p (a t h)"),
                                 dsm[:, 2, :, :, :].rearrange("p a t h -> p (a t h)"), ACT.Exp, scale=-1.0)
            nc.scalar.activation(wsm[:, S_ALOG:S_ALOG + 8], wsm[:, S_ALOG:S_ALOG + 8], ACT.Exp).then_inc(gate_e, 1)
            act.wait_ge(gate_e, 1)
            nc.scalar.activation(dsm[:, 2, :, :, :].rearrange("p a t h -> p (a t h)"),
                                 dsm[:, 2, :, :, :].rearrange("p a t h -> p (a t h)"), ACT.Ln,
                                 bias=ones[:, 0:1]).then_inc(gate_l, 1)
            act.wait_ge(qkv_ready, 12)
            act_colsquares(l2_groups)
            for c in range(8):
                j = rope_order.index(("P", c))
                if c >= 2:
                    done(act, "qk", rope_order.index(("R", c - 2)))
                s = full(act, "qk", j)
                nc.scalar.activation(qkraw[:, c % 2, :].rearrange("p (b n) -> p b n", b=2), pair(s), ACT.Copy,
                                     scale=64 ** -0.5 if c < H else 1.0).then_inc(ps_free[s], 1)

        def dve_rope(st, raw_in, dst, s, prompt=True):
            nc.vector.tensor_copy(dst[:, 0:SEQ], raw_in[:, 0:SEQ])
            nc.vector.tensor_tensor(dst[:, SEQ:T], raw_in[:, SEQ:T], cos, ALU.mult)
            st.then(nc.vector.tensor_tensor(rtmp, ps[:, s, 0:DEC_SEQ], sin, ALU.mult))
            nc.vector.tensor_tensor(dst[:, SEQ:T], dst[:, SEQ:T], rtmp, ALU.add).then_inc(ps_free[s], 1)

        def dve_even_in(dve, st):
            for c in range(12):
                done(dve, "qkv", c)
                if c:
                    dve.wait_ge(qkv_ready, c)
                cw = wsm[:, S_CONV + 3 * c:S_CONV + 3 * c + 3]
                st.then(nc.vector.tensor_scalar(cv, raw[:, 0:641], cw[:, 0:1], None, ALU.mult))
                st.then(nc.vector.scalar_tensor_tensor(cv, raw[:, 1:642], cw[:, 1:2], cv, ALU.mult, ALU.add))
                nc.vector.scalar_tensor_tensor(cv, raw[:, 2:643], cw[:, 2:3], cv, ALU.mult, ALU.add
                                               ).then_inc(conv_ready, 1)
            s = full(dve, "gat", 0)
            nc.vector.tensor_copy(gates_sb[:, :], ps[:, s, 0:80]).then_inc(ps_free[s], 1)
            done(dve, "gat", 0)
            gr = gates_sb[:, :].rearrange("p (t d h) -> p t d h", d=4, h=H)
            sp = dsm[:, 2, :, :, :]
            for d in range(2):
                last = nc.vector.tensor_tensor(g_[:, d, :, :], gr[:, :, d, :],
                                               spread(wsm[:, S_DTB + d * H:S_DTB + (d + 1) * H], 1, NT), ALU.add)
            st.then(last)
            st.then(nc.vector.tensor_scalar(sp, g_, -1.0, None, ALU.mult))
            nc.vector.tensor_tensor(sp, sp, g_, ALU.max).then_inc(gate_in, 1)
            st.then(nc.vector.tensor_scalar(g_, g_, 0.0, None, ALU.max))
            dve.wait_ge(gate_e, 1)
            dve.wait_ge(gate_l, 1)
            st.then(nc.vector.tensor_tensor(g_, g_, sp, ALU.add))
            for d in range(2):
                nc.vector.scalar_tensor_tensor(g_[:, d, :, :], g_[:, d, :, :], -1.0,
                                               spread(wsm[:, S_ALOG + d * H:S_ALOG + (d + 1) * H], 1, NT),
                                               ALU.mult, ALU.mult)
                last = nc.vector.tensor_scalar(beta[:, d, :, :], gr[:, :, 2 + d, :], 1.0, None, ALU.add)
            st.then(last)
            nc.vector.reciprocal(beta, beta).then_inc(g_ready, 1)
            for c in range(8):
                s = full(dve, "qk", rope_order.index(("R", c)))
                if c:
                    done(dve, "qk", rope_order.index(("R", c - 1)))
                dve_rope(st, qkraw[:, c % 2, :], qT[:, c, :] if c < H else kT[:, c - H, 0:T], s)
            dve_colnorm(dve, st, "l2", l2_groups)
            for t in range(NT):
                s = full(dve, "vb", t)
                nc.vector.tensor_copy(vB[:, t, :], ps[:, s, 0:512]).then_inc(ps_free[s], 1)

        def attention(heads, streams, stage, order, scores, values, probs, turned, item_base, stat):
            items = attention_items(heads)
            at = {x: j for j, x in enumerate(order)}
            nstat = 3 * streams

            def cells(i):
                return att[:, (i % 2) * 8:(i % 2) * 8 + 8]

            def pe():
                for j, (what, i, st_) in enumerate(order):
                    h, t = items[i]
                    blocks = (0,) if t == 0 else tuple(range(1, NT + 1))
                    if what == "scores":
                        s = take(stage, j)
                        if t == 0:
                            terms = scores(h, t, st_, 0, P)
                            for n, (q, k) in enumerate(terms):
                                last = mm(ps[:, s, 0:P], q, k, n == 0, n == len(terms) - 1)
                        else:
                            for half in range(2):
                                terms = scores(h, t, st_, P + half * HT, P + (half + 1) * HT)
                                for n, (q, k) in enumerate(terms):
                                    last = mm(pair(s)[:, half, :], q, k, n == 0, n == len(terms) - 1)
                    elif what == "turn":
                        nc.tensor.wait_ge(a_ready, item_base + i + 1)
                        s = take(stage, j)
                        for n in range(len(blocks)):
                            last = nc.tensor.transpose(ps[:, s, n * P:(n + 1) * P],
                                                       probs(i, 0)[:, n * P:(n + 1) * P], ident)
                    else:
                        done(nc.tensor, stage, at[("turn", i, 0)])
                        s = take(stage, j)
                        for n, b in enumerate(blocks):
                            last = mm(ps[:, s, 0:P], values(h, b), turned(i)[:, n * P:(n + 1) * P],
                                      n == 0, n == len(blocks) - 1)
                    last.then_inc(ps_full[s], 1)

            def view(i, ap, s):
                if items[i][1] == 0:
                    return ps[:, s, 0:P], ap[:, 0:P]
                return pair(s), ap.rearrange("p (b n) -> p b n", b=2)

            def dve(eng, st):
                for i in range(len(items) + 2):
                    if i < len(items):
                        h, t = items[i]
                        for st_ in range(streams):
                            s = full(eng, stage, at[("scores", i, st_)])
                            src, _ = view(i, probs(i, st_), s)
                            nc.vector.tensor_reduce(cells(i)[:, st_:st_ + 1], src, AX.X if t == 0 else AX.XY,
                                                    ALU.max, negate=True).then_inc(mx_ready, 1)
                        for st_ in range(streams):
                            done(eng, stage, at[("scores", i, st_)])
                        w = P if t == 0 else T
                        sums, inv = cells(i)[:, 2:2 + streams], cells(i)[:, 4:4 + streams]
                        st.then(nc.vector.reciprocal(inv, sums))
                        if streams == 1:
                            nc.vector.tensor_scalar(probs(i, 0)[:, 0:w], probs(i, 0)[:, 0:w], inv[:, 0:1], None,
                                                    ALU.mult).then_inc(a_ready, 1)
                        else:
                            nc.vector.tensor_scalar(probs(i, 0)[:, 0:w], probs(i, 0)[:, 0:w], inv[:, 0:1], None,
                                                    ALU.mult)
                            st.then(nc.vector.tensor_scalar(inv[:, 1:2], inv[:, 1:2], neglam[:, 0:1], None, ALU.mult))
                            nc.vector.scalar_tensor_tensor(probs(i, 0)[:, 0:w], probs(i, 1)[:, 0:w], inv[:, 1:2],
                                                           probs(i, 0)[:, 0:w], ALU.mult, ALU.add
                                                           ).then_inc(a_ready, 1)
                    if i >= 2:
                        h, t = items[i - 2]
                        s = full(eng, stage, at[("values", i - 2, 0)])
                        nc.vector.tensor_copy(hT[:, stat + h, t * P:(t + 1) * P], ps[:, s, 0:P]
                                              ).then_inc(ps_free[s], 1)

            def act(eng):
                for i in range(len(items) + 1):
                    if i < len(items):
                        for st_ in range(streams):
                            eng.wait_ge(mx_ready, (item_base * 2 if streams == 1 else 0) + i * streams + st_ + 1)
                            s, _ = R.use(stage, at[("scores", i, st_)])
                            src, dst = view(i, probs(i, st_), s)
                            nc.scalar.activation(dst, src, ACT.Exp, bias=cells(i)[:, st_:st_ + 1],
                                                 accum_out=cells(i)[:, 2 + st_:3 + st_]).then_inc(ps_free[s], 1)
                    if i >= 1:
                        s = full(eng, stage, at[("turn", i - 1, 0)])
                        w = P if items[i - 1][1] == 0 else T
                        nc.scalar.activation(turned(i - 1)[:, 0:w], ps[:, s, 0:w], ACT.Copy).then_inc(ps_free[s], 1)

            return pe, dve, act

        def diff_scores(h, t, st_, a, b):
            r = slice(st_ * ROPE, (st_ + 1) * ROPE)
            return [(qT[r, h, t * P:(t + 1) * P], kT[r, h, a:b])]

        def mla_scores(h, t, st_, a, b):
            r = slice((h % 2) * ROPE, (h % 2 + 1) * ROPE)
            return [(qn[:, h, t * P:(t + 1) * P], kn[:, h, a:b]), (qr[r, h // 2, t * P:(t + 1) * P], krT[r, a:b])]

        att0 = attention(H, 2, "att0", plan_b, diff_scores, lambda h, b: vB[:, b, h * P:(h + 1) * P],
                         lambda i, s: pB[:, (i % 2) * 2 + s, :], lambda i: aB[:, i % 2, :], 0, H)
        att1 = attention(HC, 1, "att1", plan_c, mla_scores, lambda h, b: vC[:, b, h * P:(h + 1) * P],
                         lambda i, s: pC[:, i % 2, :], lambda i: aC[:, i % 2, :], H * NT, 0)

        def quad(ap):
            return ap.rearrange("p (d h c) -> p d h c", d=2, h=H)

        def per_head(ap):
            return ap.rearrange("p (h c) -> p h c", h=H)

        gb = dT1

        def prod(t, what):
            return DL * t + TRI.index(what)

        def heads_of(d):
            return [slice((d * H + h) * P, (d * H + h + 1) * P) for h in range(H)]

        def bank(s):
            return [ps[:, s, h * P:(h + 1) * P] for h in range(H)]

        def pool_delta(pool):
            for t in range(NT):
                if t == 0:
                    pool.wait_ge(g_ready, 1)
                    full(pool, "obn", H - 1)
                    pool.wait_ge(cn_out, 8 + H)
                else:
                    full(pool, "tri", prod(t - 1, ("XT", LEVELS - 1, 1)))
                for d in range(2):
                    last = nc.gpsimd.tensor_copy(quad(gb)[:, d, :, :], spread(g_[:, d, t, :], 2, P))
                last.then_inc(gb_ready, 1)
                done(pool, "tri", prod(t, "gram"))
                for lv in range(LEVELS):
                    if lv == 1:
                        pool.wait_ge(dt_ready, t + 1)
                        full(pool, "tri", prod(t, "C0"))
                    for d in range(2):
                        if lv > 1:
                            full(pool, "tri", prod(t, ("T1", lv - 1, d)))
                        mask = cst[:, C_LVL + (lv * 2 + d) * P:C_LVL + (lv * 2 + d + 1) * P]
                        nc.gpsimd.tensor_tensor(quad(dC)[:, d, :, :], quad(dM)[:, d, :, :],
                                                spread(mask, 1, H), ALU.mult).then_inc(c_ready, 1)

        def pe_delta():
            nc.tensor.wait_ge(g_ready, 1)
            nc.tensor.wait_ge(cn_out, 8)
            s = take("cum", 0)
            for d in range(2):
                mm(ps[:, s, d * 20:d * 20 + 20], tri[d], g_[:, d, :, :].rearrange("p t h -> p (t h)"), True, True)
            mm(ps[:, s, 40:80], ones, g_.rearrange("p d t h -> p (d t h)"), True, True).then_inc(ps_full[s], 1)
            for t in range(NT):
                a, b = t * P, (t + 1) * P
                s = take("tri", prod(t, "tok"))
                for h in range(H):
                    nc.tensor.transpose(ps[:, s, h * P:(h + 1) * P], qkvT[:, H + h, a:b], ident)
                for h in range(H):
                    last = nc.tensor.transpose(ps[:, s, 512 + h * P:512 + (h + 1) * P], qkvT[:, 2 * H + h, a:b], ident)
                last.then_inc(ps_full[s], 1)
                s = take("tri", prod(t, "gram"))
                for h in range(H):
                    mm(ps[:, s, h * P:(h + 1) * P], qkvT[:, H + h, a:b], qkvT[:, H + h, a:b], True, True)
                for h in range(H):
                    last = mm(ps[:, s, 512 + h * P:512 + (h + 1) * P], qkvT[:, H + h, a:b], qkvT[:, h, a:b], True, True)
                last.then_inc(ps_full[s], 1)
                nc.tensor.wait_ge(gb_ready, t + 1)
                s = take("tri", prod(t, "grow"))
                for i in range(2 * H):
                    last = mm(ps[:, s, i * P:(i + 1) * P], gb[:, i * P:(i + 1) * P], tri[i // H], True, True)
                last.then_inc(ps_full[s], 1)
                for b in range(2):
                    pe_mod_a(t, b)
                for b in range(2):
                    pe_mod_b(t, b)
                nc.tensor.wait_ge(c_ready, 2 * LEVELS * t + 2)
                s = take("tri", prod(t, "C0"))
                for i in range(2 * H):
                    last = nc.tensor.transpose(ps[:, s, i * P:(i + 1) * P], dC[:, i * P:(i + 1) * P], ident)
                last.then_inc(ps_full[s], 1)
                nc.tensor.wait_ge(dt_ready, t + 1)
                for lv in range(1, LEVELS):
                    for d in range(2):
                        nc.tensor.wait_ge(c_ready, 2 * (LEVELS * t + lv) + d + 1)
                        done(nc.tensor, "tri", prod(t, "C0" if lv == 1 else ("X", lv - 1, d)))
                        s = take("tri", prod(t, ("T1", lv, d)))
                        for out, r in zip(bank(s), heads_of(d)):
                            last = mm(out, dC[:, r], dD[:, r], True, True)
                        last.then_inc(ps_full[s], 1)
                    pe_mod_a(t, lv + 1)
                    for d in range(2):
                        done(nc.tensor, "tri", prod(t, ("T1", lv, d)))
                        if lv > 1:
                            done(nc.tensor, "tri", prod(t, ("XT", lv - 1, d)))
                        s = take("tri", prod(t, ("XT", lv, d)))
                        for out, r in zip(bank(s), heads_of(d)):
                            last = mm(out, dT1[:, r], DTs[:, t, r], True, True)
                        last.then_inc(ps_full[s], 1)
                        if lv < LEVELS - 1:
                            s = take("tri", prod(t, ("X", lv, d)))
                            for out, r in zip(bank(s), heads_of(d)):
                                last = mm(out, DTs[:, t, r], dT1[:, r], True, True)
                            last.then_inc(ps_full[s], 1)
                        if d == 0:
                            pe_mod_b(t, lv + 1)

        def pe_mod_a(t, b):
            if t == 0 and b == 0:
                nc.tensor.wait_ge(crow_ready, 2)
            w, j = block("mod2", 8 * t + b), prod(t, ("mA", b))
            s = take("tri", j)
            filled(pe_mod_rows(w, s), "tri", j)

        def pe_mod_b(t, b):
            done(nc.tensor, "tri", prod(t, ("mA", b)))
            j = prod(t, ("mB", b))
            s = take("tri", j)
            filled(pe_mod_cols(b % 2, s), "tri", j)

        def dve_mod_a(dve, t, b):
            j = prod(t, ("mA", b))
            s = full(dve, "tri", j)
            freed(nc.vector.tensor_copy(mrow[:, (b % 2) * 256:(b % 2 + 1) * 256], ps[:, s, 0:256]), "tri", j)

        def dve_mod_b(dve, t, b):
            j = prod(t, ("mB", b))
            s = full(dve, "tri", j)
            freed(dve_mod_cols(s, MOD_FIRST + 8 * t + b), "tri", j)

        def act_delta(act):
            act.wait_ge(decay_in, 1)
            flat = [dsm[:, i, :, :, :].rearrange("p d t h -> p (d t h)") for i in range(7)]
            nc.scalar.activation(flat[4], flat[2], ACT.Exp)
            nc.scalar.activation(flat[5], flat[5], ACT.Exp)
            nc.scalar.activation(flat[6], flat[3], ACT.Exp).then_inc(decay_out, 1)
            act.wait_ge(kv_out, 32)
            for t in range(NT):
                s = full(act, "tri", prod(t, "tok"))
                nc.scalar.activation(tok[:, t, :], ps[:, s, :], ACT.Copy).then_inc(ps_free[s], 1)
                act.wait_ge(e_in, t + 1)
                nc.scalar.activation(dE, dE, ACT.Exp).then_inc(e_out, 1)
                for lv in range(1, LEVELS):
                    for d in range(2):
                        s = full(act, "tri", prod(t, ("T1", lv, d)))
                        nc.scalar.activation(dT1[:, d * 512:(d + 1) * 512], ps[:, s, 0:512], ACT.Copy
                                             ).then_inc(ps_free[s], 1)

        def dve_delta(dve, st):
            s = full(dve, "cum", 0)
            nc.vector.tensor_copy(dsm[:, 2:4, :, :, :].rearrange("p i d t h -> p (i d t h)"), ps[:, s, 0:80]
                                  ).then_inc(ps_free[s], 1)
            done(dve, "cum", 0)
            nc.vector.tensor_tensor(ed, glast, gcum, ALU.subtract).then_inc(decay_in, 1)
            dve.wait_ge(kv_out, 32)
            for t in range(NT):
                s = full(dve, "tri", prod(t, "grow"))
                if t == 0:
                    dve.wait_ge(cn_out, 8 + H)
                for d in range(2):
                    last = nc.vector.tensor_tensor(quad(dE)[:, d, :, :], quad(ps[:, s, :])[:, d, :, :],
                                                   spread(gcum[:, d, t, :], 2, P), ALU.subtract)
                last.then_inc(ps_free[s], 1)
                done(dve, "tri", prod(t, "grow"))
                for d in range(2):
                    last = nc.vector.scalar_tensor_tensor(
                        quad(dE)[:, d, :, :], quad(dE)[:, d, :, :], 0.0,
                        spread(cst[:, C_NEG + d * P:C_NEG + (d + 1) * P], 1, H), ALU.min, ALU.add)
                last.then_inc(e_in, 1)
                dve.wait_ge(e_out, t + 1)
                s = full(dve, "tri", prod(t, "gram"))
                for d in range(2):
                    nc.vector.tensor_tensor(per_head(Ais[:, t, d * 512:(d + 1) * 512]), per_head(ps[:, s, 512:1024]),
                                            quad(dE)[:, d, :, :], ALU.mult)
                    last = nc.vector.tensor_tensor(quad(dM)[:, d, :, :], quad(dE)[:, d, :, :],
                                                   spread(beta[:, d, t, :], 2, P), ALU.mult)
                st.then(last)
                for d in range(2):
                    last = nc.vector.tensor_tensor(quad(dM)[:, d, :, :], per_head(ps[:, s, 0:512]),
                                                   quad(dM)[:, d, :, :], ALU.mult)
                last.then_inc(ps_free[s], 1)
                for b in range(2):
                    dve_mod_a(dve, t, b)
                for b in range(2):
                    dve_mod_b(dve, t, b)
                dve.wait_ge(c_ready, 2 * LEVELS * t + 2)
                nc.vector.tensor_tensor(DTs[:, t, :].rearrange("p (i c) -> p i c", c=P), spread(ident, 1, 2 * H),
                                        dC.rearrange("p (i c) -> p i c", c=P), ALU.subtract).then_inc(dt_ready, 1)
                s = full(dve, "tri", prod(t, "C0"))
                nc.vector.tensor_tensor(dD.rearrange("p (i c) -> p i c", c=P), spread(ident, 1, 2 * H),
                                        ps[:, s, :].rearrange("p (i c) -> p i c", c=P), ALU.subtract
                                        ).then_inc(ps_free[s], 1)
                for lv in range(1, LEVELS):
                    dve_mod_a(dve, t, lv + 1)
                    for d in range(2):
                        c = slice(d * 512, (d + 1) * 512)
                        sx = full(dve, "tri", prod(t, ("XT", lv, d)))
                        if lv < LEVELS - 1:
                            s = full(dve, "tri", prod(t, ("X", lv, d)))
                            done(dve, "tri", prod(t, "C0" if lv == 1 else ("X", lv - 1, d)))
                            nc.vector.tensor_tensor(dD[:, c], dD[:, c], ps[:, s, 0:512], ALU.subtract
                                                    ).then_inc(ps_free[s], 1)
                        if lv == 1:
                            dve.wait_ge(dt_ready, t + 1)
                        else:
                            done(dve, "tri", prod(t, ("XT", lv - 1, d)))
                        nc.vector.tensor_tensor(DTs[:, t, c], DTs[:, t, c], ps[:, sx, 0:512], ALU.subtract
                                                ).then_inc(ps_free[sx], 1)
                        if d == 0:
                            dve_mod_b(dve, t, lv + 1)
            done(dve, "tri", prod(NT - 1, ("mB", LEVELS)))
            dve_modA([1, 2, 3])

        sR, sV, sD, sO = dE, dM, dC, dD

        def pe_scan():
            nc.tensor.wait_ge(s_zero, 1)
            nc.tensor.wait_ge(state_in, 16)
            for d in range(2):
                done(nc.tensor, "tri", prod(NT - 1, ("XT", LEVELS - 1, d)))
            for i, tiles in enumerate(SCAN):
                S = Sst[min(i, 1)]
                if i > 1:
                    done(nc.tensor, "scan", 5 * (i - 1) + 4)
                for n, base in ((0, H), (1, 0)):
                    s = take("scan", 5 * i + n)
                    for j in range(2 * H):
                        d, h = j // H, j % H
                        t = tiles[d]
                        last = mm(ps[:, s, j * P:(j + 1) * P], qkvT[:, base + h, t * P:(t + 1) * P],
                                  S[:, j * P:(j + 1) * P], True, True)
                    last.then_inc(ps_full[s], 1)
                nc.tensor.wait_ge(r_ready, i + 1)
                s = take("scan", 5 * i + 2)
                for j in range(2 * H):
                    r = slice(j * P, (j + 1) * P)
                    last = mm(ps[:, s, r], DTs[:, tiles[j // H], r], sR[:, r], True, True)
                last.then_inc(ps_full[s], 1)
                done(nc.tensor, "scan", 5 * i + 2)
                s = take("scan", 5 * i + 3)
                for j in range(2 * H):
                    r = slice(j * P, (j + 1) * P)
                    last = mm(ps[:, s, r], Ais[:, tiles[j // H], r], sV[:, r], True, True)
                last.then_inc(ps_full[s], 1)
                nc.tensor.wait_ge(vd_ready, i + 1)
                s = take("scan", 5 * i + 4)
                for j in range(2 * H):
                    r = slice(j * P, (j + 1) * P)
                    last = mm(ps[:, s, r], tok[:, tiles[j // H], (j % H) * P:(j % H + 1) * P], sD[:, r], True, True)
                last.then_inc(ps_full[s], 1)

        def dve_scan(dve, st):
            dve.wait_ge(decay_out, 1)
            seen = set()
            for i, tiles in enumerate(SCAN):
                S = Sst[min(i, 1)]

                def scaled(out, inp, factor):
                    for d, t in enumerate(tiles):
                        last = nc.vector.tensor_tensor(quad(out)[:, d, :, :], quad(inp)[:, d, :, :],
                                                       spread(factor[:, d, t, :], 2, P), ALU.mult)
                    return last

                s = full(dve, "scan", 5 * i)
                scaled(sR, ps[:, s, :], eg).then_inc(ps_free[s], 1)
                done(dve, "scan", 5 * i)
                for d, t in enumerate(tiles):
                    last = nc.vector.tensor_tensor(sR[:, d * 512:(d + 1) * 512], tok[:, t, 512:1024],
                                                   sR[:, d * 512:(d + 1) * 512], ALU.subtract)
                last.then_inc(r_ready, 1)
                s = full(dve, "scan", 5 * i + 1)
                scaled(sO, ps[:, s, :], eg).then_inc(ps_free[s], 1)
                st.then(scaled(S, S, el))
                s = full(dve, "scan", 5 * i + 2)
                scaled(sV, ps[:, s, :], beta).then_inc(ps_free[s], 1)
                done(dve, "scan", 5 * i + 2)
                scaled(sD, sV, ed).then_inc(vd_ready, 1)
                done(dve, "scan", 5 * i + 1)
                s = full(dve, "scan", 5 * i + 3)
                for d, t in enumerate(tiles):
                    o = oS[:, t, :] if t not in seen else sO[:, d * 512:(d + 1) * 512]
                    last = nc.vector.tensor_tensor(o, sO[:, d * 512:(d + 1) * 512], ps[:, s, d * 512:(d + 1) * 512],
                                                   ALU.add)
                    if d == 0:
                        again = [x for x in enumerate(tiles) if x[1] in seen or (x[0] == 1 and tiles[0] == tiles[1])]
                        seen.add(t)
                seen.add(tiles[1])
                last.then_inc(ps_free[s], 1)
                done(dve, "scan", 5 * i + 3)
                for d, t in again:
                    st.then(nc.vector.tensor_tensor(oS[:, t, :], oS[:, t, :], sO[:, d * 512:(d + 1) * 512], ALU.add))
                s = full(dve, "scan", 5 * i + 4)
                nc.vector.tensor_tensor(S, S, ps[:, s, :], ALU.add).then_inc(ps_free[s], 1)
                done(dve, "scan", 5 * i + 4)
            sq = tmp[:, 0:NT * 512]
            oF = oS.rearrange("p t c -> p (t c)")
            st.then(nc.vector.tensor_tensor(sq, oF, oF, ALU.mult))
            nc.vector.tensor_reduce(osd[:, :], sq.rearrange("p (i c) -> p i c", c=P), AX.X, ALU.add
                                    ).then_inc(os_ready, 1)
            dve.wait_ge(od_ready, 1)
            st.then(nc.vector.reciprocal(osd[:, :], osd[:, :]))
            nc.vector.tensor_tensor(oF.rearrange("p (i c) -> p i c", c=P), oF.rearrange("p (i c) -> p i c", c=P),
                                    spread(osd[:, :], 2, P), ALU.mult).then_inc(on_ready, 1)
            dve.wait_ge(state_out, 16)
            for t in range(NT):
                s = full(dve, "onrm", t)
                nc.vector.scalar_tensor_tensor(hT[:, 0:H, t * P:(t + 1) * P], per_head(ps[:, s, 0:512]),
                                               wsm[:, S_ONORM:S_ONORM + 1], zT[:, :, t * P:(t + 1) * P],
                                               ALU.mult, ALU.mult).then_inc(ps_free[s], 1)

        def act_onorm(act):
            act.wait_ge(os_ready, 1)
            nc.scalar.activation(osd[:, :], osd[:, :], ACT.Sqrt, bias=eps, scale=1.0 / P).then_inc(od_ready, 1)

        def pe_onorm():
            nc.tensor.wait_ge(on_ready, 1)
            for t in range(NT):
                s = take("onrm", t)
                for h in range(H):
                    last = nc.tensor.transpose(ps[:, s, h * P:(h + 1) * P], oS[:, t, h * P:(h + 1) * P], ident)
                last.then_inc(ps_full[s], 1)

        def pe_out(stage):
            with nc.tensor.Fori(0, 2) as turn:
                for j in range(4):
                    if j % 2 == 0:
                        w = block(stage, j // 2, turn)
                    pe_linear(stage, j, turn, cols(w, KD, 256, j % 2), from_h)

        def dve_residual(dve, stage, each, turns, gate):
            with dve.Fori(0, turns) as turn:
                for j in range(each):
                    dve_residual_chunk(dve, stage, each, turn, j, gate)

        def dve_residual_chunk(dve, stage, each, turn, j, gate):
            s = full(dve, stage, j, turn)
            c = turn * each + j
            for a, b, at, grp in ((0, SEQ, 0, 0), (SEQ, HT, SEQ, 1), (HT, T, 512, 1)):
                xs = xT[:, bass.ds(c * T + a, b - a)]
                last = nc.vector.scalar_tensor_tensor(xs, ps[:, s, at:at + b - a],
                                                      modcol[:, bass.ds(c * 2 + (gate * 16 + grp), 1)], xs,
                                                      ALU.mult, ALU.add)
            last.then_inc(ps_free[s], 1)

        def pe_ffn():
            with nc.tensor.Fori(0, 2) as turn:
                for j in range(EC):
                    nc.tensor.wait_ge(fhi_ready, turn * EC + (j + 1))
                    lead, rest = fhi[:, j % 3, :], wring_x[:, wuse("fgu", j, turn)[0], :]
                    for u in range(2):
                        s = take("fgu", 2 * j + u, turn)
                        for n, (w, h) in enumerate(((lead, fh[0]), (lead, fh[1]), (rest, fh[0]))):
                            if n == 2 and u == 0:
                                nc.tensor.wait_ge(flo_ready, turn * EC + (j + 1))
                            for k in range(KD):
                                if j + u == 0 and n < 2:
                                    nc.tensor.wait_ge(*((h_ready, 8 + k + 1) if n == 0 else (hlo_ready, k + 1)))
                                for half in range(2):
                                    last = mm(pair(s)[:, half, :],
                                              w[:, k * 256 + u * P:k * 256 + (u + 1) * P],
                                              h[:, k, half * HT:(half + 1) * HT],
                                              n + k == 0, n == 2 and k == KD - 1)
                        last.then_inc(ps_full[s], 1)
            with nc.tensor.Fori(0, 4) as turn:
                for j in range(2):
                    s = take("fdn", j, turn)
                    for n in range(3):
                        for k in range(FC):
                            b, c = 2 * j + k // LK, slice((k % LK) * P, (k % LK + 1) * P)
                            if n < 2 and k % LK == 0:
                                nc.tensor.wait_ge(dlo_ready if n else dhi_ready, turn * 4 + (b + 1))
                            if j == 0 and n == 0:
                                nc.tensor.wait_ge(lead_ready, k + 1)
                            if j == 0 and n == 2:
                                nc.tensor.wait_ge(*((left_ready, k + 1) if k < LEFT else (left_pool_ready, k + 1 - LEFT)))
                            w = wslot_x[b][:, c] if n == 1 else dhi[:, b, c]
                            for half in range(2):
                                h = slice(half * HT, (half + 1) * HT)
                                last = mm(pair(s)[:, half, :], w, act_x[:, k, h] if n == 2 else act_lead[k][:, h],
                                          n + k == 0, n == 2 and k == FC - 1)
                    last.then_inc(ps_full[s], 1)

        def act_fhi(act, j, turn):
            s, n = wuse("fgu", j, turn)
            act.wait_ge(w_full[s], 16 * (n + 1))
            if not (isinstance(turn, int) and j < 3):
                full(act, "fgu", 2 * (j - 3 if j >= 3 else (9, 10, 8)[j]) + 1, turn if j >= 3 else turn - 1)
            nc.scalar.activation(fhi[:, j % 3, :], wring[:, s, :], ACT.Copy).then_inc(fhi_ready, 1)

        def dve_flo(dve, j, turn):
            dve.wait_ge(fhi_ready, turn * EC + (j + 1))
            s = wuse("fgu", j, turn)[0]
            nc.vector.tensor_tensor(wring_x[:, s, :], wring[:, s, :], fhi[:, j % 3, :].bitcast(F32), ALU.subtract).then_inc(flo_ready, 1)

        LEFT = 14

        def act_lead_parts(act):
            full(act, "fgu", 2 * EC - 1, 1)
            for b in range(2):
                act_dhi(act, b, 0)
            done(act, "fgu", 2 * EC - 1, 1)
            for k in range(FC):
                nc.scalar.activation(act_lead[k], actT[:, k, :], ACT.Copy).then_inc(lead_ready, 1)

        def write_left(eng, ks, ready):
            for k in ks:
                eng.wait_ge(lead_ready, k + 1)
                eng.tensor_tensor(act_x[:, k, :], actT[:, k, :], act_lead[k].bitcast(F32), ALU.subtract
                                  ).then_inc(ready, 1)

        def act_dhi(act, b, turn):
            s, n = wuse("fdn", b, turn)
            act.wait_ge(w_full[s], 16 * (n + 1))
            if not (isinstance(turn, int) and turn == 0):
                full(act, "fdn", b // 2, turn - 1)
            nc.scalar.activation(dhi[:, b, :], wslot[s][:, 0:LK * P], ACT.Copy).then_inc(dhi_ready, 1)

        def dve_dlo(dve, b, turn):
            dve.wait_ge(dhi_ready, turn * 4 + (b + 1))
            s = wuse("fdn", b, turn)[0]
            nc.vector.tensor_tensor(wslot_x[s][:, 0:LK * P], wslot[s][:, 0:LK * P], dhi[:, b, :].bitcast(F32),
                                    ALU.subtract).then_inc(dlo_ready, 1)

        def act_fdn(act):
            act_lead_parts(act)
            with act.Fori(0, 4) as turn:
                for b in range(2, 4):
                    act_dhi(act, b, turn)
                with act.If(turn < 3):
                    for b in range(2):
                        act_dhi(act, b, turn + 1)

        def dve_fdn(dve):
            for b in range(2):
                dve_dlo(dve, b, 0)
            write_left(dve, range(LEFT), left_ready)
            with dve.Fori(0, 4) as turn:
                for b in range(2, 4):
                    dve_dlo(dve, b, turn)
                dve_residual_chunk(dve, "fdn", 2, turn, 0, 5)
                with dve.If(turn < 3):
                    for b in range(2):
                        dve_dlo(dve, b, turn + 1)
                dve_residual_chunk(dve, "fdn", 2, turn, 1, 5)

        def ahead(eng, split, j, turn):
            if j + 2 < EC:
                split(eng, j + 2, turn)
            else:
                with eng.If(turn < 1):
                    split(eng, j + 2 - EC, turn + 1)

        def pool_hlo(pool):
            for k in range(KD):
                pool.wait_ge(h_ready, 8 + k + 1)
                nc.gpsimd.tensor_tensor(fh[1][:, k, :], hT[:, k, :], fh[0][:, k, :].bitcast(F32), ALU.subtract
                                        ).then_inc(hlo_ready, 1)

        def act_gate(act, stage, j, turn):
            if j >= 2:
                done(act, stage, 2 * (j - 2) + 1, turn)
            else:
                done(act, stage, 2 * (EC - 1 - j) + 1, turn - 1)
            s = full(act, stage, 2 * j, turn)
            nc.scalar.activation(sg[:, j % 2, :].rearrange("p (b n) -> p b n", b=2), pair(s), ACT.Silu
                                 ).then_inc(ps_free[s], 1)

        def dve_up(dve, stage, j, turn, out):
            done(dve, stage, 2 * j, turn)
            s = full(dve, stage, 2 * j + 1, turn)
            nc.vector.tensor_tensor(out.rearrange("p (b n) -> p b n", b=2),
                                    sg[:, j % 2, :].rearrange("p (b n) -> p b n", b=2), pair(s), ALU.mult
                                    ).then_inc(ps_free[s], 1)

        def pe_odd_in():
            for c in range(6):
                if c % 2 == 0:
                    w = block("oi", c // 2)
                pe_linear("oi", c, 0, cols(w, KD, 256, c % 2), from_h, h_base=None if c else 16)
            pe_colnorm("mlan", mla_groups, 12)
            done(nc.tensor, "oi", 5)
            s = take("oi", 6)
            mm(ps[:, s, 0:DEC_SEQ], rot, krraw[:, SEQ:T], True, True).then_inc(ps_full[s], 1)

        def pe_odd_qkv():
            nc.tensor.wait_ge(cn_out, 13)

            def from_cq(k, a, b):
                return cq[:, k, a:b]

            for c in range(HC):
                if c % 4 == 0:
                    w = block("uqn", c // 4)
                pe_linear("uqn", c, 0, cols(w, 3, 512, c % 4), from_cq)
            w = block("uqr", 0)
            for j, (what, c) in enumerate(uq_order):
                if what == "P":
                    pe_linear("uqr", j, 0, cols(w, 3, 512, c), from_cq)
                else:
                    done(nc.tensor, "uqr", uq_order.index(("P", c)))
                    s = take("uqr", j)
                    mm(ps[:, s, 0:DEC_SEQ], rot, qraw[:, c % 2, SEQ:T], True, True).then_inc(ps_full[s], 1)
            nc.tensor.wait_ge(cn_out, 14)
            nc.tensor.wait_ge(mla_caches_in, 32)
            w = block("kn", 0)
            for c in range(HC):
                pe_linear("kn", c, 0, cols(w, 2, D, c), lambda k, a, b: ckv[:, k, a:b], TK // 2)
            w = block("vv", 0)
            for t in range(NT + 1):
                s = take("vv", t)
                for half in range(2):
                    for k in range(2):
                        last = mm(ps[:, s, half * 512:(half + 1) * 512], ckv[:, k, t * P:(t + 1) * P],
                                  w[:, k * D + half * 512:k * D + (half + 1) * 512], k == 0, k == 1)
                last.then_inc(ps_full[s], 1)

        def act_odd_in(act):
            for c in range(6):
                s = full(act, "oi", c)
                dst = cq[:, c, :] if c < 3 else ckv[:, c - 3, 0:T] if c < 5 else krraw
                nc.scalar.activation(dst.rearrange("p (b n) -> p b n", b=2), pair(s), ACT.Copy
                                     ).then_inc(ps_free[s], 1)
            done(act, "oi", 4)
            act_colnorm(act, "mlan", mla_groups, 12, [1 / 384, 1 / 256])

        def act_odd_qkv(act):
            scale = 192 ** -0.5
            act.wait_ge(cn_out, 14)
            for c in range(HC):
                s = full(act, "uqn", c)
                nc.scalar.activation(qn[:, c, :].rearrange("p (b n) -> p b n", b=2), pair(s), ACT.Copy, scale=scale
                                     ).then_inc(ps_free[s], 1)
            for c in range(4):
                if c >= 2:
                    done(act, "uqr", uq_order.index(("R", c - 2)))
                s = full(act, "uqr", uq_order.index(("P", c)))
                nc.scalar.activation(qraw[:, c % 2, :].rearrange("p (b n) -> p b n", b=2), pair(s), ACT.Copy,
                                     scale=scale).then_inc(ps_free[s], 1)
            for c in range(HC):
                s = full(act, "kn", c)
                nc.scalar.activation(kn[:, c, :].rearrange("p (b n) -> p b n", b=2), pair(s, TK // 2), ACT.Copy
                                     ).then_inc(ps_free[s], 1)

        def dve_odd(dve, st):
            dve_colnorm(dve, st, "mlan", mla_groups)
            s = full(dve, "oi", 6)
            dve_rope(st, krraw, krT[:, 0:T], s)
            for c in range(4):
                s = full(dve, "uqr", uq_order.index(("R", c)))
                if c == 0:
                    done(dve, "oi", 6)
                else:
                    done(dve, "uqr", uq_order.index(("R", c - 1)))
                dve_rope(st, qraw[:, c % 2, :], qr[:, c, :], s)
            for t in range(NT + 1):
                s = full(dve, "vv", t)
                nc.vector.tensor_copy(vC[:, t, :], ps[:, s, :]).then_inc(ps_free[s], 1)

        MISC = 4096

        def rows8(k, n=NE):
            return tmp[:, MISC + 64 * k:MISC + 64 * k + NT * n].rearrange("p (t e) -> p t e", e=n)

        rt = gates_sb[:, 0:NT * NE].rearrange("p (t e) -> p t e", e=NE)
        top, topi, topf, oh1, oh2, oh, pos, prd = (rows8(k) for k in range(8))
        topi = topi.bitcast(U32)
        tw = tmp[:, MISC + 512:MISC + 512 + NT]
        cnt, tiles_e, last_e, first_e = (tmp[:, MISC + 528 + 8 * i:MISC + 536 + 8 * i] for i in range(4))
        cmp = tmp[:, MISC + 576:MISC + 576 + (ITEMS + 1) * NE].rearrange("p (i e) -> p i e", e=NE)
        sgE, actf = (expf[:, i * 512:(i + 1) * 512].rearrange("p (b m s) -> p b m s", b=2, m=2) for i in range(2))
        POOLS = (0, 1, 4, 7, 10, 13)
        started, endp = (tmp[:, MISC + 820 + 8 * i:MISC + 828 + 8 * i] for i in range(2))
        begun = tmp[:, MISC + 840:MISC + 840 + (ITEMS + 1) * NE].rearrange("p (i e) -> p i e", e=NE)
        bigf = tmp[:, MISC + 960:MISC + 960 + ITEMS + 1]
        whof = tmp[:, MISC + 800:MISC + 800 + ITEMS + 1]

        def pe_router():
            nc.tensor.wait_ge(h_ready, 32)
            w, s = block("rt", 0), take("rt", 0)
            for t in range(NT):
                for k in range(KD):
                    last = mm(ps[:, s, t * NE:(t + 1) * NE], hT[:, k, t * P:(t + 1) * P], w[:, k * NE:(k + 1) * NE],
                              k == 0, k == KD - 1)
            last.then_inc(ps_full[s], 1)
            for t in range(NT):
                s = take("ht", t)
                for k in range(KD):
                    last = nc.tensor.transpose(ps[:, s, k * P:(k + 1) * P], hT[:, k, t * P:(t + 1) * P], ident)
                last.then_inc(ps_full[s], 1)
            nc.tensor.wait_ge(oh_ready, 1)
            s = take("cnt", 0)
            for t in range(NT):
                for u in range(t + 1):
                    mm(ps[:, s, t * NE:(t + 1) * NE], tri[0] if u == t else ones, oh[:, u, :], u == 0, u == t)
            for u in range(NT):
                last = mm(ps[:, s, NT * NE:(NT + 1) * NE], ones, oh[:, u, :], u == 0, u == NT - 1)
            last.then_inc(ps_full[s], 1)

        def dve_router(dve, st):
            dve.wait_ge(mla_out, 32)
            s = full(dve, "rt", 0)
            nc.vector.tensor_copy(gates_sb[:, 0:NT * NE], ps[:, s, 0:NT * NE]).then_inc(ps_free[s], 1)
            done(dve, "rt", 0)
            for t in range(NT):
                last = nc.vector.max(top[:, t, :], rt[:, t, :])
            st.then(last)
            for t in range(NT):
                st.then(nc.vector.max_index(topi[:, t, :], top[:, t, :], rt[:, t, :]))
            nc.vector.tensor_copy(topf, topi)
            nc.vector.tensor_tensor(tw, top[:, :, 1], top[:, :, 0], ALU.subtract).then_inc(top_ready, 1)
            dve.wait_ge(top_ready, 1)
            for t in range(NT):
                for i, o in enumerate((oh1, oh2)):
                    last = nc.vector.tensor_scalar(o[:, t, :], iota[:, 0:NE], topf[:, t, i:i + 1], None, ALU.is_equal)
            st.then(last)
            nc.vector.tensor_tensor(oh, oh1, oh2, ALU.add).then_inc(oh_ready, 1)
            dve.wait_ge(top_exp, 1)
            st.then(nc.vector.tensor_scalar(tokw[:, 1, :], tw, 1.0, None, ALU.add))
            st.then(nc.vector.reciprocal(tokw[:, 0, :], tokw[:, 1, :]))
            st.then(nc.vector.tensor_tensor(tokw[:, 1, :], tw, tokw[:, 0, :], ALU.mult))
            for t in range(NT):
                dve.wait_ge(hhi_ready, t + 1)
                s, _ = R.use("ht", t)
                nc.vector.tensor_tensor(hlo[:, t, :], ps[:, s, :], hhi[:, t, :].bitcast(F32), ALU.subtract
                                        ).then_inc(ps_free[s], 1)
            s = full(dve, "cnt", 0)
            nc.vector.tensor_copy(pos, ps[:, s, 0:NT * NE].rearrange("p (t e) -> p t e", e=NE))
            nc.vector.tensor_copy(cnt, ps[:, s, NT * NE:(NT + 1) * NE]).then_inc(ps_free[s], 1)
            done(dve, "cnt", 0)
            st.then(nc.vector.tensor_scalar(tiles_e, cnt, 0.0, None, ALU.is_gt))
            for m in range(1, -(-T // IT)):
                st.then(nc.vector.scalar_tensor_tensor(tiles_e, cnt, float(m * IT), tiles_e, ALU.is_gt, ALU.add))
            st.then(nc.vector.tensor_tensor_scan(last_e, ones[:, 0:NE], tiles_e, 0.0, ALU.mult, ALU.add))
            nc.vector.tensor_tensor(cmp, spread(last_e, 1, ITEMS + 1), spread(iota[:, 0:ITEMS + 1], 2, NE), ALU.is_le)
            nc.vector.tensor_tensor(started, last_e, tiles_e, ALU.subtract)
            st.then(nc.vector.tensor_tensor(first_e, last_e, tiles_e, ALU.subtract))
            nc.vector.tensor_reduce(whof, cmp, AX.X, ALU.add)
            st.then(nc.vector.tensor_scalar(first_e, first_e, float(IT), -1.0, ALU.mult, ALU.add))
            st.then(nc.vector.tensor_scalar(whof, whof, float(NE - 1), None, ALU.min))
            nc.vector.tensor_copy(item_expert[0:1, 0:ITEMS + 1], whof[0:1, :])
            nc.vector.tensor_copy(item_expert[0:1, ITEMS + 1:ITEMS + 2], last_e[0:1, NE - 1:NE])
            st.then(nc.vector.scalar_tensor_tensor(endp, first_e, 1.0, cnt, ALU.add, ALU.add))
            st.then(nc.vector.scalar_tensor_tensor(cmp, spread(iota[:, 0:ITEMS + 1], 2, NE), float(-IT),
                                                   spread(endp, 1, ITEMS + 1), ALU.mult, ALU.add))
            nc.vector.tensor_tensor(begun, spread(iota[:, 0:ITEMS + 1], 2, NE), spread(started, 1, ITEMS + 1), ALU.is_ge)
            st.then(nc.vector.tensor_scalar(cmp, cmp, float(P), None, ALU.is_gt))
            st.then(nc.vector.tensor_tensor(cmp, cmp, begun, ALU.mult))
            st.then(nc.vector.tensor_reduce(bigf, cmp, AX.X, ALU.add))
            nc.vector.tensor_copy(item_expert[0:1, ITEMS + 2:2 * ITEMS + 3], bigf[0:1, :]).then_inc(items_ready, 1)
            st.then(nc.vector.tensor_tensor(pos, pos, spread(first_e, 1, NT), ALU.add))
            for i, o in enumerate((oh1, oh2)):
                st.then(nc.vector.tensor_tensor(prd, pos, o, ALU.mult))
                st.then(nc.vector.tensor_reduce(slot_of[:, i, :], prd, AX.X, ALU.add))
            dve_select(st)

        def dve_select(st):
            w2 = inw[:, 1:3, :]
            for t in range(NT):
                last = nc.vector.tensor_scalar(sel[:, t, :], iota, slot_of[:, 0, t:t + 1], None, ALU.is_equal)
            st.then(nc.vector.tensor_scalar(w2, slot_of[:, :, :], 0.0, None, ALU.is_ge))
            st.then(nc.vector.scalar_tensor_tensor(w2, slot_of[:, :, :], float(IT), w2, ALU.is_lt, ALU.mult))
            st.then(nc.vector.tensor_tensor(w2, w2, tokw[:, :, :], ALU.mult))
            nc.vector.tensor_tensor(inw[:, 0, :], inw[:, 1, :], inw[:, 2, :], ALU.add)
            for t in range(NT):
                last = nc.vector.scalar_tensor_tensor(sel[:, t, :], iota, slot_of[:, 1, t:t + 1],
                                                      sel[:, t, :].bitcast(F32), ALU.is_equal, ALU.add)
            last.then_inc(sel_ready, 1)

        def wsize(b):
            return 3 * 512 if b in (EC + 2, EC + 5) else WB

        def product(b):
            return f"gu{b}" if b < EC else f"dn{(b - EC) // 3}"

        def act_whi(act, b, i):
            act.wait_ge(w_full[wuse("moe", b, i)[0]], 16 * (wuse("moe", b, i)[1] + 1))
            full(act, "moe", ITEM.index(product(b - 3 if b >= 3 else EC + 6 - (2, 1, 3)[b])), i if b >= 3 else i - 1)
            nc.scalar.activation(whi[:, b % 3, 0:wsize(b)], wslot[wuse("moe", b, i)[0]][:, 0:wsize(b)], ACT.Copy
                                 ).then_inc(whi_ready, 1)

        def write_wlo(eng, b, i, ready):
            eng.wait_ge(whi_ready, i * (EC + 6) + (b + 1))
            s, size = wuse("moe", b, i)[0], wsize(b)
            eng.tensor_tensor(wslot_x[s][:, 0:size], wslot[s][:, 0:size], whi[:, b % 3, 0:wsize(b)].bitcast(F32), ALU.subtract
                              ).then_inc(ready, 1)

        def pe_whi(b, i):
            nc.tensor.wait_ge(whi_ready, i * (EC + 6) + (b + 1))
            return whi[:, b % 3, :]

        def pe_wlo(b, i):
            if b in POOLS:
                nc.tensor.wait_ge(wlo_pool_ready, i * len(POOLS) + (POOLS.index(b) + 1))
            else:
                nc.tensor.wait_ge(wlo_ready, i * (EC + 6 - len(POOLS)) + len([c for c in range(b + 1) if c not in POOLS]))
            return wslot_x[wuse("moe", b, i)[0]]

        def xpart(part, k):
            return xg[:, k // 2, part, (k % 2) * IT:(k % 2 + 1) * IT]

        def pe_gather(stage, base, turn, item):
            nc.tensor.wait_ge(sel_ready, item + 1)
            for q in range(4):
                s = take(stage, base + q, turn)
                for part, x in enumerate((hhi, hlo)):
                    for k in range(2):
                        for t in range(NT):
                            last = mm(ps[:, s, part * 512 + k * IT:part * 512 + (k + 1) * IT],
                                      x[:, t, (2 * q + k) * P:(2 * q + k + 1) * P], sel[:, t, :], t == 0, t == NT - 1)
                last.then_inc(ps_full[s], 1)

        def act_gathered(act, stage, j, q, turn):
            s = full(act, stage, j, turn)
            nc.scalar.activation(xg[:, q, :, :].rearrange("p r n -> p (r n)"), ps[:, s, :], ACT.Copy
                                 ).then_inc(ps_free[s], 1)

        def pe_item(i, tiles):
            at = ITEM.index

            def turned(j):
                done(nc.tensor, "moe", at(f"gu{j}"), i)
                s = take("moe", at(f"tr{j}"), i)
                for m in range(tiles):
                    last = nc.tensor.transpose(ps[:, s, m * P:(m + 1) * P], actf[:, j % 2, m, :], ident)
                last.then_inc(ps_full[s], 1)

            done(nc.tensor, "moe", at("ga3"), i - 1)
            for j in range(EC):
                w, s = pe_whi(j, i), take("moe", at(f"gu{j}"), i)
                for m in range(tiles):
                    for k in range(KD):
                        for part in range(2):
                            mm(ps[:, s, m * 512:m * 512 + 256], xpart(part, k)[:, m * P:(m + 1) * P],
                               w[:, k * 256:(k + 1) * 256], k + part == 0, False)
                w = pe_wlo(j, i)
                for m in range(tiles):
                    for k in range(KD):
                        last = mm(ps[:, s, m * 512:m * 512 + 256], xpart(0, k)[:, m * P:(m + 1) * P],
                                  w[:, k * 256:(k + 1) * 256], False, k == KD - 1)
                last.then_inc(ps_full[s], 1)
                if j:
                    turned(j - 1)
            for m in range(2):
                s = take("moe", at(f"turnP{m}"), i)
                for t in range(NT):
                    last = nc.tensor.transpose(ps[:, s, t * P:(t + 1) * P],
                                               sel[:, t, m * P:(m + 1) * P].bitcast(F32), ident)
                last.then_inc(ps_full[s], 1)
            s = take("moe", at("gs"), i)
            for m in range(2):
                for t in range(NT):
                    last = mm(ps[:, s, m:m + 1], sel[:, t, m * P:(m + 1) * P].bitcast(F32), inw[:, 0, t:t + 1],
                              t == 0, t == NT - 1)
            last.then_inc(ps_full[s], 1)
            turned(EC - 1)
            done(nc.tensor, "moe", at(f"tr{EC - 1}"), i)
            for half in range(2):
                if half == 1:
                    pe_gather("moe", at("ga0"), i, i + 1)
                s = take("moe", at(f"dn{half}"), i)
                for b in range(3):
                    blk, ks = EC + 3 * half + b, range(4 * b, min(4 * b + 4, EC))
                    w = pe_whi(blk, i)
                    for k in ks:
                        for m in range(tiles):
                            for a in (ahi, alo):
                                mm(ps[:, s, m * 512:(m + 1) * 512], a[:, k, m * P:(m + 1) * P],
                                   w[:, (k % 4) * 512:(k % 4 + 1) * 512], k == 0 and a is ahi, False)
                    w = pe_wlo(blk, i)
                    for k in ks:
                        for m in range(tiles):
                            last = mm(ps[:, s, m * 512:(m + 1) * 512], ahi[:, k, m * P:(m + 1) * P],
                                      w[:, (k % 4) * 512:(k % 4 + 1) * 512], False, k == EC - 1)
                last.then_inc(ps_full[s], 1)
            for c in range(KD):
                if c % 4 == 0:
                    done(nc.tensor, "moe", at(f"dn{c // 4}"), i)
                s = take("moe", at(f"sc{c}"), i)
                for half in range(2):
                    for m in range(tiles):
                        for part, y in enumerate((yhi, ylo)):
                            last = mm(pair(s)[:, half, :], y[:, m, c * P:(c + 1) * P],
                                      selT[:, m, half * HT:(half + 1) * HT], m + part == 0, m == tiles - 1 and part == 1)
                last.then_inc(ps_full[s], 1)

        def pe_moe():
            done(nc.tensor, "ht", NT - 1)
            pe_gather("moe0", 0, 0, 0)
            done(nc.tensor, "moe0", 3)
            at = ITEM.index
            n = items_of(nc.tensor)
            with nc.tensor.Fori(0, ITEMS) as i:
                with nc.tensor.If(i < n):
                    big = nc.tensor.value_load(item_expert[0:1, bass.ds(i + (ITEMS + 2), 1)], min_val=0, max_val=1)
                    with nc.tensor.If(big > 0):
                        pe_item(i, 2)
                    with nc.tensor.If(big < 1):
                        pe_item(i, 1)
            for j in range(len(ITEM) - 4, len(ITEM)):
                done(nc.tensor, "moe", j, n - 1)

        def act_moe(act):
            at = ITEM.index
            act.wait_ge(mla_out, 32)
            for t in range(NT):
                s = full(act, "ht", t)
                nc.scalar.activation(hhi[:, t, :], ps[:, s, :], ACT.Copy).then_inc(hhi_ready, 1)
            for q in range(4):
                act_gathered(act, "moe0", q, q, 0)
            n = items_of(act)
            with act.Fori(0, ITEMS) as i:
                with act.If(i < n):
                    act_whi(act, 0, i)
                    act_whi(act, 1, i)
                    for j in range(EC):
                        act_whi(act, j + 2, i)
                        done(act, "moe", at(f"gu{j - 2 if j >= 2 else EC - 1 - j}"), i if j >= 2 else i - 1)
                        s = full(act, "moe", at(f"gu{j}"), i)
                        nc.scalar.activation(sgE[:, j % 2, :, :], pair(s, P), ACT.Silu).then_inc(silu_ready, 1)
                        if j:
                            act_ahi(act, j - 1, i)
                    act_whi(act, EC + 2, i)
                    act_ahi(act, EC - 1, i)
                    act_whi(act, EC + 3, i)
                    act_gathered(act, "moe", at("ga0"), 0, i)
                    act_whi(act, EC + 4, i)
                    act_gathered(act, "moe", at("ga1"), 1, i)
                    act_whi(act, EC + 5, i)
                    act_gathered(act, "moe", at("ga2"), 2, i)
                    act_gathered(act, "moe", at("ga3"), 3, i)
            return n

        def act_ahi(act, j, i):
            s = full(act, "moe", ITEM.index(f"tr{j}"), i)
            nc.scalar.activation(ahi[:, j, :], ps[:, s, 0:IT], ACT.Copy).then_inc(ahi_ready, 1)

        def dve_alo(dve, j, i):
            dve.wait_ge(ahi_ready, i * EC + (j + 1))
            s, _ = R.use("moe", ITEM.index(f"tr{j}"), i)
            nc.vector.tensor_tensor(alo[:, j, :], ps[:, s, 0:IT], ahi[:, j, :].bitcast(F32), ALU.subtract
                                    ).then_inc(ps_free[s], 1)

        def pool_moe(pool):
            n = items_of(pool)
            with pool.Fori(0, ITEMS) as i:
                with pool.If(i < n):
                    for b in POOLS:
                        write_wlo(pool, b, i, wlo_pool_ready)

        def dve_results(dve, st, half, i):
            s, c = full(dve, "moe", ITEM.index(f"dn{half}"), i), slice(half * 512, (half + 1) * 512)
            for m in range(2):
                last = nc.vector.tensor_scalar(yhi[:, m, c], ps[:, s, m * 512:(m + 1) * 512],
                                               gslot[:, m:m + 1], None, ALU.mult)
            st.then(last)
            for m in range(2):
                last = nc.vector.scalar_tensor_tensor(ylo[:, m, c], ps[:, s, m * 512:(m + 1) * 512],
                                                      gslot[:, m:m + 1], yhi[:, m, c].bitcast(F32), ALU.mult, ALU.subtract)
            last.then_inc(ps_free[s], 1)

        def dve_moe(dve, st):
            at = ITEM.index
            n = items_of(dve)
            with dve.Fori(0, ITEMS) as i:
                with dve.If(i < n):
                    st.loop(i, 6)
                    for j in range(EC):
                        if j + 2 not in POOLS:
                            write_wlo(dve, j + 2, i, wlo_ready)
                        if j >= 2:
                            dve_alo(dve, j - 2, i)
                        dve.wait_ge(silu_ready, i * EC + (j + 1))
                        s, _ = R.use("moe", at(f"gu{j}"), i)
                        nc.vector.tensor_tensor(actf[:, j % 2, :, :], sgE[:, j % 2, :, :],
                                                ps[:, s, :].rearrange("p (m n) -> p m n", m=2)[:, :, P:2 * P], ALU.mult
                                                ).then_inc(ps_free[s], 1)
                    dve_alo(dve, EC - 2, i)
                    for m in range(2):
                        s = full(dve, "moe", at(f"turnP{m}"), i)
                        nc.vector.tensor_copy(selT[:, m, :], ps[:, s, 0:T]).then_inc(ps_free[s], 1)
                    s = full(dve, "moe", at("gs"), i)
                    nc.vector.tensor_copy(gslot[:, :], ps[:, s, 0:2]).then_inc(ps_free[s], 1)
                    dve_alo(dve, EC - 1, i)
                    done(dve, "moe", at("gs"), i)
                    st.then(nc.vector.tensor_scalar(slot_of[:, :, :], slot_of[:, :, :], float(-IT), None, ALU.add))
                    dve_select(st)
                    dve_results(dve, st, 0, i)
                    for b in range(EC + 3, EC + 6):
                        write_wlo(dve, b, i, wlo_ready)
                    dve_results(dve, st, 1, i)
                    for c in range(KD):
                        s = full(dve, "moe", at(f"sc{c}"), i)
                        for a, b, grp in ((0, SEQ, 0), (SEQ, HT, 1), (HT, T, 1)):
                            last = nc.vector.scalar_tensor_tensor(
                                xc[:, c, a:b], pair(s)[:, a // HT, a % HT:(b - 1) % HT + 1],
                                modcol[:, 11 * 16 + 2 * c + grp:11 * 16 + 2 * c + grp + 1], xc[:, c, a:b],
                                ALU.mult, ALU.add)
                        last.then_inc(ps_free[s], 1)

        block_ = ctx.enter_context(nc.Block())

        @block_.sync
        def _(sync):
            sync.dma_start(wsm[:, :], I["wsm"]).then_inc(consts_in, 16)
            sync.dma_start(cst[:, 0:C_COLS], I["cst"]).then_inc(consts_in, 16)
            sync.dma_start(lam_in[:, :], I["lam"]).then_inc(consts_in, 16)
            sync.dma_start(cossin[:, :, :], I["cossin"]).then_inc(consts_in, 16)
            for stage in loads:
                if stage == "moe":
                    load_items(sync)
                else:
                    load_stage(sync, stage)
                if stage == "mod":
                    sync.dma_start(xT[:, :], I["x"]).then_inc(x_in, 16)
            sync.wait_ge(hs_ready, 8 * 5)
            sync.dma_start(O["y"], hT[:, :, :].rearrange("p k t -> p (k t)")).then_inc(y_out, 16)
            sync.wait_ge(y_out, 16)

        @block_.gpsimd
        def _(pool):
            pool.dma_start(kT[:, :, T:TK], I["ck"]).then_inc(caches_in, 16)
            pool.dma_start(vB[:, NT, :], I["cv"]).then_inc(caches_in, 16)
            done(pool, "qk", 15)
            pool.dma_start(O["dk"], kT[:, :, 0:SEQ]).then_inc(kv_out, 16)
            done(pool, "vb", 0)
            pool.dma_start(O["dv"], vB[:, 0, :]).then_inc(kv_out, 16)
            full(pool, "vb", NT - 1)
            pool.dma_start(Sst[1], I["state"]).then_inc(state_in, 16)
            pool_delta(pool)
            done(pool, "scan", 4)
            pool.dma_start(O["state"], Sst[0]).then_inc(state_out, 16)
            pool_hlo(pool)
            write_left(pool, range(LEFT, FC), left_pool_ready)
            full(pool, "fdn", 1, 3)
            pool.dma_start(ckv[:, :, T:TK], I["cckv"]).then_inc(mla_caches_in, 16)
            pool.dma_start(krT[:, T:TK], I["ckr"]).then_inc(mla_caches_in, 16)
            done(pool, "oi", 6)
            pool.dma_start(O["kr"], krT[0:ROPE, 0:SEQ]).then_inc(mla_out, 16)
            pool.wait_ge(cn_out, 14)
            pool.dma_start(O["ckv"], ckv[:, :, 0:SEQ]).then_inc(mla_out, 16)
            pool_moe(pool)
            pool.wait_ge(kv_out, 32)
            pool.wait_ge(state_out, 16)
            pool.wait_ge(mla_out, 32)

        @block_.scalar
        def _(act):
            act.wait_ge(consts_in, 16 * 4)
            nc.scalar.activation(csilu[:, :], wsm[:, S_C:S_C + 16], ACT.Silu).then_inc(csilu_ready, 1)
            for i in range(2):
                s = full(act, "lam", i)
                nc.scalar.activation(lam_e[:, i:i + 1], ps[:, s, 0:1], ACT.Exp).then_inc(ps_free[s], 1)
            act_norm(act, 0, lambda a, k: a.wait_ge(x_in, 16))
            act_even_in(act)
            act_colnorm(act, "l2", l2_groups, 0, [1.0] * 8, squared=True)
            att0[2](act)
            done(act, "att0", len(plan_b) - 1)
            act.wait_ge(cn_out, 8)
            act_colnorm(act, "obn", obn_groups, 8, [1 / P] * H)
            act_delta(act)
            act_onorm(act)
            act_norm(act, 1, lambda a, k: done(a, "eo", k % 4, k // 4), lambda: [act_fhi(act, j, 0) for j in range(2)])
            with act.Fori(0, 2) as turn:
                for j in range(EC):
                    ahead(act, act_fhi, j, turn)
                    act_gate(act, "fgu", j, turn)
            act_fdn(act)
            act_norm(act, 2, lambda a, k: done(a, "fdn", 1, 3) if k == 0 else None)
            act_odd_in(act)
            act_odd_qkv(act)
            att1[2](act)
            act_norm(act, 3, lambda a, k: done(a, "oo", k % 4, k // 4))
            act.wait_ge(top_ready, 1)
            nc.scalar.activation(tw, tw, ACT.Exp).then_inc(top_exp, 1)
            n = act_moe(act)
            act_norm(act, 4, lambda a, k: k == 0 and done(a, "moe", ITEM.index(f"sc{KD - 1}"), n - 1))

        @block_.vector
        def _(dve):
            st = Steps(dve, dve_step)
            dve.wait_ge(consts_in, 16 * 4)
            for i in range(2):
                last = nc.vector.tensor_tensor(lam_pr[:, i:i + 1], lam_in[:, 2 * i:2 * i + 1],
                                               lam_in[:, 2 * i + 1:2 * i + 2], ALU.mult)
            last.then_inc(lam_ready, 1)
            for col in (0, 1 + SEQ, 2 + T):
                last = nc.vector.memset(raw[:, col:col + 1], 0.0)
            st.then(last)
            done(dve, "lam", 0)
            done(dve, "lam", 1)
            st.then(nc.vector.tensor_tensor(neglam[:, :], lam_e[:, 1:2], lam_e[:, 0:1], ALU.subtract))
            st.then(nc.vector.tensor_scalar(neglam[:, :], neglam[:, :], -LAM_INIT, None, ALU.add))
            st.then(nc.vector.tensor_scalar(wsm[:, S_SUBLN:S_SUBLN + 1], wsm[:, S_SUBLN:S_SUBLN + 1],
                                            1.0 - LAM_INIT, None, ALU.mult))
            dve_mod(dve, st)
            dve_norm(dve, st, 0)
            dve_even_in(dve, st)
            dve.wait_ge(caches_in, 32)
            att0[1](dve, st)
            dve_colnorm(dve, st, "obn", obn_groups)
            nc.vector.memset(Sst[0], 0.0).then_inc(s_zero, 1)
            dve_crow(dve, st)
            dve_delta(dve, st)
            dve_scan(dve, st)
            dve_residual(dve, "eo", 4, 2, 2)
            for j in range(2):
                dve_flo(dve, j, 0)
            dve_norm(dve, st, 1)
            with dve.Fori(0, 2) as turn:
                for j in range(EC):
                    ahead(dve, dve_flo, j, turn)
                    dve_up(dve, "fgu", j, turn, arena[:, bass.ds((turn * EC + j) * T, T)])
            dve_fdn(dve)
            dve_norm(dve, st, 2)
            dve_odd(dve, st)
            att1[1](dve, st)
            dve_residual(dve, "oo", 4, 2, 8)
            dve_norm(dve, st, 3)
            dve_router(dve, st)
            dve_moe(dve, st)
            dve_norm(dve, Steps(dve, dve_end_step), 4)

        @block_.tensor
        def _(pe):
            pe_lam()
            pe_mod()
            pe_norm(0)
            pe_even_in()
            pe.wait_ge(caches_in, 32)
            att0[0]()
            pe_colnorm("obn", obn_groups, 8)
            pe_delta()
            pe_scan()
            pe_onorm()
            done(pe, "onrm", NT - 1)
            pe.wait_ge(cn_out, 12)
            pe_out("eo")
            pe_norm(1)
            pe_ffn()
            pe_norm(2)
            pe_odd_in()
            pe_odd_qkv()
            done(pe, "vv", NT)
            done(pe, "uqr", 7)
            att1[0]()
            done(pe, "att1", len(plan_c) - 1)
            pe_out("oo")
            pe_norm(3)
            pe_router()
            pe_moe()
            pe_norm(4)


def kernel(**inputs):
    import numpy as _np
    import concourse.bacc as _bacc
    from concourse.bass_utils import run_bass_kernel_spmd as _run

    v = {k: _np.asarray(a) for k, a in inputs.items()}

    def cut(w, ncols):
        k, n = w.shape
        return w.reshape(k // P, P, n // ncols, ncols).transpose(2, 1, 0, 3).reshape(n // ncols, P, -1)

    def col(w):
        return w.reshape(-1, P).T

    def rows(w):
        return _np.broadcast_to(w.reshape(1, -1), (P, w.size))

    def gate_up(w, nf):
        return w.reshape(KD, P, 2, nf, P).transpose(3, 1, 0, 2, 4).reshape(nf, P, KD * 256)

    i = _np.arange(P)
    ident = _np.eye(P)
    before = (i[:, None] <= i[None, :]).astype(_np.float64)
    masks = [before, before.T]
    levels = []
    for lv in range(LEVELS):
        w = 2 ** lv
        same = (i[:, None] // (2 * w)) == (i[None, :] // (2 * w))
        fwd = same & (i[None, :] % (2 * w) >= w) & (i[:, None] % (2 * w) < w)
        levels += [fwd, fwd.T]
    rot = _np.zeros((P, P))
    for b in range(0, P, 32):
        for j in range(16):
            rot[b + 16 + j, b + j] = -1.0
            rot[b + j, b + 16 + j] = 1.0
    table = _np.concatenate(
        [ident, _np.ones((P, P)), *masks, *[_np.where(m > 0, 0.0, NEG) for m in masks], *levels, rot,
         _np.broadcast_to(_np.arange(float(IT)), (P, IT)), _np.full((P, 1), EPS),
         _np.stack([i % 32 == 0, i % 32 == 1], axis=1)], axis=1).astype(_np.float32)
    half = ROPE // 2
    inv = (_np.float32(10000.0) ** (-_np.arange(0, half, 2, dtype=_np.float32) / _np.float32(half))).astype(_np.float32)
    tokens = _np.arange(DEC_SEQ)
    ar = (tokens // 64).astype(_np.float32)[:, None] * inv[None, :]
    ac = (tokens % 64).astype(_np.float32)[:, None] * inv[None, :]
    ang = _np.concatenate([ar, ar, ac, ac, ar, ar, ac, ac], axis=1).astype(_np.float32).T
    cossin = _np.stack([_np.cos(ang), _np.sin(ang)], axis=1).astype(_np.float32)

    w_in = v["ev_w_in"][0]
    main = _np.concatenate([w_in[:, 0:2048], w_in[:, 2064:3600]], axis=1)
    od_in = _np.concatenate([v["od_w_in"][0], v["od_w_in"][0][:, 640:704]], axis=1)
    uq = v["od_w_uq"][0].reshape(384, HC, 192)
    ukv = v["od_w_ukv"][0].reshape(256, HC, 256)
    arrays = {
        "wsm": _np.concatenate(
            [col(w) for w in (v["norm_mix"][0], v["norm_ffn"][0], v["norm_mix"][1], v["norm_ffn"][1],
                              v["final_norm"], v["mod_b"])]
            + [v["ev_conv_w"][0].reshape(3, 12, P).transpose(2, 1, 0).reshape(P, 36),
               col(v["ev_onorm"][0]), col(v["ev_subln"][0]), col(v["od_q_norm"][0]), col(v["od_kv_norm"][0]),
               rows(v["ev_dt_bias"][0]), rows(v["ev_a_log"][0]),
               _np.stack([col(v["c_ctx"]), col(v["c"][0])], axis=2).reshape(P, 16)], axis=1),
        "cst": table,
        "lam": v["ev_lambda"][0].T,
        "cossin": cossin,
        "x": _np.concatenate([v["x_prompt"][0], v["x_sample"][0]], axis=0).T.reshape(KD, P, T)
             .transpose(1, 0, 2).reshape(P, KD * T),
        "ck": v["cache_diff_k"][0, 0].transpose(2, 0, 1),
        "cv": v["cache_diff_v"][0, 0].transpose(1, 0, 2).reshape(P, 512),
        "cckv": v["cache_mla_ckv"][0, 0].T.reshape(2, P, PAST).transpose(1, 0, 2),
        "ckr": _np.concatenate([v["cache_mla_krope"][0, 0].T] * 2, axis=0),
        "state": v["state_delta"][0, 0].transpose(2, 0, 1, 3).reshape(P, 1024),
        "w_mod": _np.concatenate([cut(v["mod_w"][0], 256), cut(v["mod_w"][1], 256)], axis=0),
        "w_ev": cut(main, 256),
        "w_evg": cut(w_in[:, 2048:2064], 16),
        "w_eo": cut(v["ev_w_out"][0], 256),
        "w_gu": gate_up(v["ffn_w_gu"][0], FC),
        "w_dn": v["ffn_w_down"][0].reshape(2, LK, P, KD, P).transpose(3, 0, 2, 1, 4).reshape(16, P, LK * P),
        "w_oi": cut(od_in, 256),
        "w_uq": _np.concatenate([cut(uq[:, :, 0:128].reshape(384, 1024), 512),
                                 cut(uq[:, :, 128:192].reshape(384, 512), 512)], axis=0),
        "w_ukv": _np.stack([cut(ukv[:, :, 0:128].reshape(256, D), D)[0], cut(ukv[:, :, 128:].reshape(256, D), D)[0]]),
        "w_oo": cut(v["od_w_out"][0], 256),
        "w_rt": cut(v["moe_router"][0], NE),
        "w_mgu": _np.concatenate([gate_up(v["moe_w_gu"][0, e], EC) for e in range(NE)], axis=0),
        "w_mdn": v["moe_w_down"][0].reshape(NE, EC, P, 2, 512).transpose(0, 3, 2, 1, 4).reshape(2 * NE, P, EC * 512),
    }
    outs = {"y": (P, KD * T), "state": (P, 1024), "dk": (P, H, SEQ), "dv": (SEQ, 512),
            "ckv": (P, 2, SEQ), "kr": (ROPE, SEQ)}
    nc = _bacc.Bacc("TRN2", target_bir_lowering=False, num_devices=1, dynamic_dma_scratch_size=2048)
    arrays = {f"in_{n}": _np.ascontiguousarray(a) for n, a in arrays.items()}
    I = {n[3:]: nc.dram_tensor(n, a.shape, F32, kind="ExternalInput").ap() for n, a in arrays.items()}
    O = {n: nc.dram_tensor(f"out_{n}", s, F32, kind="ExternalOutput").ap() for n, s in outs.items()}
    program(nc, I, O)
    r = _run(nc, [arrays], core_ids=[0]).results[0]
    y = r["out_y"].reshape(P, KD, T).transpose(2, 1, 0).reshape(T, D)
    return (
        y[0:SEQ].reshape(1, SEQ, D), y[SEQ:T].reshape(1, DEC_SEQ, D),
        r["out_state"].reshape(P, 2, H, P).transpose(1, 2, 0, 3).reshape(1, 1, 2, H, P, P),
        r["out_dk"].transpose(1, 2, 0).reshape(1, 1, H, SEQ, P),
        r["out_dv"].reshape(SEQ, H, P).transpose(1, 0, 2).reshape(1, 1, H, SEQ, P),
        r["out_ckv"].transpose(2, 1, 0).reshape(1, 1, SEQ, 256),
        r["out_kr"].T.reshape(1, 1, SEQ, ROPE),
    )
```
